# Optimizing a Trainium2 kernel written in Bass

```python
import math
import jax, jax.numpy as jnp
from jax import lax
import numpy as np

D_MODEL = 1024
BATCH = 1
SEQ = 512
DEPTH = 2

CHUNK = 64
MEM_LEN = 256
N_MIXERS = 4
GROUP_W = D_MODEL // N_MIXERS
POOL_GROUPS = 4
POOL_CH = GROUP_W // POOL_GROUPS
POOL_WINDOWS = (2, 4, 8, 16)
SCONV_W = 3
DIFF_HEADS = 4
DIFF_DV = GROUP_W // DIFF_HEADS
DIFF_DK = DIFF_DV // 2
ROT_DIMS = DIFF_DK // 4
ROPE_THETA = 500000.0
CONF_W = 31
X_HEADS = 4
X_HD = D_MODEL // X_HEADS
D_FF = ((8 * D_MODEL // 3 + 127) // 128) * 128
Q_BLOCK = 128
EPS = 1e-6

POOL_COLS = GROUP_W
SCONV_COLS = 3 * GROUP_W
DIFF_COLS = 3 * GROUP_W
CONF_COLS = 2 * GROUP_W
IN_COLS = POOL_COLS + SCONV_COLS + DIFF_COLS + CONF_COLS
SPLITS = [POOL_COLS, POOL_COLS + SCONV_COLS, POOL_COLS + SCONV_COLS + DIFF_COLS]

kernel_name = "hybrid_parallel_group_streaming_encoder"

def rms_norm(x, g):
    x32 = x.astype(jnp.float32)
    y = x32 * lax.rsqrt(jnp.mean(x32 * x32, axis=-1, keepdims=True) + EPS)
    return (y * g.astype(jnp.float32)).astype(x.dtype)

def layer_norm(x, g, b):
    x32 = x.astype(jnp.float32)
    mu = jnp.mean(x32, axis=-1, keepdims=True)
    xc = x32 - mu
    y = xc * lax.rsqrt(jnp.mean(xc * xc, axis=-1, keepdims=True) + EPS)
    return (y * g.astype(jnp.float32) + b.astype(jnp.float32)).astype(x.dtype)

def swiglu(h, w_gate, w_up, w_down):
    return (jax.nn.silu(h @ w_gate) * (h @ w_up)) @ w_down

def causal_depthwise_conv(u, w):
    k = w.shape[0]
    return lax.conv_general_dilated(
        u, w[:, None, :].astype(u.dtype), window_strides=(1,), padding=[(k - 1, 0)],
        dimension_numbers=("NWC", "WIO", "NWC"), feature_group_count=u.shape[-1])

def pool_mixer(u, pool_w, pool_scale):
    b, s, _ = u.shape
    ug = u.reshape(b, s, POOL_GROUPS, POOL_CH)
    u32 = ug.astype(jnp.float32)
    cs = jnp.cumsum(u32, axis=1)
    t = jnp.arange(s)
    means = []
    for g, w in enumerate(POOL_WINDOWS):
        c = cs[:, :, g]
        lo = jnp.pad(c, ((0, 0), (w, 0), (0, 0)))[:, :s]
        cnt = jnp.minimum(t + 1, w).astype(jnp.float32)
        means.append((c - lo) / cnt[None, :, None])
    mixed = (jnp.stack(means, axis=2) - u32).astype(u.dtype)
    y = jnp.einsum("bsgc,gcd->bsgd", mixed, pool_w)
    return y.reshape(b, s, GROUP_W) * pool_scale

def partial_rope(x, cos, sin):
    half = ROT_DIMS // 2
    xr = x[..., :ROT_DIMS].astype(jnp.float32)
    x1, x2 = xr[..., :half], xr[..., half:]
    c = cos[:, :, None, None, :]
    s = sin[:, :, None, None, :]
    rot = jnp.concatenate([x1 * c - x2 * s, x2 * c + x1 * s], axis=-1)
    return jnp.concatenate([rot.astype(x.dtype), x[..., ROT_DIMS:]], axis=-1)

def diff_attention(q, k, v, lam):
    b, s = q.shape[:2]
    nb = s // Q_BLOCK
    qb = jnp.moveaxis(q.reshape(b, nb, Q_BLOCK, DIFF_HEADS, 2, DIFF_DK), 1, 0)
    kpos = jnp.arange(s)
    scale = DIFF_DK ** -0.5

    def block(args):
        qblk, i = args
        sc = jnp.einsum("bqhcd,bkhcd->bchqk", qblk, k).astype(jnp.float32) * scale
        qpos = i * Q_BLOCK + jnp.arange(Q_BLOCK)
        limit = (qpos // CHUNK + 1) * CHUNK
        mask = kpos[None, :] < limit[:, None]
        sc = jnp.where(mask, sc, -jnp.inf)
        p = jax.nn.softmax(sc, axis=-1)
        a = p[:, 0] - lam * p[:, 1]
        return jnp.einsum("bhqk,bkhd->bqhd", a.astype(v.dtype), v)

    o = lax.map(block, (qb, jnp.arange(nb)))
    return jnp.moveaxis(o, 0, 1).reshape(b, s, DIFF_HEADS, DIFF_DV)

def setup_inputs(seed: int = 0) -> dict:
    key = jax.random.key(seed)
    ks = iter(jax.random.split(key, 64))

    def nrm(shape, scale):
        return scale * jax.random.normal(next(ks), shape, jnp.float32)

    def gain(shape):
        return 1.0 + nrm(shape, 0.02)

    L, D, F, G = DEPTH, D_MODEL, D_FF, GROUP_W
    return {
        "x": nrm((BATCH, SEQ, D), 1.0),
        "mem": nrm((BATCH, MEM_LEN, D), 1.0),
        "positions": jnp.broadcast_to(jnp.arange(SEQ, dtype=jnp.int32), (BATCH, SEQ)),
        "f1_pre_g": gain((L, D)),
        "f1_w_gate": nrm((L, D, F), D ** -0.5),
        "f1_w_up": nrm((L, D, F), D ** -0.5),
        "f1_w_down": nrm((L, F, D), F ** -0.5),
        "f1_post_g": gain((L, D)),
        "mix_pre_g": gain((L, D)),
        "w_in": nrm((L, D, IN_COLS), D ** -0.5),
        "pool_w": nrm((L, POOL_GROUPS, POOL_CH, POOL_CH), POOL_CH ** -0.5),
        "pool_scale": gain((L, G)),
        "sconv_w": nrm((L, SCONV_W, G), SCONV_W ** -0.5),
        "lam_q1": nrm((L, DIFF_DK), 0.1),
        "lam_k1": nrm((L, DIFF_DK), 0.1),
        "lam_q2": nrm((L, DIFF_DK), 0.1),
        "lam_k2": nrm((L, DIFF_DK), 0.1),
        "diff_subln_g": gain((L, DIFF_DV)),
        "conf_dw_w": nrm((L, CONF_W, G), CONF_W ** -0.5),
        "conf_dw_b": nrm((L, G), 0.02),
        "conf_ln_g": gain((L, G)),
        "conf_ln_b": nrm((L, G), 0.02),
        "w_o": nrm((L, D, D), D ** -0.5),
        "mix_post_g": gain((L, D)),
        "x_pre_g": gain((L, D)),
        "x_mem_g": gain((L, D)),
        "x_wq": nrm((L, D, D), D ** -0.5),
        "x_wk": nrm((L, D, D), D ** -0.5),
        "x_wv": nrm((L, D, D), D ** -0.5),
        "x_wo": nrm((L, D, D), D ** -0.5),
        "x_post_g": gain((L, D)),
        "f2_pre_g": gain((L, D)),
        "f2_w_gate": nrm((L, D, F), D ** -0.5),
        "f2_w_up": nrm((L, D, F), D ** -0.5),
        "f2_w_down": nrm((L, F, D), F ** -0.5),
        "f2_post_g": gain((L, D)),
    }

def reference(x, mem, positions,
              f1_pre_g, f1_w_gate, f1_w_up, f1_w_down, f1_post_g,
              mix_pre_g, w_in, pool_w, pool_scale, sconv_w,
              lam_q1, lam_k1, lam_q2, lam_k2, diff_subln_g,
              conf_dw_w, conf_dw_b, conf_ln_g, conf_ln_b, w_o, mix_post_g,
              x_pre_g, x_mem_g, x_wq, x_wk, x_wv, x_wo, x_post_g,
              f2_pre_g, f2_w_gate, f2_w_up, f2_w_down, f2_post_g):
    b, s, d = x.shape
    m_len = mem.shape[1]
    inv_freq = ROPE_THETA ** (-jnp.arange(0, ROT_DIMS, 2, dtype=jnp.float32) / ROT_DIMS)
    ang = positions.astype(jnp.float32)[..., None] * inv_freq
    cos, sin = jnp.cos(ang), jnp.sin(ang)

    for l in range(DEPTH):
        h = rms_norm(x, f1_pre_g[l])
        x = x + 0.5 * rms_norm(swiglu(h, f1_w_gate[l], f1_w_up[l], f1_w_down[l]), f1_post_g[l])

        h = rms_norm(x, mix_pre_g[l])
        z = h @ w_in[l]
        za, zb, zc, zd = jnp.split(z, SPLITS, axis=-1)

        ya = pool_mixer(za, pool_w[l], pool_scale[l])

        xs, bg, cg = jnp.split(zb, 3, axis=-1)
        yb = bg * causal_depthwise_conv(cg * xs, sconv_w[l])

        zq, zk, zv = jnp.split(zc, 3, axis=-1)
        q = partial_rope(zq.reshape(b, s, DIFF_HEADS, 2, DIFF_DK), cos, sin)
        k = partial_rope(zk.reshape(b, s, DIFF_HEADS, 2, DIFF_DK), cos, sin)
        v = zv.reshape(b, s, DIFF_HEADS, DIFF_DV)
        lambda_init = 0.8 - 0.6 * math.exp(-0.3 * l)
        lam = (jnp.exp(jnp.sum(lam_q1[l].astype(jnp.float32) * lam_k1[l].astype(jnp.float32)))
               - jnp.exp(jnp.sum(lam_q2[l].astype(jnp.float32) * lam_k2[l].astype(jnp.float32)))
               + lambda_init)
        o = diff_attention(q, k, v, lam)
        yc = (rms_norm(o, diff_subln_g[l]) * (1.0 - lambda_init)).reshape(b, s, GROUP_W)

        ga, gg = jnp.split(zd, 2, axis=-1)
        u = ga * jax.nn.sigmoid(gg)
        u = causal_depthwise_conv(u, conf_dw_w[l]) + conf_dw_b[l]
        yd = jax.nn.silu(layer_norm(u, conf_ln_g[l], conf_ln_b[l]))

        y = jnp.concatenate([ya, yb, yc, yd], axis=-1) @ w_o[l]
        x = x + rms_norm(y, mix_post_g[l])

        h = rms_norm(x, x_pre_g[l])
        mn = rms_norm(mem, x_mem_g[l])
        qx = (h @ x_wq[l]).reshape(b, s, X_HEADS, X_HD)
        kx = (mn @ x_wk[l]).reshape(b, m_len, X_HEADS, X_HD)
        vx = (mn @ x_wv[l]).reshape(b, m_len, X_HEADS, X_HD)
        sc = jnp.einsum("bshd,bmhd->bhsm", qx, kx).astype(jnp.float32) * (X_HD ** -0.5)
        p = jax.nn.softmax(sc, axis=-1)
        ox = jnp.einsum("bhsm,bmhd->bshd", p.astype(vx.dtype), vx).reshape(b, s, d) @ x_wo[l]
        x = x + rms_norm(ox, x_post_g[l])

        h = rms_norm(x, f2_pre_g[l])
        x = x + 0.5 * rms_norm(swiglu(h, f2_w_gate[l], f2_w_up[l], f2_w_down[l]), f2_post_g[l])
    return x


_drawn_inputs = setup_inputs


def setup_inputs(seed=0):
    import zlib

    import numpy as np

    out = dict(_drawn_inputs(seed))
    spreads = {}
    factors = {'f1_pre_g': 2.69,
     'f1_post_g': 3.856,
     'pool_scale': 5.801,
     'lam_q2': 3.022,
     'diff_subln_g': 6.017,
     'conf_dw_b': 3.923,
     'conf_ln_g': 7.132,
     'conf_ln_b': 8.0,
     'mix_post_g': 3.094,
     'x_pre_g': 3.68,
     'x_post_g': 3.664,
     'f2_pre_g': 5.297,
     'f2_post_g': 22.463}
    for name, (base, spread) in spreads.items():
        noise = np.random.default_rng([zlib.crc32(name.encode()), seed]).standard_normal(out[name].shape)
        drawn = base * np.exp(spread * noise) if base else spread * noise
        out[name] = __import__('jax').numpy.asarray(drawn.astype(out[name].dtype))
    for name, factor in factors.items():
        out[name] = (out[name] * factor).astype(out[name].dtype)
    return out
```

```python
import math
from contextlib import ExitStack

import numpy as np

import concourse.bass as bass
from concourse import mybir

F32, F32R, I32 = mybir.dt.float32, mybir.dt.float32r, mybir.dt.int32
ALU, ACT, AX = mybir.AluOpType, mybir.ActivationFunctionType, mybir.AxisListType

P, D, SEQ, DEPTH, MEM, FF = 128, 1024, 512, 2, 256, 2816
KD, KF, KFH = D // P, FF // P, FF // P // 2
EPS = 1e-6
POOL_WINDOWS = (2, 4, 8, 16)
SCW, CFW = 3, 31
DIFF_DK, DIFF_DV, DIFF_H, X_H, X_HD, CHUNK = 32, 64, 4, 4, 256, 64
ROT, THETA = DIFF_DK // 4, 500000.0
QB = SEQ // P

SIZES = (("f1gu", 2 * KF), ("f1dn", 2 * KD), ("kx", KD), ("win", 18), ("vx", KD), ("wo", KD),
         ("qx", KD), ("xo", KD), ("f2gu", 2 * KF), ("f2dn", 2 * KD))
BASE, NB = {}, 0
for _n, _k in SIZES:
    BASE[_n] = NB
    NB += _k
DT, NDT = {}, 0
for _n, _k in (("f1gu", 2 * KF), ("f1dn", KD), ("win", 18), ("wo", KD), ("qx", KD), ("xo", KD),
               ("f2gu", 2 * KF), ("f2dn", KD)):
    DT[_n] = NDT
    NDT += _k
NAT = 2 * KD
RING = 2

PAR, NPAR = {}, 0
for _n, _k in (("f1_pre_g", KD), ("f1_post_g", KD), ("mix_pre_g", KD), ("mix_post_g", KD),
               ("x_pre_g", KD), ("x_mem_g", KD), ("x_post_g", KD), ("f2_pre_g", KD),
               ("f2_post_g", KD), ("pool_scale", 2), ("sconv_w", 2 * SCW), ("subln", 1),
               ("conf_w", 2 * CFW), ("conf_b", 2), ("ln_g", 2), ("ln_b", 2)):
    PAR[_n] = NPAR
    NPAR += _k
C_ID, C_FREQ, C_SIGN, C_INVW, C_EDGE, C_ROW = 0, 128, 129, 130, 132, 164
NCONST = C_ROW + 128 + CHUNK

(S_PRE1, S_POST1, S_PRE2, S_LN, S_POST2, S_PRE3, S_POST3, S_PRE4, S_POST4), NSTAT = range(9), 9
H_PRE1, H_PRE2, H_MIX, H_PRE3, H_OX, H_PRE4, NH = 0, 8, 16, 22, 30, 38, 46
NSQ = 4 * KD + 2
SQ = {S_PRE1: 0, S_PRE2: 8, S_LN: 16, S_PRE3: 18, S_PRE4: 26}
YSQ = {S_POST1: 0, S_POST2: 8, S_POST3: 16, S_POST4: 24}
XR = {S_PRE2: 0, S_PRE3: 8, S_PRE4: 16}
NUNIT = QB * DIFF_H
DIFF_SCALE, X_SCALE = DIFF_DK ** -0.5, X_HD ** -0.5


def build(nc, x_d, mem_d, pos_d, w8_d, wd_d, par_d, poolw_d, lam_d, const_d, out_d):
    ctx = ExitStack()
    with ctx:
        place = [(nc.sbuf_base + 63) // 64 * 64]

        def at(name, shape, dt, where=None):
            n = int(np.prod(shape[1:])) * 4
            off = place[0] if where is None else where
            t = nc.alloc_sbuf_tensor_at(name, shape, dt, offset=off)
            if where is None:
                place[0] += (n + 31) // 32 * 32
            return t

        x = at("x", [P, KD, SEQ], F32)
        y_at = place[0]
        h_hi = at("h_hi", [P, KD, SEQ], F32R)
        y = at("y", [P, KD, SEQ], F32, y_at)
        h_lo = at("h_lo", [P, KD, SEQ], F32R)
        w_in_f32 = at("w_stage", [P, RING, KFH, P], F32)
        w_hi = at("w_hi", [P, RING, KFH, P], F32R)
        w_lo = at("w_lo", [P, RING, KFH, P], F32R)
        mem_hi = at("mem_hi", [P, KD, MEM], F32R)
        mem_lo = at("mem_lo", [P, KD, MEM], F32R)
        const = at("const", [P, NCONST], F32)
        ones = at("ones", [P, P], F32)
        mean256 = at("mean256", [P, P], F32)
        cos_t = at("cos_t", [P, SEQ], F32)
        sin_t = at("sin_t", [P, SEQ], F32)
        par_all = at("par_all", [P, DEPTH, NPAR], F32)
        par = at("par", [P, NPAR], F32)
        neg_lam = at("neg_lam", [P, DEPTH], F32)
        neg_lam_l = at("neg_lam_l", [P, 1], F32)
        r_mem = at("r_mem", [P, MEM], F32)
        r_pre = at("r_pre", [P, SEQ], F32)
        r_post = at("r_post", [P, SEQ], F32)
        e0_at = place[0]
        epi = at("epi", [P, 2, SEQ], F32)
        acc = at("acc", [P, SEQ], F32)
        diag = at("diag", [P, QB, P], F32)
        stat = at("stat", [P, 4, 4], F32)
        att_s = at("att_s", [P, 2, 3, 4], F32)
        ident = const[:, C_ID:C_ID + P]

        r_at = place[0]
        hid_hi = at("hid_hi", [P, KF, SEQ], F32R)
        hid_lo = at("hid_lo", [P, KF, SEQ], F32R)
        assert place[0] <= nc.sbuf_usable_end, place[0]
        mem_f32 = at("mem_f32", [P, KD, MEM], F32, place[0] - KD * MEM * 4)
        rp = [r_at]

        def r_alloc(name, shape):
            t = at(name, shape, F32, rp[0])
            rp[0] += (int(np.prod(shape[1:])) * 4 + 31) // 32 * 32
            return t

        kx = r_alloc("kx", [P, KD, MEM])
        vx_at = rp[0]
        xs = r_alloc("xs", [P, 2, SEQ])
        cg = r_alloc("cg", [P, 2, SEQ])
        vx = at("vx", [P, MEM // P, D], F32, vx_at)
        vxt_at = rp[0]
        ga = r_alloc("ga", [P, 2, SEQ])
        gg = r_alloc("gg", [P, 2, SEQ])
        vxt = at("vxt", [P, KD, MEM], F32, vxt_at)
        cross_at = rp[0]
        bg = r_alloc("bg", [P, 2, SEQ])
        PAD = POOL_WINDOWS[-1]
        za = r_alloc("za", [P, 2, PAD + SEQ])
        zb = r_alloc("zb", [P, 2, PAD + SEQ])
        zc = r_alloc("zc", [P, 2, PAD + SEQ])
        qk = r_alloc("qk", [P, 4, SEQ])
        vt = r_alloc("vt", [P, 2, SEQ])
        v = r_alloc("v", [P, QB, 2 * P])
        cpad = r_alloc("cpad", [P, 2, SCW - 1 + SEQ])
        upad = r_alloc("upad", [P, 2, CFW - 1 + SEQ])
        u = r_alloc("u", [P, 2, SEQ])
        p_at = rp[0]
        prob = r_alloc("prob", [P, 2, 2, SEQ])
        rope = at("rope", [P, 4, SEQ], F32, p_at)
        amix = r_alloc("amix", [P, 2, SEQ])
        amix_t = r_alloc("amix_t", [P, 2, SEQ])
        oc = r_alloc("oc", [P, 2 * P])
        junk = r_alloc("junk", [P, DIFF_H, DIFF_DV])
        assert rp[0] <= place[0], (rp[0], place[0])
        rp[0] = cross_at
        qx = r_alloc("qx", [P, KD, SEQ])
        y_r = at("y_r", [P, KD, SEQ], F32, cross_at)
        px = r_alloc("px", [P, 2, X_H, MEM])
        pxt = r_alloc("pxt", [P, 2, X_H, SEQ])
        assert rp[0] <= place[0]
        ang = at("ang", [P, 6, SEQ], F32, r_at)
        pos_i = at("pos_i", [P, SEQ], I32, r_at + 6 * SEQ * 4)
        lam_in = at("lam_in", [P, DEPTH, 4, DIFF_DK], F32, r_at + 7 * SEQ * 4)
        lam_s = at("lam_s", [P, 2 * DEPTH], F32, r_at + 8 * SEQ * 4)
        lam_p = at("lam_p", [P, DEPTH, 2, DIFF_DK], F32, r_at + 8 * SEQ * 4 + 64)
        poolw = at("poolw", [P, 2, P], F32, place[0])
        assert place[0] + 2 * P * 4 <= nc.sbuf_usable_end, place[0]

        ps = ctx.enter_context(nc.psum_tensor("ps", [P, 8, 512], F32))
        B_STAT, B_BC = 6, 7

        def sem(name):
            return ctx.enter_context(nc.semaphore(name))

        w_loaded = [sem("w_loaded0"), sem("w_loaded1")]
        w_hi_done, w_lo_done, w_used = sem("w_hi_done"), sem("w_lo_done"), sem("w_used")
        dve_tiles, act_tiles = sem("dve_tiles"), sem("act_tiles")
        h_hi_done, h_lo_done = sem("h_hi_done"), sem("h_lo_done")
        sq_ready, sq_used = sem("sq_ready"), sem("sq_used")
        ysq_ready, ysq_used, ysq_free = sem("ysq_ready"), sem("ysq_used"), sem("ysq_free")
        stat_sum, stat_diag, stat_bc = sem("stat_sum"), sem("stat_diag"), sem("stat_bc")
        x_ready = sem("x_ready")
        silu_done, prod_done = sem("silu_done"), sem("prod_done")
        hid_hi_done, hid_lo_done = sem("hid_hi_done"), sem("hid_lo_done")
        consts_in, x_in, poolw_in = sem("consts_in"), sem("x_in"), sem("poolw_in")
        mem_in, mem_n, mem_hi_done, mem_lo_done = sem("mem_in"), sem("mem_n"), sem("mem_hi_done"), sem("mem_lo_done")
        par_ready, setup_p, setup_d, trig_arg, trig_done = sem("par_ready"), sem("setup_p"), sem("setup_d"), sem("trig_arg"), sem("trig_done")
        lam_arg, lam_exp = sem("lam_arg"), sem("lam_exp")
        tanh_done, c_done, pads_done = sem("tanh_done"), sem("c_done"), sem("pads_done")
        pool_sums, mixed, pool_y = sem("pool_sums"), sem("mixed"), sem("pool_y")
        yb_ready, u_ready, mu_done, xc_ready = sem("yb_ready"), sem("u_ready"), sem("mu_done"), sem("xc_ready")
        ln_ready, yd_ready = sem("ln_ready"), sem("yd_ready")
        rope_shuf, rope_mul, qk_ready = sem("rope_shuf"), sem("rope_mul"), sem("qk_ready")
        v_tr, v_tok, vx_tr, vx_tok = sem("v_tr"), sem("v_tok"), sem("vx_tr"), sem("vx_tok")
        a_s, a_max, a_exp, a_mix, a_tr, a_trc, a_pv = (sem(n) for n in ("a_s", "a_max", "a_exp", "a_mix", "a_tr", "a_trc", "a_pv"))
        o_sq, o_out, o_tr, yc_hi, yc_lo = (sem(n) for n in ("o_sq", "o_out", "o_tr", "yc_hi", "yc_lo"))
        x_s, x_max, x_exp, x_nrm, x_tr, x_trc, x_pv = (sem(n) for n in ("x_s", "x_max", "x_exp", "x_nrm", "x_tr", "x_trc", "x_pv"))
        stored = sem("stored")

        def g(name, i=0):
            return par[:, PAR[name] + i:PAR[name] + i + 1]

        block = ctx.enter_context(nc.Block())

        @block.sync
        def _(sp):
            sp.dma_start(const[:], const_d).then_inc(consts_in, 16)
            sp.dma_start(par_all[:], par_d).then_inc(consts_in, 16)
            sp.dma_start(pos_i[:], pos_d.to_broadcast([P, SEQ])).then_inc(consts_in, 16)
            sp.dma_start(lam_in[:], lam_d.to_broadcast([P, DEPTH * 4 * DIFF_DK])
                         .rearrange("p (l a k) -> p l a k", l=DEPTH, a=4)).then_inc(consts_in, 16)
            sp.dma_start(mem_f32[:], mem_d).then_inc(mem_in, 16)
            sp.dma_start(x[:], x_d).then_inc(x_in, 16)
            with sp.Fori(0, DEPTH) as l:
                def load(p, s, kc, src):
                    sp.wait_ge(w_lo_done, 2 * p + s + 1)
                    sp.dma_start(w_in_f32[:, s, 0:kc, :], src.rearrange("p (k m) -> p k m", k=kc))\
                        .then_inc(w_loaded[s], 16)

                def loads(lo, n, kc, dram, first):
                    with sp.Fori(0, n // 2) as j:
                        for s in range(2):
                            load(l * (NB // 2) + lo // 2 + j, s, kc,
                                 dram[bass.ds(l * (NB - 4 * KD if kc == KD else 4 * KD) + first + 2 * j + s, 1), :, :]
                                 .rearrange("a p n -> (a p) n"))

                sp.wait_ge(w_used, l * NB + RING)
                sp.wait_ge(setup_d, 1)
                sp.dma_start(mem_f32[:], mem_d).then_inc(mem_in, 16)
                sp.dma_start(poolw[:], poolw_d[bass.ds(l, 1), :, :, :].rearrange("a p t n -> (a p) t n"))\
                    .then_inc(poolw_in, 16)
                loads(BASE["f1gu"], 2 * KF, KD, w8_d, 0)
                loads(BASE["f1dn"], 2 * KD, KFH, wd_d, 0)
                loads(BASE["kx"], BASE["f2dn"] - BASE["kx"], KD, w8_d, 2 * KF)
                loads(BASE["f2dn"], 2 * KD, KFH, wd_d, 2 * KD)
            sp.wait_ge(x_ready, DEPTH * 4 * KD + 1)
            sp.dma_start(out_d, x[:]).then_inc(stored, 16)
            sp.wait_ge(stored, 16)

        @block.tensor
        def _(pe):
            pe.sem_inc(w_used, RING)
            pe.sem_inc(sq_used, 2)

            pe.wait_ge(setup_p, 1)
            for m in range(KD):
                pe.wait_ge(sq_ready, m + 1)
                for c in range(MEM // P):
                    mm = pe.matmul(ps[:, B_STAT, c:c + 1], epi[:, m % 2, c * P:(c + 1) * P], ones[:, 0:1],
                                   start=(m == 0 and c == 0), stop=(m == KD - 1), skip_group_check=True)
                mm.then_inc(sq_used, 1)
            pe.wait_ge(stat_diag, 1)
            pe.matmul(ps[:, B_BC, 0:MEM], ones[:, :], diag[:, 0:MEM // P, :], start=True, stop=True)\
                .then_inc(stat_bc, 1)

            with pe.Fori(0, DEPTH) as l:
                def product(bank, width, p, kcs, rhs, first, last):
                    s = p[1]
                    pe.wait_ge(w_lo_done, 2 * p[0] + s + 1 + RING)
                    for k in range(kcs[1] - kcs[0]):
                        hi, lo = rhs(kcs[0] + k)
                        for n, (a, b) in enumerate(((w_hi, hi), (w_hi, lo), (w_lo, hi))):
                            mm = pe.matmul(ps[:, bank, 0:width], a[:, s, k, :], b,
                                           start=(first and k == 0 and n == 0),
                                           stop=(last and k == kcs[1] - kcs[0] - 1 and n == 2))
                    mm.then_inc(w_used, 1)

                def project(name, n_tiles, rhs, inputs, width=SEQ, kf=False):
                    by_act = name in ("kx", "vx")
                    with pe.Fori(0, n_tiles // 2) as j:
                        for sem_, value in inputs:
                            pe.wait_ge(sem_, value)
                        for s in range(2):
                            if by_act:
                                pe.wait_ge(act_tiles, l * NAT + (KD if name == "vx" else 0) + 2 * j + s + 1)
                            else:
                                pe.wait_ge(dve_tiles, l * NDT + DT[name] + 2 * j + s + 1)
                            if kf:
                                for half in range(2):
                                    product(s, width, (l * (NB // 2) + BASE[name] // 2 + 2 * j + s, half),
                                            (half * KFH, half * KFH + KFH), rhs, half == 0, half == 1)
                            else:
                                product(s, width, (l * (NB // 2) + BASE[name] // 2 + j, s), (0, KD), rhs, True, True)

                def h_rhs(k):
                    return h_hi[:, k, :], h_lo[:, k, :]

                def hid_rhs(k):
                    return hid_hi[:, k, :], hid_lo[:, k, :]

                def mem_rhs(k):
                    return mem_hi[:, k, :], mem_lo[:, k, :]

                def pre_norm(no):
                    base = l * NSQ + KD + SQ[no]
                    for m in range(KD):
                        pe.wait_ge(sq_ready, base + m + 1)
                        for c in range(QB):
                            mm = pe.matmul(ps[:, B_STAT, c:c + 1], epi[:, m % 2, c * P:(c + 1) * P], ones[:, 0:1],
                                           start=(m == 0 and c == 0), stop=(m == KD - 1), skip_group_check=True)
                        mm.then_inc(sq_used, 1)
                    spread(no)

                def spread(no):
                    pe.wait_ge(stat_diag, l * NSTAT + no + 2)
                    pe.matmul(ps[:, B_BC, :], ones[:, :], diag[:, :, :], start=True, stop=True)\
                        .then_inc(stat_bc, 1)

                def post_norm(no):
                    pe.wait_ge(ysq_used, l * 4 * KD + YSQ[no] + KD)
                    for c in range(QB):
                        mm = pe.matmul(ps[:, B_STAT, c:c + 1], acc[:, c * P:(c + 1) * P], ones[:, 0:1],
                                       start=(c == 0), stop=True, skip_group_check=True)
                    mm.then_inc(stat_sum, 1)
                    spread(no)

                def ffn(n, first_h):
                    project(f"f{n}gu", 2 * KF, h_rhs, [(h_lo_done, l * NH + first_h + KD)])
                    project(f"f{n}dn", KD, hid_rhs, [(hid_lo_done, l * 2 * KF + n * KF)], kf=True)

                pre_norm(S_PRE1)
                ffn(1, H_PRE1)
                post_norm(S_POST1)
                project("kx", KD, mem_rhs, [(mem_lo_done, l * KD + KD), (dve_tiles, l * NDT + DT["f1dn"] + KD + RING)],
                        width=MEM)
                pre_norm(S_PRE2)
                project("win", 18, h_rhs, [(act_tiles, l * NAT + KD + RING), (h_lo_done, l * NH + H_PRE2 + KD)])
                project("vx", KD, mem_rhs, [(dve_tiles, l * NDT + DT["win"] + 18 + RING)], width=MEM)

                for t in range(2):
                    for c in range(QB):
                        mm = pe.transpose(ps[:, 4 + t, c * P:(c + 1) * P], vt[:, t, c * P:(c + 1) * P], ident)
                    mm.then_inc(v_tr, 1)
                pe.wait_ge(act_tiles, l * NAT + 2 * KD + RING)
                for n in range(4):
                    if n >= 2:
                        pe.wait_ge(vx_tok, l * 4 + n - 1)
                    for f in range(4):
                        mm = pe.transpose(ps[:, 2 + n % 2, f * P:(f + 1) * P],
                                          vxt[:, 4 * (n % 2) + f, (n // 2) * P:(n // 2 + 1) * P], ident)
                    mm.then_inc(vx_tr, 1)
                pe.wait_ge(u_ready, l + 1)
                for t in range(2):
                    mm = pe.matmul(ps[:, 6, :], mean256[:, :], u[:, t, :], start=(t == 0), stop=(t == 1))
                mm.then_inc(mu_done, 1)
                pe.wait_ge(mixed, l * 2 + 2)
                pe.wait_ge(poolw_in, l * 16 + 16)
                for t in range(2):
                    pe.matmul(ps[:, t, :], poolw[:, t, :], zb[:, t, PAD:PAD + SEQ], start=True, stop=True)\
                        .then_inc(pool_y, 1)
                pe.wait_ge(xc_ready, l * 2 + 2)
                for m in range(2):
                    pe.wait_ge(sq_ready, l * NSQ + KD + SQ[S_LN] + m + 1)
                    for c in range(QB):
                        mm = pe.matmul(ps[:, B_STAT, c:c + 1], epi[:, m % 2, c * P:(c + 1) * P], ones[:, 0:1],
                                       start=(m == 0 and c == 0), stop=(m == 1), skip_group_check=True)
                    mm.then_inc(sq_used, 1)
                spread(S_LN)

                def scores(n):
                    qb, h = n // DIFF_H, n % DIFF_H
                    keys = (qb + 1) * P
                    if n == 0:
                        pe.wait_ge(vx_tok, l * 4 + 4)
                        pe.wait_ge(v_tok, l * 2 + 2)
                        pe.wait_ge(qk_ready, l * 4 + 4)
                    if n >= 2:
                        pe.wait_ge(a_exp, l * NUNIT + n - 1)
                    for c in range(2):
                        f = (2 * h + c) * DIFF_DK
                        t, r = f // P, f % P
                        bank = 2 + 2 * (n % 2) + c
                        pe.matmul(ps[:, bank, 0:keys], qk[r:r + DIFF_DK, t, qb * P:(qb + 1) * P],
                                  qk[r:r + DIFF_DK, 2 + t, 0:keys], start=True, stop=False)
                        mm = pe.matmul(ps[:, bank, keys - CHUNK:keys], const[r:r + 1, C_ROW:C_ROW + P],
                                       const[r:r + 1, C_ROW + P:C_ROW + P + CHUNK], start=False, stop=True)
                    mm.then_inc(a_s, 1)

                def mix_transpose(n):
                    pe.wait_ge(a_mix, l * NUNIT + n + 1)
                    if n == 0:
                        pe.wait_ge(ln_ready, l + 1)
                    else:
                        pe.wait_ge(a_trc, l * NUNIT + n)
                    for k in range(n // DIFF_H + 1):
                        mm = pe.transpose(ps[:, 6, k * P:(k + 1) * P], amix[:, n % 2, k * P:(k + 1) * P], ident)
                    mm.then_inc(a_tr, 1)

                def values(n):
                    qb, h = n // DIFF_H, n % DIFF_H
                    pe.wait_ge(a_trc, l * NUNIT + n + 1)
                    if h == 0 and qb >= 2:
                        pe.wait_ge(o_out, l * QB + qb - 1)
                    if n == 4:
                        pe.wait_ge(h_lo_done, l * NH + H_MIX + 2)
                    for k in range(qb + 1):
                        mm = pe.matmul(ps[:, (7, 1)[qb % 2], h * DIFF_DV:(h + 1) * DIFF_DV],
                                       amix_t[:, n % 2, k * P:(k + 1) * P], v[:, k, h * DIFF_DV:(h + 1) * DIFF_DV],
                                       start=(k == 0), stop=(k == qb))
                    mm.then_inc(a_pv, 1)

                def out_transpose(qb):
                    pe.wait_ge(o_out, l * QB + qb + 1)
                    pe.wait_ge(h_lo_done, l * NH + H_MIX + 2)
                    if qb >= 1:
                        pe.wait_ge(yc_lo, l * QB + qb)
                    for t in range(2):
                        mm = pe.transpose(ps[:, 0, t * P:(t + 1) * P], oc[:, t * P:(t + 1) * P], ident)
                    mm.then_inc(o_tr, 1)

                for t in range(NUNIT + 4):
                    if t < NUNIT:
                        scores(t)
                    if 1 <= t <= NUNIT:
                        mix_transpose(t - 1)
                    if 2 <= t <= NUNIT + 1:
                        values(t - 2)
                    if t >= 7 and (t - 7) % 4 == 0:
                        out_transpose((t - 7) // 4)

                project("wo", KD, h_rhs, [(yc_lo, l * QB + QB), (h_lo_done, l * NH + H_MIX + 6)])
                post_norm(S_POST2)
                pre_norm(S_PRE3)
                project("qx", KD, h_rhs, [(h_lo_done, l * NH + H_PRE3 + KD)])

                pe.wait_ge(dve_tiles, l * NDT + DT["qx"] + KD + RING)
                for t in range(QB + 1):
                    if t < QB:
                        if t >= 2:
                            pe.wait_ge(x_exp, l * QB + t - 1)
                        for h in range(X_H):
                            for c in range(2):
                                mm = pe.matmul(ps[:, 2 + 2 * (t % 2) + h // 2, (h % 2) * MEM:(h % 2 + 1) * MEM],
                                               qx[:, 2 * h + c, t * P:(t + 1) * P], kx[:, 2 * h + c, :],
                                               start=(c == 0), stop=(c == 1))
                        mm.then_inc(x_s, 1)
                    if t >= 1:
                        pe.wait_ge(x_nrm, l * QB + t)
                        if t >= 2:
                            pe.wait_ge(x_trc, l * QB + t - 1)
                        for mc in range(2):
                            for h in range(X_H):
                                mm = pe.transpose(ps[:, 6 + mc, h * P:(h + 1) * P],
                                                  px[:, (t - 1) % 2, h, mc * P:(mc + 1) * P], ident)
                        mm.then_inc(x_tr, 1)
                pe.wait_ge(x_trc, l * QB + QB)
                for n in range(2 * X_H):
                    if n >= 2:
                        pe.wait_ge(h_lo_done, l * NH + H_OX + n - 1)
                    for mc in range(2):
                        mm = pe.matmul(ps[:, n % 2, :], vx[:, mc, n * P:(n + 1) * P], pxt[:, mc, n // 2, :],
                                       start=(mc == 0), stop=(mc == 1))
                    mm.then_inc(x_pv, 1)
                project("xo", KD, h_rhs, [(h_lo_done, l * NH + H_OX + KD)])
                post_norm(S_POST3)
                pre_norm(S_PRE4)
                ffn(2, H_PRE4)
                post_norm(S_POST4)

        @block.scalar
        def _(act):
            act.wait_ge(consts_in, 64)
            act.wait_ge(trig_arg, 1)
            act.activation(sin_t[:], ang[:, 4, :], ACT.Sin).then_inc(trig_done, 1)
            act.activation(cos_t[:], ang[:, 5, :], ACT.Sin).then_inc(trig_done, 1)
            act.wait_ge(mem_in, 16)
            for m in range(KD):
                act.wait_ge(sq_used, m + 1)
                act.activation(epi[:, m % 2, 0:MEM], mem_f32[:, m, :], ACT.Square).then_inc(sq_ready, 1)
            act.wait_ge(lam_arg, 1)
            act.activation(lam_s[:], lam_s[:], ACT.Exp).then_inc(lam_exp, 1)

            with act.Fori(0, DEPTH) as l:
                LB = l * (NB // 2)

                def prep(p, s, kc):
                    act.wait_ge(w_loaded[s], (LB + p + 1) * 16)
                    act.wait_ge(w_used, 2 * (LB + p) + s + 1)
                    act.activation(w_hi[:, s, 0:kc, :], w_in_f32[:, s, 0:kc, :], ACT.Copy).then_inc(w_hi_done, 1)

                def pre_norm(no, first_h, gain):
                    for m in range(KD):
                        act.wait_ge(x_ready, l * 4 * KD + XR[no] + m + 2 if no != S_PRE1 else l * 4 * KD + 1)
                        act.wait_ge(sq_used, l * NSQ + KD + SQ[no] + m + 1)
                        act.activation(epi[:, m % 2, :], x[:, m, :], ACT.Square).then_inc(sq_ready, 1)
                        act.activation(h_hi[:, m, :], x[:, m, :], ACT.Copy, scale=g(gain, m)).then_inc(h_hi_done, 1)

                def y_square(name, no, m, s, y):
                    act.wait_ge(dve_tiles, l * NDT + DT[name] + m + 1 + RING)
                    act.wait_ge(ysq_free, l * 4 * KD + YSQ[no] + m + 1)
                    act.activation(epi[:, s, :], y[:, bass.ds(m, 1), :], ACT.Square).then_inc(ysq_ready, 1)

                def ffn(n, post):
                    base = BASE[f"f{n}gu"] // 2
                    fi = l * 2 * KF + (n - 1) * KF

                    def pair(j, kc):
                        prep(base + j + 1, 0, kc)
                        act.wait_ge(dve_tiles, l * NDT + DT[f"f{n}gu"] + 2 * j + 1 + RING)
                        act.activation(epi[:, 0, :], epi[:, 0, :], ACT.Silu).then_inc(silu_done, 1)
                        prep(base + j + 1, 1, kc)
                        act.wait_ge(prod_done, fi + j + 1)
                        act.activation(hid_hi[:, bass.ds(j, 1), :], epi[:, 1, :], ACT.Copy).then_inc(hid_hi_done, 1)

                    with act.Fori(0, KF - 1) as j:
                        pair(j, KD)
                    pair(KF - 1, KFH)
                    base = BASE[f"f{n}dn"] // 2

                    def out_pair(j, kc):
                        for s in range(2):
                            prep(base + 2 * j + 1 + s, 0, KFH if s == 0 else kc) if kc or s == 0 else None
                            prep(base + 2 * j + 1 + s, 1, KFH if s == 0 else kc) if kc or s == 0 else None
                            y_square(f"f{n}dn", post, 2 * j + s, s, y)

                    with act.Fori(0, KD // 2 - 1) as j:
                        out_pair(j, KFH)
                    out_pair(KD // 2 - 1, KD if n == 1 else None)

                def out_project(name, post):
                    with act.Fori(0, KD // 2) as j:
                        for s in range(2):
                            prep(BASE[name] // 2 + j + 1, s, KD)
                            y_square(name, post, 2 * j + s, s, y_r)

                act.wait_ge(par_ready, l + 1)
                prep(0, 0, KD)
                prep(0, 1, KD)
                pre_norm(S_PRE1, H_PRE1, "f1_pre_g")
                act.wait_ge(mem_n, l + 1)
                for m in range(KD):
                    act.activation(mem_hi[:, m, :], mem_f32[:, m, :], ACT.Copy, scale=g("x_mem_g", m)).then_inc(mem_hi_done, 1)
                ffn(1, S_POST1)

                for m in range(KD):
                    prep(BASE["kx"] // 2 + m // 2 + 1, m % 2, KD)
                    act.wait_ge(w_used, l * NB + BASE["kx"] + m + 1 + RING)
                    act.activation(kx[:, m, :], ps[:, m % 2, 0:MEM], ACT.Copy).then_inc(act_tiles, 1)
                    act.wait_ge(x_ready, l * 4 * KD + XR[S_PRE2] + m + 2)
                    act.wait_ge(sq_used, l * NSQ + KD + SQ[S_PRE2] + m + 1) if m < 2 else None
                    if m < 2:
                        act.activation(epi[:, m % 2, :], x[:, m, :], ACT.Square).then_inc(sq_ready, 1)
                    act.activation(h_hi[:, m, :], x[:, m, :], ACT.Copy, scale=g("mix_pre_g", m)).then_inc(h_hi_done, 1)
                for m in range(2, KD):
                    act.wait_ge(sq_used, l * NSQ + KD + SQ[S_PRE2] + m + 1)
                    act.activation(epi[:, m % 2, :], x[:, m, :], ACT.Square).then_inc(sq_ready, 1)

                for j in range(9):
                    prep(BASE["win"] // 2 + j + 1, 0, KD)
                    prep(BASE["win"] // 2 + j + 1, 1, KD)
                    if j == 2:
                        act.wait_ge(dve_tiles, l * NDT + DT["win"] + 4 + RING)
                        act.activation(gg[:], gg[:], ACT.Tanh, scale=0.5).then_inc(tanh_done, 1)
                act.wait_ge(u_ready, l + 1)
                for m in range(KD):
                    prep(BASE["vx"] // 2 + m // 2 + 1, m % 2, KD)
                    act.wait_ge(w_used, l * NB + BASE["vx"] + m + 1 + RING)
                    act.activation(vxt[:, m, :], ps[:, m % 2, 0:MEM], ACT.Copy).then_inc(act_tiles, 1)
                for t in range(2):
                    act.wait_ge(v_tr, l * 2 + t + 1)
                    act.activation(v[:, :, t * P:(t + 1) * P],
                                   ps[:, 4 + t, :].rearrange("p (c n) -> p c n", c=QB), ACT.Copy).then_inc(v_tok, 1)
                act.wait_ge(yb_ready, l + 1)
                for n in range(4):
                    act.wait_ge(vx_tr, l * 4 + n + 1)
                    act.activation(vx[:, n // 2, (n % 2) * SEQ:(n % 2 + 1) * SEQ], ps[:, 2 + n % 2, :], ACT.Copy)\
                        .then_inc(vx_tok, 1)
                for t in range(2):
                    act.wait_ge(pool_y, l * 2 + t + 1)
                    act.activation(h_hi[:, t, :], ps[:, t, :], ACT.Copy, scale=g("pool_scale", t)).then_inc(h_hi_done, 1)
                for t in range(2):
                    act.activation(h_hi[:, 2 + t, :], bg[:, t, :], ACT.Copy).then_inc(h_hi_done, 1)
                for t in range(2):
                    act.wait_ge(xc_ready, l * 2 + t + 1)
                    act.wait_ge(sq_used, l * NSQ + KD + SQ[S_LN] + t + 1)
                    act.activation(epi[:, t, :], u[:, t, :], ACT.Square).then_inc(sq_ready, 1)
                act.wait_ge(ln_ready, l + 1)
                for t in range(2):
                    act.activation(u[:, t, :], u[:, t, :], ACT.Silu, bias=g("ln_b", t)).then_inc(yd_ready, 1)
                for t in range(2):
                    act.wait_ge(yd_ready, l * 2 + t + 1)
                    act.activation(h_hi[:, 6 + t, :], u[:, t, :], ACT.Copy).then_inc(h_hi_done, 1)

                for t in range(NUNIT + 4):
                    if t < NUNIT:
                        act.wait_ge(a_max, l * NUNIT + t + 1)
                        if t >= 2:
                            act.wait_ge(a_mix, l * NUNIT + t - 1)
                        keys = (t // DIFF_H + 1) * P
                        for c in range(2):
                            e = act.activation(prob[:, t % 2, c, 0:keys], ps[:, 2 + 2 * (t % 2) + c, 0:keys], ACT.Exp,
                                               bias=att_s[:, t % 2, 0, c:c + 1], scale=DIFF_SCALE,
                                               accum_out=att_s[:, t % 2, 1, c:c + 1])
                        e.then_inc(a_exp, 1)
                    if 1 <= t <= NUNIT:
                        n = t - 1
                        keys = (n // DIFF_H + 1) * P
                        act.wait_ge(a_tr, l * NUNIT + n + 1)
                        if n >= 2:
                            act.wait_ge(a_pv, l * NUNIT + n - 1)
                        act.activation(amix_t[:, n % 2, 0:keys], ps[:, 6, 0:keys], ACT.Copy).then_inc(a_trc, 1)
                    if t >= 6 and (t - 6) % 4 == 0:
                        qb = (t - 6) // 4
                        act.wait_ge(a_pv, l * NUNIT + 4 * qb + 4)
                        if qb >= 1:
                            act.wait_ge(o_out, l * QB + qb)
                        for h in range(DIFF_H):
                            e = act.activation(junk[:, h, :], ps[:, (7, 1)[qb % 2], h * DIFF_DV:(h + 1) * DIFF_DV],
                                               ACT.Square, accum_out=stat[:, 3, h:h + 1])
                        e.then_inc(o_sq, 1)
                    if t >= 7 and (t - 7) % 4 == 0:
                        qb = (t - 7) // 4
                        act.wait_ge(o_tr, l * QB + qb + 1)
                        for f in range(2):
                            e = act.activation(h_hi[:, 4 + f, qb * P:(qb + 1) * P], ps[:, 0, f * P:(f + 1) * P],
                                               ACT.Copy, scale=g("subln"))
                        e.then_inc(yc_hi, 1)

                out_project("wo", S_POST2)
                pre_norm(S_PRE3, H_PRE3, "x_pre_g")
                with act.Fori(0, KD // 2) as j:
                    prep(BASE["qx"] // 2 + j + 1, 0, KD)
                    prep(BASE["qx"] // 2 + j + 1, 1, KD)
                for t in range(QB + 1):
                    if t < QB:
                        act.wait_ge(x_max, l * QB + t + 1)
                        if t >= 2:
                            act.wait_ge(x_tr, l * QB + t - 1)
                        for h in range(X_H):
                            e = act.activation(px[:, t % 2, h, :],
                                               ps[:, 2 + 2 * (t % 2) + h // 2, (h % 2) * MEM:(h % 2 + 1) * MEM], ACT.Exp,
                                               bias=att_s[:, t % 2, 0, h:h + 1], scale=X_SCALE,
                                               accum_out=att_s[:, t % 2, 1, h:h + 1])
                        e.then_inc(x_exp, 1)
                    if t >= 1:
                        act.wait_ge(x_tr, l * QB + t)
                        for mc in range(2):
                            e = act.activation(pxt[:, mc, :, (t - 1) * P:t * P],
                                               ps[:, 6 + mc, :].rearrange("p (h n) -> p h n", h=X_H), ACT.Copy)
                        e.then_inc(x_trc, 1)
                for n in range(2 * X_H):
                    act.wait_ge(x_pv, l * 2 * X_H + n + 1)
                    act.activation(h_hi[:, n, :], ps[:, n % 2, :], ACT.Copy).then_inc(h_hi_done, 1)
                out_project("xo", S_POST3)
                pre_norm(S_PRE4, H_PRE4, "f2_pre_g")
                ffn(2, S_POST4)

        @block.gpsimd
        def _(pool):
            pool.memset(ones[:], 1.0)
            pool.memset(mean256[:], 1.0 / (2 * P))
            pool.drain()
            pool.sem_inc(setup_p, 1)
            pool.sem_inc(w_lo_done, RING)
            pool.sem_inc(ysq_free, 2)

            with pool.Fori(0, DEPTH) as l:
                LB = l * (NB // 2)

                def prep(p, s, kc):
                    pool.wait_ge(w_hi_done, 2 * (LB + p) + s + 1)
                    pool.tensor_tensor(w_lo[:, s, 0:kc, :], w_in_f32[:, s, 0:kc, :],
                                       w_hi[:, s, 0:kc, :].bitcast(F32), ALU.subtract).then_inc(w_lo_done, 1)

                def y_square(no, m, s):
                    pool.wait_ge(ysq_ready, l * 4 * KD + YSQ[no] + m + 1)
                    pool.tensor_tensor(acc[:], acc[:], epi[:, s, :], ALU.add)
                    pool.drain()
                    pool.sem_inc(ysq_free, 1)
                    pool.sem_inc(ysq_used, 1)

                def ffn(n, post):
                    base = BASE[f"f{n}gu"] // 2
                    with pool.Fori(0, KF - 1) as j:
                        prep(base + j + 1, 0, KD)
                        prep(base + j + 1, 1, KD)
                    prep(base + KF, 0, KFH)
                    prep(base + KF, 1, KFH)
                    base = BASE[f"f{n}dn"] // 2

                    def out_pair(j, kc, first):
                        for s in range(2):
                            if kc or s == 0:
                                prep(base + 2 * j + 1 + s, 0, KFH if s == 0 else kc)
                            if first and s == 0:
                                pool.memset(acc[:], 0.0)
                                pool.drain()
                            if kc or s == 0:
                                prep(base + 2 * j + 1 + s, 1, KFH if s == 0 else kc)
                            y_square(post, 2 * j + s, s)

                    out_pair(0, KFH, True)
                    with pool.Fori(1, KD // 2 - 1) as j:
                        out_pair(j, KFH, False)
                    out_pair(KD // 2 - 1, KD if n == 1 else None, False)

                def out_project(name, post):
                    for s in range(2):
                        prep(BASE[name] // 2 + 1, s, KD)
                        if s == 0:
                            pool.memset(acc[:], 0.0)
                            pool.drain()
                        y_square(post, s, s)
                    with pool.Fori(1, KD // 2) as j:
                        for s in range(2):
                            prep(BASE[name] // 2 + j + 1, s, KD)
                            y_square(post, 2 * j + s, s)

                prep(0, 0, KD)
                prep(0, 1, KD)
                ffn(1, S_POST1)
                for m in range(KD):
                    prep(BASE["kx"] // 2 + m // 2 + 1, m % 2, KD)
                pool.memset(za[:, :, 0:PAD], 0.0)
                pool.memset(zb[:, :, 0:PAD], 0.0)
                pool.memset(zc[:, :, 0:PAD], 0.0)
                pool.memset(cpad[:, :, 0:SCW - 1], 0.0)
                pool.memset(upad[:, :, 0:CFW - 1], 0.0)
                pool.drain()
                pool.sem_inc(pads_done, 1)
                for j in range(9):
                    prep(BASE["win"] // 2 + j + 1, 0, KD)
                    prep(BASE["win"] // 2 + j + 1, 1, KD)
                    if j == 4:
                        pool.wait_ge(dve_tiles, l * NDT + DT["win"] + 8 + RING)
                        pool.tensor_tensor(cpad[:, :, SCW - 1:], cg[:], xs[:], ALU.mult).then_inc(c_done, 1)
                    if j == 6:
                        pool.wait_ge(dve_tiles, l * NDT + DT["win"] + 12 + RING)

                        def shifted(t, part, tile, by):
                            return t[part, tile, PAD - by:PAD - by + SEQ]
                        every, upper = slice(0, P), slice(P // 2, P)
                        for src, dst, part, t, by in (
                                (za, zb, every, 0, 1), (za, zb, every, 1, 1),
                                (zb, zc, every, 1, 2), (zb, zc, upper, 0, 2),
                                (zc, zb, every, 1, 4),
                                (zb, zc, upper, 1, 8)):
                            if (t, by) != (0, 1):
                                pool.drain()
                            pool.tensor_tensor(shifted(dst, part, t, 0), shifted(src, part, t, 0),
                                               shifted(src, part, t, by), ALU.add)
                        for t in range(2):
                            pool.drain()
                            pool.tensor_copy(shifted(zb, upper, t, 0), shifted(zc, upper, t, 0))
                        pool.drain()
                        pool.sem_inc(pool_sums, 1)
                for i in range(4):
                    pool.wait_ge(rope_shuf, l * 4 + i + 1)
                    pool.tensor_tensor(rope[:, i, :], rope[:, i, :], sin_t[:], ALU.mult)
                    pool.tensor_tensor(qk[:, i, :], qk[:, i, :], cos_t[:], ALU.mult)
                    pool.drain()
                    pool.sem_inc(rope_mul, 1)
                    prep(BASE["vx"] // 2 + i // 2 + 1, i % 2, KD)
                for m in range(4, KD):
                    prep(BASE["vx"] // 2 + m // 2 + 1, m % 2, KD)
                out_project("wo", S_POST2)
                with pool.Fori(0, KD // 2) as j:
                    prep(BASE["qx"] // 2 + j + 1, 0, KD)
                    prep(BASE["qx"] // 2 + j + 1, 1, KD)
                out_project("xo", S_POST3)
                ffn(2, S_POST4)

        @block.vector
        def _(dve):
            stt = dve.scalar_tensor_tensor

            def rsqrt(src, n, count):
                hv, r, w = stat[:, 0, 0:n], stat[:, 1, 0:n], stat[:, 2, 0:n]
                dve.tensor_scalar(w, src, 1.0 / count, EPS, ALU.mult, ALU.add)
                dve.drain()
                dve.tensor_scalar(hv, w, -0.5, None, ALU.mult)
                dve.tensor_scalar(r.bitcast(I32), w.bitcast(I32), -0.5, float(0x5F3759DF), ALU.mult, ALU.add)
                dve.drain()
                for _ in range(3):
                    dve.tensor_tensor(w, r, r, ALU.mult)
                    dve.drain()
                    dve.tensor_tensor(w, w, hv, ALU.mult)
                    dve.drain()
                    stt(r, w, 1.5, r, ALU.add, ALU.mult)
                    dve.drain()

            def token_factors(no, summed, n_summed, width, count, dst):
                n = width // P
                dve.wait_ge(summed, n_summed)
                rsqrt(ps[:, B_STAT, 0:n], n, count)
                dve.tensor_tensor(diag[:, 0:n, :], ident.rearrange("p (o n) -> p o n", o=1).to_broadcast([P, n, P]),
                                  stat[:, 1, 0:n].rearrange("p (n o) -> p n o", o=1).to_broadcast([P, n, P]),
                                  ALU.mult).then_inc(stat_diag, 1)
                dve.wait_ge(stat_bc, no + 1)
                dve.tensor_copy(dst, ps[:, B_BC, 0:width])
                dve.drain()

            dve.sem_inc(dve_tiles, RING)
            dve.sem_inc(act_tiles, RING)
            dve.wait_ge(x_in, 16)
            dve.sem_inc(x_ready, 1)
            dve.wait_ge(consts_in, 64)
            ang_, k, kh, kl = ang[:, 0, :], ang[:, 1, :], ang[:, 2, :], ang[:, 3, :]
            two_pi = 2 * math.pi
            c1 = math.floor(two_pi * 2 ** 9) / 2 ** 9
            c2 = math.floor((two_pi - c1) * 2 ** 22) / 2 ** 22
            c3 = two_pi - c1 - c2
            dve.tensor_copy(ang_, pos_i[:])
            dve.drain()
            dve.tensor_scalar(ang_, ang_, const[:, C_FREQ:C_FREQ + 1], None, ALU.mult)
            dve.drain()
            dve.tensor_scalar(k, ang_, 1 / two_pi, 1.5 * 2 ** 23, ALU.mult, ALU.add)
            dve.drain()
            dve.tensor_scalar(k, k, 1.5 * 2 ** 23, None, ALU.subtract)
            dve.drain()
            dve.tensor_scalar(kh, k, 1.5 * 2 ** 35, None, ALU.add)
            dve.drain()
            dve.tensor_scalar(kh, kh, 1.5 * 2 ** 35, None, ALU.subtract)
            dve.drain()
            dve.tensor_tensor(kl, k, kh, ALU.subtract)
            dve.drain()
            for part in (c1, c2):
                for kk in (kh, kl):
                    stt(ang_, kk, -part, ang_, ALU.mult, ALU.add)
                    dve.drain()
            stt(ang_, k, -c3, ang_, ALU.mult, ALU.add)
            dve.drain()
            dve.tensor_scalar(ang[:, 4, :], ang_, 3.1415925, -3.1415925, ALU.min, ALU.max)
            dve.tensor_scalar(kh, ang_, -1.0, None, ALU.mult)
            dve.drain()
            dve.tensor_tensor(kh, kh, ang_, ALU.max)
            dve.drain()
            dve.tensor_scalar(ang[:, 5, :], kh, -1.0, math.pi / 2, ALU.mult, ALU.add)
            dve.drain()
            dve.sem_inc(trig_arg, 1)
            for a in range(2):
                dve.tensor_tensor(lam_p[:, :, a, :], lam_in[:, :, 2 * a, :], lam_in[:, :, 2 * a + 1, :], ALU.mult)
            dve.drain()
            dve.tensor_reduce(lam_s[:], lam_p[:], AX.X, ALU.add)
            dve.drain()
            dve.sem_inc(lam_arg, 1)
            for l in range(DEPTH):
                for name in ("f1_post_g", "f2_post_g"):
                    c = par_all[:, l, PAR[name]:PAR[name] + KD]
                    dve.tensor_scalar(c, c, 0.5, None, ALU.mult)
                c = par_all[:, l, PAR["conf_w"]:PAR["conf_w"] + 2 * CFW]
                dve.tensor_scalar(c, c, 0.5, None, ALU.mult)
                c = par_all[:, l, PAR["subln"]:PAR["subln"] + 1]
                dve.tensor_scalar(c, c, 1.0 - (0.8 - 0.6 * math.exp(-0.3 * l)), None, ALU.mult)
            dve.wait_ge(trig_done, 2)
            dve.tensor_scalar(sin_t[:], sin_t[:], const[:, C_SIGN:C_SIGN + 1], None, ALU.mult)
            token_factors(0, sq_used, 2 + KD, MEM, D, r_mem[:])
            dve.wait_ge(lam_exp, 1)
            for l in range(DEPTH):
                stt(neg_lam[:, l:l + 1], lam_s[:, 2 * l + 1:2 * l + 2], -(0.8 - 0.6 * math.exp(-0.3 * l)),
                    lam_s[:, 2 * l:2 * l + 1], ALU.add, ALU.subtract)
            dve.drain()
            dve.sem_inc(setup_d, 1)

            with dve.Fori(0, DEPTH) as l:
                def lo_of(m_dst, in0, gain=None):
                    hi = h_hi[:, m_dst, :].bitcast(F32)
                    if gain is None:
                        dve.tensor_tensor(h_lo[:, m_dst, :], in0, hi, ALU.subtract).then_inc(h_lo_done, 1)
                    else:
                        stt(h_lo[:, m_dst, :], in0, gain, hi, ALU.mult, ALU.subtract).then_inc(h_lo_done, 1)

                def pre_norm(no, first_h, gain):
                    for m in range(KD):
                        dve.wait_ge(h_hi_done, l * NH + first_h + m + 1)
                        lo_of(m, x[:, m, :], g(gain, m))
                    token_factors(l * NSTAT + 1 + no, sq_used, l * NSQ + KD + SQ[no] + KD + 2, SEQ, D, r_pre[:])

                def post_norm(no, gain, y):
                    token_factors(l * NSTAT + 1 + no, stat_sum, l * 4 + YSQ[no] // KD + 1, SEQ, D, r_post[:])
                    for m in range(KD):
                        stt(y[:, m, :], y[:, m, :], g(gain, m), r_post[:], ALU.mult, ALU.mult)
                        dve.drain()
                        dve.tensor_tensor(x[:, m, :], x[:, m, :], y[:, m, :], ALU.add).then_inc(x_ready, 1)

                def ffn(n, post):
                    tile0 = l * NB + BASE[f"f{n}gu"]
                    fi = l * 2 * KF + (n - 1) * KF
                    with dve.Fori(0, KF) as j:
                        dve.wait_ge(w_used, tile0 + 2 * j + 1 + RING)
                        dve.tensor_tensor(epi[:, 0, :], ps[:, 0, :], r_pre[:], ALU.mult).then_inc(dve_tiles, 1)
                        dve.wait_ge(w_used, tile0 + 2 * j + 2 + RING)
                        dve.tensor_tensor(epi[:, 1, :], ps[:, 1, :], r_pre[:], ALU.mult).then_inc(dve_tiles, 1)
                        dve.drain()
                        dve.wait_ge(silu_done, fi + j + 1)
                        dve.tensor_tensor(epi[:, 1, :], epi[:, 1, :], epi[:, 0, :], ALU.mult).then_inc(prod_done, 1)
                        dve.drain()
                        dve.wait_ge(hid_hi_done, fi + j + 1)
                        dve.tensor_tensor(hid_lo[:, bass.ds(j, 1), :], epi[:, 1, :],
                                          hid_hi[:, bass.ds(j, 1), :].bitcast(F32), ALU.subtract).then_inc(hid_lo_done, 1)
                        dve.drain()
                    with dve.Fori(0, KD // 2) as j:
                        for s in range(2):
                            dve.wait_ge(w_used, l * NB + BASE[f"f{n}dn"] + 4 * j + 2 * s + 2 + RING)
                            dve.tensor_copy(y[:, bass.ds(2 * j + s, 1), :], ps[:, s, :]).then_inc(dve_tiles, 1)
                    dve.drain()
                    post_norm(*post, y)

                def out_project(name, post):
                    with dve.Fori(0, KD // 2) as j:
                        for s in range(2):
                            dve.wait_ge(w_used, l * NB + BASE[name] + 2 * j + s + 1 + RING)
                            dve.tensor_copy(y_r[:, bass.ds(2 * j + s, 1), :], ps[:, s, :]).then_inc(dve_tiles, 1)
                    dve.drain()
                    post_norm(*post, y_r)

                dve.drain()
                dve.tensor_copy(par[:], par_all[:, bass.ds(l, 1), :])
                dve.tensor_copy(neg_lam_l[:], neg_lam[:, bass.ds(l, 1)])
                dve.drain()
                dve.sem_inc(par_ready, 1)
                pre_norm(S_PRE1, H_PRE1, "f1_pre_g")
                dve.wait_ge(mem_in, l * 16 + 32)
                dve.tensor_tensor(mem_f32[:], mem_f32[:],
                                  r_mem[:].rearrange("p (o n) -> p o n", o=1).to_broadcast([P, KD, MEM]), ALU.mult)
                dve.drain()
                dve.sem_inc(mem_n, 1)
                for m in range(KD):
                    dve.wait_ge(mem_hi_done, l * KD + m + 1)
                    stt(mem_lo[:, m, :], mem_f32[:, m, :], g("x_mem_g", m), mem_hi[:, m, :].bitcast(F32),
                        ALU.mult, ALU.subtract).then_inc(mem_lo_done, 1)
                dve.drain()
                ffn(1, (S_POST1, "f1_post_g"))
                pre_norm(S_PRE2, H_PRE2, "mix_pre_g")

                dve.wait_ge(pads_done, l + 1)
                dests = ([ga[:, t, :] for t in range(2)] + [gg[:, t, :] for t in range(2)] + [xs[:, t, :] for t in range(2)]
                         + [cg[:, t, :] for t in range(2)] + [bg[:, t, :] for t in range(2)]
                         + [za[:, t, PAD:PAD + SEQ] for t in range(2)] + [qk[:, t, :] for t in range(4)]
                         + [vt[:, t, :] for t in range(2)])
                per_tile = -(-(CFW - 1) // 13)
                done_taps = 0
                for i in range(18):
                    dve.wait_ge(w_used, l * NB + BASE["win"] + i + 1 + RING)
                    dve.tensor_tensor(dests[i], ps[:, i % 2, :], r_pre[:], ALU.mult).then_inc(dve_tiles, 1)
                    if i == 4:
                        dve.wait_ge(tanh_done, l + 1)
                        stt(upad[:, :, CFW - 1:], gg[:], 1.0, ga[:], ALU.add, ALU.mult)
                        dve.drain()
                        for t in range(2):
                            dve.tensor_scalar(u[:, t, :], upad[:, t, CFW - 1:CFW - 1 + SEQ], g("conf_w", 2 * (CFW - 1) + t),
                                              g("conf_b", t), ALU.mult, ALU.add)
                        dve.drain()
                    if i >= 5:
                        n = min(per_tile, CFW - 1 - done_taps)
                        if n > 0:
                            with dve.Fori(done_taps, done_taps + n) as tap:
                                for t in range(2):
                                    stt(u[:, t, :], upad[:, t, bass.ds(tap, SEQ)],
                                        par[:, bass.ds(PAR["conf_w"] + t + 2 * tap, 1)], u[:, t, :], ALU.mult, ALU.add)
                                dve.drain()
                            done_taps += n
                assert done_taps == CFW - 1
                dve.sem_inc(u_ready, 1)
                half = ROT // 2
                swap = [i + half if i < half else i - half if i < ROT else i for i in range(32)]
                for i in range(4):
                    dve.stream_shuffle(rope[:, i, :], qk[:, i, :], swap).then_inc(rope_shuf, 1)
                dve.wait_ge(c_done, l + 1)
                for t in range(2):
                    dve.tensor_scalar(xs[:, t, :], cpad[:, t, 0:SEQ], g("sconv_w", t), None, ALU.mult)
                dve.drain()
                for k_ in range(1, SCW):
                    for t in range(2):
                        stt(xs[:, t, :], cpad[:, t, k_:k_ + SEQ], g("sconv_w", 2 * k_ + t), xs[:, t, :], ALU.mult, ALU.add)
                    dve.drain()
                dve.tensor_tensor(bg[:], bg[:], xs[:], ALU.mult)
                dve.drain()
                dve.sem_inc(yb_ready, 1)
                dve.wait_ge(pool_sums, l + 1)
                for t in range(2):
                    edge = zc[:, t, PAD:2 * PAD]
                    dve.tensor_tensor(edge, zb[:, t, PAD:2 * PAD], const[:, C_EDGE + t * PAD:C_EDGE + (t + 1) * PAD], ALU.mult)
                    dve.drain()
                    stt(zb[:, t, PAD:PAD + SEQ], zb[:, t, PAD:PAD + SEQ], const[:, C_INVW + t:C_INVW + t + 1],
                        za[:, t, PAD:PAD + SEQ], ALU.mult, ALU.subtract)
                    dve.drain()
                    dve.tensor_tensor(zb[:, t, PAD:2 * PAD], edge, za[:, t, PAD:2 * PAD], ALU.subtract).then_inc(mixed, 1)
                for i in range(4):
                    dve.wait_ge(rope_mul, l * 4 + i + 1)
                    dve.tensor_tensor(qk[:, i, :], qk[:, i, :], rope[:, i, :], ALU.add).then_inc(qk_ready, 1)
                dve.wait_ge(mu_done, l + 1)
                for t in range(2):
                    dve.tensor_tensor(u[:, t, :], u[:, t, :], ps[:, 6, :], ALU.subtract).then_inc(xc_ready, 1)
                for t in range(2):
                    dve.wait_ge(h_hi_done, l * NH + H_MIX + t + 1)
                    lo_of(t, ps[:, t, :], g("pool_scale", t))
                for t in range(2):
                    dve.wait_ge(h_hi_done, l * NH + H_MIX + 2 + t + 1)
                    lo_of(2 + t, bg[:, t, :])
                token_factors(l * NSTAT + 1 + S_LN, sq_used, l * NSQ + KD + SQ[S_LN] + 4, SEQ, 2 * P, r_post[:])
                for t in range(2):
                    stt(u[:, t, :], u[:, t, :], g("ln_g", t), r_post[:], ALU.mult, ALU.mult)
                dve.drain()
                dve.sem_inc(ln_ready, 1)
                for t in range(2):
                    dve.wait_ge(h_hi_done, l * NH + H_MIX + 4 + t + 1)
                    lo_of(6 + t, u[:, t, :])

                for t in range(NUNIT + 4):
                    if t < NUNIT:
                        keys = (t // DIFF_H + 1) * P
                        dve.wait_ge(a_s, l * NUNIT + t + 1)
                        b = 2 + 2 * (t % 2)
                        dve.tensor_reduce(att_s[:, t % 2, 0, 0:2], ps[:, b:b + 2, 0:keys], AX.X, ALU.max, negate=True)
                        dve.drain()
                        m_ = att_s[:, t % 2, 0, 0:2]
                        dve.tensor_scalar(m_, m_, DIFF_SCALE, None, ALU.mult).then_inc(a_max, 1)
                    if 1 <= t <= NUNIT:
                        n = t - 1
                        keys = (n // DIFF_H + 1) * P
                        r = att_s[:, n % 2, 2, 0:2]
                        dve.wait_ge(a_exp, l * NUNIT + n + 1)
                        if n >= 2:
                            dve.wait_ge(a_tr, l * NUNIT + n - 1)
                        dve.reciprocal(r, att_s[:, n % 2, 1, 0:2])
                        dve.drain()
                        dve.tensor_scalar(r[:, 1:2], r[:, 1:2], neg_lam_l[:], None, ALU.mult)
                        dve.tensor_scalar(amix[:, n % 2, 0:keys], prob[:, n % 2, 0, 0:keys], r[:, 0:1], None, ALU.mult)
                        dve.drain()
                        stt(amix[:, n % 2, 0:keys], prob[:, n % 2, 1, 0:keys], r[:, 1:2], amix[:, n % 2, 0:keys],
                            ALU.mult, ALU.add).then_inc(a_mix, 1)
                    if t >= 6 and (t - 6) % 4 == 0:
                        qb = (t - 6) // 4
                        dve.wait_ge(o_sq, l * QB + qb + 1)
                        rsqrt(stat[:, 3, :], DIFF_H, DIFF_DV)
                        if qb >= 1:
                            dve.wait_ge(o_tr, l * QB + qb)
                        dve.tensor_tensor(oc[:].rearrange("p (h n) -> p h n", h=DIFF_H),
                                          ps[:, (7, 1)[qb % 2], 0:2 * P].rearrange("p (h n) -> p h n", h=DIFF_H),
                                          stat[:, 1, 0:DIFF_H].rearrange("p (h o) -> p h o", o=1)
                                          .to_broadcast([P, DIFF_H, DIFF_DV]), ALU.mult).then_inc(o_out, 1)
                    if t >= 7 and (t - 7) % 4 == 0:
                        qb = (t - 7) // 4
                        dve.wait_ge(yc_hi, l * QB + qb + 1)
                        for f in range(2):
                            e = stt(h_lo[:, 4 + f, qb * P:(qb + 1) * P], ps[:, 0, f * P:(f + 1) * P], g("subln"),
                                    h_hi[:, 4 + f, qb * P:(qb + 1) * P].bitcast(F32), ALU.mult, ALU.subtract)
                        e.then_inc(yc_lo, 1)

                out_project("wo", (S_POST2, "mix_post_g"))
                pre_norm(S_PRE3, H_PRE3, "x_pre_g")
                with dve.Fori(0, KD // 2) as j:
                    for s in range(2):
                        dve.wait_ge(w_used, l * NB + BASE["qx"] + 2 * j + s + 1 + RING)
                        dve.tensor_tensor(qx[:, bass.ds(2 * j + s, 1), :], ps[:, s, :], r_pre[:], ALU.mult).then_inc(dve_tiles, 1)
                dve.drain()
                for t in range(QB + 1):
                    if t < QB:
                        b = 2 + 2 * (t % 2)
                        m_ = att_s[:, t % 2, 0, :]
                        dve.wait_ge(x_s, l * QB + t + 1)
                        dve.tensor_reduce(m_, ps[:, b:b + 2, :].rearrange("p b (h n) -> p (b h) n", h=2), AX.X, ALU.max, negate=True)
                        dve.drain()
                        dve.tensor_scalar(m_, m_, X_SCALE, None, ALU.mult).then_inc(x_max, 1)
                    if t >= 1:
                        n = t - 1
                        dve.wait_ge(x_exp, l * QB + n + 1)
                        dve.reciprocal(att_s[:, n % 2, 2, :], att_s[:, n % 2, 1, :])
                        dve.drain()
                        for h in range(X_H):
                            e = dve.tensor_scalar(px[:, n % 2, h, :], px[:, n % 2, h, :], att_s[:, n % 2, 2, h:h + 1], None, ALU.mult)
                        e.then_inc(x_nrm, 1)
                for n in range(2 * X_H):
                    dve.wait_ge(h_hi_done, l * NH + H_OX + n + 1)
                    lo_of(n, ps[:, n % 2, :])
                dve.drain()
                out_project("xo", (S_POST3, "x_post_g"))
                pre_norm(S_PRE4, H_PRE4, "f2_pre_g")
                ffn(2, (S_POST4, "f2_post_g"))


def _blocks(w, kc):
    L, K, N = w.shape
    w = w.reshape(L, K // (kc * P), kc, P, N // P, P)
    return w.transpose(0, 4, 1, 3, 2, 5).reshape(L, -1, P, kc * P)


def _columns(a):
    a = np.asarray(a)
    L = a.shape[0]
    return a.reshape(L, -1, P).transpose(2, 0, 1)


def _constants():
    c = np.zeros((P, NCONST), np.float32)
    c[:, C_ID:C_ID + P] = np.eye(P, dtype=np.float32)
    inv = np.float32(THETA) ** (-np.arange(0, ROT, 2, dtype=np.float32) / np.float32(ROT))
    for p in range(P):
        d = p % DIFF_DK
        if d < ROT:
            c[p, C_FREQ] = inv[d % (ROT // 2)]
            c[p, C_SIGN] = -1.0 if d < ROT // 2 else 1.0
        for t in range(2):
            w = POOL_WINDOWS[2 * t + p // 64]
            c[p, C_INVW + t] = 1.0 / w
            for i in range(POOL_WINDOWS[-1]):
                c[p, C_EDGE + t * POOL_WINDOWS[-1] + i] = 1.0 / min(i + 1, w)
    c[::DIFF_DK, C_ROW:C_ROW + CHUNK] = 1.0
    c[::DIFF_DK, C_ROW + P:] = -1e30
    return c


def kernel(**a):
    import concourse.bacc as bacc
    from concourse.bass_utils import run_bass_kernel_spmd as run

    a = {k: np.asarray(v) for k, v in a.items()}
    win = a["w_in"]
    G = 2 * P
    win = np.concatenate([win[:, :, i * G:(i + 1) * G] for i in (7, 8, 1, 3, 2, 0, 4, 5, 6)], axis=2)

    def gate_up(n):
        gt, up = _blocks(a[f"f{n}_w_gate"], KD), _blocks(a[f"f{n}_w_up"], KD)
        return np.stack([gt, up], axis=2).reshape(DEPTH, 2 * KF, P, KD * P)

    w8 = np.concatenate([gate_up(1)] + [_blocks(w, KD) for w in (a["x_wk"], win, a["x_wv"], a["w_o"], a["x_wq"], a["x_wo"])]
                        + [gate_up(2)], axis=1)
    wd = np.concatenate([_blocks(a["f1_w_down"], KFH), _blocks(a["f2_w_down"], KFH)], axis=1)
    par = np.concatenate([_columns(a[n]) for n in ("f1_pre_g", "f1_post_g", "mix_pre_g", "mix_post_g", "x_pre_g", "x_mem_g",
                                                   "x_post_g", "f2_pre_g", "f2_post_g", "pool_scale", "sconv_w")]
                         + [np.tile(a["diff_subln_g"], (1, 2)).T.reshape(P, DEPTH, 1)]
                         + [_columns(a[n]) for n in ("conf_dw_w", "conf_dw_b", "conf_ln_g", "conf_ln_b")], axis=2)
    poolw = np.zeros((DEPTH, P, 2, P), np.float32)
    for t in range(2):
        for s in range(2):
            poolw[:, 64 * s:64 * s + 64, t, 64 * s:64 * s + 64] = a["pool_w"][:, 2 * t + s]
    lam = np.stack([a["lam_q1"], a["lam_k1"], a["lam_q2"], a["lam_k2"]], axis=1).reshape(1, -1)
    ins = {
        "xT": a["x"][0].T.reshape(KD, P, SEQ).transpose(1, 0, 2),
        "memT": a["mem"][0].T.reshape(KD, P, MEM).transpose(1, 0, 2),
        "pos": a["positions"].reshape(1, SEQ),
        "w8": w8.reshape(-1, P, KD * P), "wd": wd.reshape(-1, P, KFH * P),
        "par": par, "poolw": poolw, "lam": lam, "const": _constants(),
    }
    ins = {k: np.ascontiguousarray(v) for k, v in ins.items()}
    nc = bacc.Bacc("TRN2", target_bir_lowering=False, num_devices=1)
    aps = [nc.dram_tensor(k, v.shape, mybir.dt.from_np(v.dtype), kind="ExternalInput").ap() for k, v in ins.items()]
    out = nc.dram_tensor("out", (P, KD, SEQ), F32, kind="ExternalOutput").ap()
    build(nc, *aps, out)
    got = run(nc, [ins], core_ids=[0]).results[0]["out"]
    return np.ascontiguousarray(got.transpose(1, 0, 2).reshape(D, SEQ).T)[None]
```

```python
import math
from contextlib import ExitStack

import numpy as np

import concourse.bass as bass
from concourse import mybir

F32, F32R, I32 = mybir.dt.float32, mybir.dt.float32r, mybir.dt.int32
ALU, ACT, AX = mybir.AluOpType, mybir.ActivationFunctionType, mybir.AxisListType

P, D, SEQ, DEPTH, MEM, FF = 128, 1024, 512, 2, 256, 2816
KD, KF, KFH = D // P, FF // P, FF // P // 2
EPS = 1e-6
POOL_WINDOWS = (2, 4, 8, 16)
SCW, CFW = 3, 31
DIFF_DK, DIFF_DV, DIFF_H, X_H, X_HD, CHUNK = 32, 64, 4, 4, 256, 64
ROT, THETA = DIFF_DK // 4, 500000.0
QB = SEQ // P

SIZES = (("f1gu", 2 * KF), ("f1dn", 2 * KD), ("kx", KD), ("win", 18), ("wo", KD), ("vx", KD),
         ("qx", KD), ("xo", KD), ("f2gu", 2 * KF), ("f2dn", 2 * KD))
BASE, NB = {}, 0
for _n, _k in SIZES:
    BASE[_n] = NB
    NB += _k
DT, NDT = {}, 0
for _n, _k in (("f1gu", 2 * KF), ("f1dn", KD), ("win", 18), ("wo", KD), ("qx", KD), ("xo", KD),
               ("f2gu", 2 * KF), ("f2dn", KD)):
    DT[_n] = NDT
    NDT += _k
NAT = 2 * KD
RING = 2
WARM_UP = 6

PAR, NPAR = {}, 0
for _n, _k in (("f1_pre_g", KD), ("f1_post_g", KD), ("mix_pre_g", KD), ("mix_post_g", KD),
               ("x_pre_g", KD), ("x_mem_g", KD), ("x_post_g", KD), ("f2_pre_g", KD),
               ("f2_post_g", KD), ("pool_scale", 2), ("sconv_w", 2 * SCW), ("subln", 1),
               ("conf_w", 2 * CFW), ("conf_b", 2), ("ln_g", 2), ("ln_b", 2)):
    PAR[_n] = NPAR
    NPAR += _k
C_ID, C_FREQ, C_SIGN, C_INVW, C_EDGE, C_ROW = 0, 128, 129, 130, 132, 164
NCONST = C_ROW + 128 + CHUNK

(S_PRE1, S_MEM, S_POST1, S_PRE2, S_LN, S_POST2, S_PRE3, S_POST3, S_PRE4, S_POST4), NSTAT = range(10), 10
H_PRE1, H_PRE2, H_MIX, H_PRE3, H_OX, H_PRE4, NH = 0, 8, 16, 22, 30, 38, 46
POST = {"f1dn": (S_POST1, 0), "wo": (S_POST2, 1), "xo": (S_POST3, 2), "f2dn": (S_POST4, 3)}
NY = KD - 1
XD = {S_PRE2: 0, S_PRE3: 4, S_PRE4: 8, S_PRE1: 11}
NXD, NXP, X0 = 14, 2, 3
NUNIT = QB * DIFF_H
DIFF_SCALE, X_SCALE = DIFF_DK ** -0.5, X_HD ** -0.5


def build(nc, x_d, mem_d, pos_d, w8_d, wd_d, par_d, poolw_d, lam_d, const_d, out_d):
    ctx = ExitStack()
    with ctx:
        place = [(nc.sbuf_base + 63) // 64 * 64]

        def at(name, shape, dt, where=None):
            n = int(np.prod(shape[1:])) * 4
            off = place[0] if where is None else where
            t = nc.alloc_sbuf_tensor_at(name, shape, dt, offset=off)
            if where is None:
                place[0] += (n + 31) // 32 * 32
            return t

        x = at("x", [P, KD, SEQ], F32)
        y_at = place[0]
        h_hi = at("h_hi", [P, KD, SEQ], F32R)
        y = at("y", [P, KD, SEQ], F32, y_at)
        h_lo = at("h_lo", [P, KD, SEQ], F32R)
        w_in_f32 = at("w_stage", [P, RING, KFH, P], F32)
        w_hi = at("w_hi", [P, RING, KFH, P], F32R)
        w_lo = at("w_lo", [P, RING, KFH, P], F32R)
        mem_hi = at("mem_hi", [P, KD, MEM], F32R)
        mem_lo = at("mem_lo", [P, KD, MEM], F32R)
        const = at("const", [P, NCONST], F32)
        ones = at("ones", [P, P], F32)
        mean256 = at("mean256", [P, P], F32)
        cos_t = at("cos_t", [P, SEQ], F32)
        sin_t = at("sin_t", [P, SEQ], F32)
        par_all = at("par_all", [P, DEPTH + 1, NPAR], F32)
        par = at("par", [P, NPAR], F32)
        neg_lam = at("neg_lam", [P, DEPTH], F32)
        neg_lam_l = at("neg_lam_l", [P, 1], F32)
        r_mem = at("r_mem", [P, MEM], F32)
        r_pre = at("r_pre", [P, SEQ], F32)
        r_post = at("r_post", [P, SEQ], F32)
        e0_at = place[0]
        epi = at("epi", [P, 2, SEQ], F32)
        acc_at = place[0]
        acc = at("acc", [P, SEQ], F32)
        poolw = at("poolw", [P, 2, P], F32, acc_at)
        diag = at("diag", [P, QB, P], F32)
        warm = at("warm", [P, 1], F32)
        stat = at("stat", [P, 4, 4], F32)
        att_s = at("att_s", [P, 2, 3, 4], F32)
        ident = const[:, C_ID:C_ID + P]

        r_at = place[0]
        hid_hi = at("hid_hi", [P, KF, SEQ], F32R)
        hid_lo = at("hid_lo", [P, KF, SEQ], F32R)
        assert place[0] <= nc.sbuf_usable_end, place[0]
        h_lo_at = y_at + KD * SEQ * 4
        mem_f32 = at("mem_f32", [P, KD, MEM], F32, h_lo_at)
        ang = at("ang", [P, 4, SEQ], F32, h_lo_at + KD * MEM * 4)
        mem_sq = at("mem_sq", [P, KD, MEM], F32, y_at + KD // 2 * SEQ * 4)
        pos_i = at("pos_i", [P, SEQ], I32, y_at + (KD // 2 - 1) * SEQ * 4)
        rp = [r_at]

        def r_alloc(name, shape):
            t = at(name, shape, F32, rp[0])
            rp[0] += (int(np.prod(shape[1:])) * 4 + 31) // 32 * 32
            return t

        kx = r_alloc("kx", [P, KD, MEM])
        vx_at = rp[0]
        xs = r_alloc("xs", [P, 2, SEQ])
        cg = r_alloc("cg", [P, 2, SEQ])
        vx = at("vx", [P, MEM // P, D], F32, vx_at)
        vxt_at = rp[0]
        ga = r_alloc("ga", [P, 2, SEQ])
        gg = r_alloc("gg", [P, 2, SEQ])
        vxt = at("vxt", [P, KD, MEM], F32, vxt_at)
        cross_at = rp[0]
        bg = r_alloc("bg", [P, 2, SEQ])
        PAD = POOL_WINDOWS[-1]
        za = r_alloc("za", [P, 2, PAD + SEQ])
        zb = r_alloc("zb", [P, 2, PAD + SEQ])
        zc = r_alloc("zc", [P, 2, PAD + SEQ])
        qk = r_alloc("qk", [P, 4, SEQ])
        vt = r_alloc("vt", [P, 2, SEQ])
        v = r_alloc("v", [P, QB, 2 * P])
        cpad = r_alloc("cpad", [P, 2, SCW - 1 + SEQ])
        upad = r_alloc("upad", [P, 2, CFW - 1 + SEQ])
        u = r_alloc("u", [P, 2, SEQ])
        p_at = rp[0]
        prob = r_alloc("prob", [P, 2, 2, SEQ])
        rope = at("rope", [P, 4, SEQ], F32, p_at)
        sqx = at("sqx", [P, KD, SEQ], F32, p_at)
        amix = r_alloc("amix", [P, 2, SEQ])
        amix_t = r_alloc("amix_t", [P, 2, SEQ])
        oc = r_alloc("oc", [P, 2 * P])
        junk = r_alloc("junk", [P, DIFF_H, DIFF_DV])
        assert rp[0] <= place[0], (rp[0], place[0])
        rp[0] = cross_at
        qx = r_alloc("qx", [P, KD, SEQ])
        y_r = at("y_r", [P, KD, SEQ], F32, cross_at)
        px = r_alloc("px", [P, 2, X_H, MEM])
        pxt = r_alloc("pxt", [P, 2, X_H, SEQ])
        assert rp[0] <= place[0]
        lam_in = at("lam_in", [P, DEPTH, 4, DIFF_DK], F32, r_at)
        lam_s = at("lam_s", [P, 2 * DEPTH], F32, r_at + SEQ * 4)
        lam_p = at("lam_p", [P, DEPTH, 2, DIFF_DK], F32, r_at + SEQ * 4 + 64)

        ps = ctx.enter_context(nc.psum_tensor("ps", [P, 8, 512], F32))
        B_STAT, B_BC = 6, 7

        def sem(name):
            return ctx.enter_context(nc.semaphore(name))

        w_loaded = [sem("w_loaded0"), sem("w_loaded1")]
        w_hi_done, w_lo_done, w_used = sem("w_hi_done"), sem("w_lo_done"), sem("w_used")
        dve_tiles, act_tiles = sem("dve_tiles"), sem("act_tiles")
        h_hi_done, h_lo_done = sem("h_hi_done"), sem("h_lo_done")
        sq_ready, sq_ready_p, r_ready = sem("sq_ready"), sem("sq_ready_p"), sem("r_ready")
        ysq_ready, ysq_used = sem("ysq_ready"), sem("ysq_used")
        stat_sum, stat_diag, stat_bc = sem("stat_sum"), sem("stat_diag"), sem("stat_bc")
        x_ready, x_ready_p = sem("x_ready"), sem("x_ready_p")
        silu_done, prod_done = sem("silu_done"), sem("prod_done")
        hid_hi_done, hid_lo_done = sem("hid_hi_done"), sem("hid_lo_done")
        consts_in, x_in, poolw_in = sem("consts_in"), [sem("x_in0"), sem("x_in1")], sem("poolw_in")
        mem_in, pos_in, mem_n, mem_hi_done, mem_lo_done = sem("mem_in"), sem("pos_in"), sem("mem_n"), sem("mem_hi_done"), sem("mem_lo_done")
        par_ready, setup_p, trig_arg, trig_done = (sem(n) for n in ("par_ready", "setup_p", "trig_arg", "trig_done"))
        lam_arg, lam_exp = sem("lam_arg"), sem("lam_exp")
        tanh_done, c_done, pads_done = sem("tanh_done"), sem("c_done"), sem("pads_done")
        pool_sums, mixed, pool_y = (sem(n) for n in ("pool_sums", "mixed", "pool_y"))
        yb_ready, u_ready, mu_done, xc_ready = sem("yb_ready"), sem("u_ready"), sem("mu_done"), sem("xc_ready")
        ln_ready, yd_ready = sem("ln_ready"), sem("yd_ready")
        rope_shuf, rope_mul, qk_ready = sem("rope_shuf"), sem("rope_mul"), sem("qk_ready")
        v_tr, v_tok, vx_tr, vx_tok = sem("v_tr"), sem("v_tok"), sem("vx_tr"), sem("vx_tok")
        a_s, a_max, a_exp, a_mix, a_tr, a_trc, a_pv = (sem(n) for n in ("a_s", "a_max", "a_exp", "a_mix", "a_tr", "a_trc", "a_pv"))
        o_sq, o_out, o_tr, yc_hi, yc_lo = (sem(n) for n in ("o_sq", "o_out", "o_tr", "yc_hi", "yc_lo"))
        x_s, x_max, x_exp, x_nrm, x_tr, x_trc, x_pv = (sem(n) for n in ("x_s", "x_max", "x_exp", "x_nrm", "x_tr", "x_trc", "x_pv"))
        stored = sem("stored")

        def g(name, i=0):
            return par[:, PAR[name] + i:PAR[name] + i + 1]

        block = ctx.enter_context(nc.Block())

        @block.sync
        def _(sp):
            sp.dma_start(par_all[:, 0:DEPTH, :], par_d).then_inc(consts_in, 16)
            sp.dma_start(const[:], const_d).then_inc(consts_in, 16)
            sp.dma_start(lam_in[:], lam_d.to_broadcast([P, DEPTH * 4 * DIFF_DK])
                         .rearrange("p (l a k) -> p l a k", l=DEPTH, a=4)).then_inc(consts_in, 16)
            with sp.Fori(0, DEPTH) as l:
                def load(p, s, kc, src):
                    sp.wait_ge(w_lo_done, 2 * p + s + 1)
                    sp.dma_start(w_in_f32[:, s, 0:kc, :], src.rearrange("p (k m) -> p k m", k=kc))\
                        .then_inc(w_loaded[s], 16)

                def loads(lo, n, kc, dram, first):
                    with sp.Fori(0, n // 2) as j:
                        for s in range(2):
                            load(l * (NB // 2) + lo // 2 + j, s, kc,
                                 dram[bass.ds(l * (NB - 4 * KD if kc == KD else 4 * KD) + first + 2 * j + s, 1), :, :]
                                 .rearrange("a p n -> (a p) n"))

                loads(BASE["f1gu"], 2 * KF, KD, w8_d, 0)
                for s in range(2):
                    load(l * (NB // 2) + BASE["f1dn"] // 2, s, KFH,
                         wd_d[bass.ds(l * 4 * KD + s, 1), :, :].rearrange("a p n -> (a p) n"))
                sp.wait_ge(w_used, l * NB + 2 * KF + RING)
                sp.dma_start(mem_f32[:], mem_d).then_inc(mem_in, 16)
                sp.dma_start(pos_i[:], pos_d.to_broadcast([P, SEQ])).then_inc(pos_in, 16)
                loads(BASE["f1dn"] + 2, 2 * KD - 2, KFH, wd_d, 2)
                loads(BASE["kx"], KD, KD, w8_d, 2 * KF)
                sp.wait_ge(stat_sum, l * NSTAT + S_POST1 + 1)
                sp.dma_start(poolw[:], poolw_d[bass.ds(l, 1), :, :, :].rearrange("a p t n -> (a p) t n"))\
                    .then_inc(poolw_in, 16)
                loads(BASE["win"], BASE["f2dn"] - BASE["win"], KD, w8_d, 2 * KF + KD)
                loads(BASE["f2dn"], 2 * KD, KFH, wd_d, 2 * KD)
            for i in (0, 1, 3, 2):
                if i == KD // 2 - 1:
                    sp.wait_ge(x_ready_p, DEPTH * NXP + 1)
                else:
                    sp.wait_ge(x_ready, (DEPTH - 1) * NXD + XD[S_PRE1] + X0 + i + 1)
                sp.dma_start(out_d[:, 2 * i:2 * i + 2, :], x[:, 2 * i:2 * i + 2, :]).then_inc(stored, 16)
            sp.wait_ge(stored, 16 * (KD // 2))

        @block.tensor
        def _(pe):
            pe.sem_inc(w_used, RING)
            pe.wait_ge(setup_p, 1)
            for _ in range(WARM_UP):
                pe.matmul(ps[:, 5, :], ones[:, :], ones[:].rearrange("p (o n) -> p o n", o=1)
                          .to_broadcast([P, SEQ // P, P]), start=True, stop=True)

            with pe.Fori(0, DEPTH) as l:
                def product(bank, width, p, kcs, rhs, first, last, chunk=None):
                    s = p[1]
                    n_k = kcs[1] - kcs[0]
                    pe.wait_ge(w_hi_done, 2 * p[0] + s + 1)
                    for k in range(n_k):
                        if chunk is not None:
                            pe.wait_ge(h_lo_done, chunk + k + 1)
                        for n, operand in enumerate(rhs(kcs[0] + k)):
                            pe.matmul(ps[:, bank, 0:width], w_hi[:, s, k, :], operand,
                                      start=(first and k == 0 and n == 0), stop=False)
                    pe.wait_ge(w_lo_done, 2 * p[0] + s + 1 + RING)
                    for k in range(n_k):
                        mm = pe.matmul(ps[:, bank, 0:width], w_lo[:, s, k, :], rhs(kcs[0] + k)[0],
                                       start=False, stop=(last and k == n_k - 1))
                    mm.then_inc(w_used, 1)

                def keep_warm(n):
                    for _ in range(n):
                        pe.matmul(ps[:, 5, :], ones[:, :], ones[:].rearrange("p (o n) -> p o n", o=1)
                                  .to_broadcast([P, SEQ // P, P]), start=True, stop=True)

                def project(name, n_tiles, rhs, inputs, width=SEQ, inputs_kf=None, chunk=None, after=(None, None)):
                    by_act = name in ("kx", "vx")

                    def tile(j, s, chunk=None):
                        if by_act:
                            pe.wait_ge(act_tiles, l * NAT + (KD if name == "vx" else 0) + 2 * j + s + 1)
                        else:
                            pe.wait_ge(dve_tiles, l * NDT + DT[name] + 2 * j + s + 1)
                        if name in POST:
                            pe.wait_ge(ysq_ready, (l * 4 + POST[name][1]) * KD + 2 * j + s + 1)
                        if inputs_kf is not None:
                            for half in range(2):
                                pe.wait_ge(hid_lo_done, inputs_kf + half * KFH + KFH)
                                product(s, width, (l * (NB // 2) + BASE[name] // 2 + 2 * j + s, half),
                                        (half * KFH, half * KFH + KFH), rhs, half == 0, half == 1)
                        else:
                            product(s, width, (l * (NB // 2) + BASE[name] // 2 + j, s), (0, KD), rhs, True, True, chunk)

                    peel = after != (None, None)
                    if peel:
                        for sem_, value in inputs:
                            pe.wait_ge(sem_, value)
                        for s in range(2):
                            tile(0, s, chunk if s == 0 else None)
                            if after[s]:
                                after[s]()
                    with pe.Fori(1 if peel else 0, n_tiles // 2) as j:
                        if not peel:
                            for sem_, value in inputs:
                                pe.wait_ge(sem_, value)
                        for s in range(2):
                            tile(j, s)

                def h_rhs(k):
                    return h_hi[:, k, :], h_lo[:, k, :]

                def hid_rhs(k):
                    return hid_hi[:, k, :], hid_lo[:, k, :]

                def mem_rhs(k):
                    return mem_hi[:, k, :], mem_lo[:, k, :]

                def sums(no, n, width, tiles, bank=B_STAT):
                    for m in range(n):
                        for c in range(width // P):
                            mm = pe.matmul(ps[:, bank, c:c + 1], tiles(m)[:, c * P:(c + 1) * P], ones[:, 0:1],
                                           start=(m == 0 and c == 0), stop=(m == n - 1), skip_group_check=True)
                    mm.then_inc(stat_sum, 1)

                def spread(no, width=SEQ, bank=B_BC):
                    pe.wait_ge(stat_diag, l * NSTAT + no + 1)
                    pe.matmul(ps[:, bank, 0:width], ones[:, :], diag[:, 0:width // P, :], start=True, stop=True)\
                        .then_inc(stat_bc, 1)

                def x_sums(no, nth):
                    pe.wait_ge(sq_ready, l * 6 + nth)
                    if no in (S_PRE1, S_PRE4):
                        pe.wait_ge(sq_ready_p, l * 2 + (1 if no == S_PRE1 else 2))
                    sums(no, KD, SEQ, lambda m: sqx[:, m, :])

                def y_sums(name):
                    no, nth = POST[name]
                    pe.wait_ge(ysq_ready, (l * 4 + nth) * KD + KD + RING)
                    pe.wait_ge(ysq_used, (l * 4 + nth) * NY + NY + RING)
                    sums(no, 2, SEQ, lambda m: (acc[:, :], epi[:, 1, :])[m])

                def left_bank_0(name):
                    return ysq_ready, (l * 4 + POST[name][1]) * KD + KD - 1 + RING

                def mem_sums():
                    pe.wait_ge(sq_ready, l * 6 + 2)
                    sums(S_MEM, KD, MEM, lambda m: mem_sq[:, m, :])

                project("f1gu", 2 * KF, h_rhs, [], chunk=l * NH + H_PRE1,
                        after=(lambda: x_sums(S_PRE1, 1), lambda: spread(S_PRE1)))
                project("f1dn", KD, hid_rhs, [], inputs_kf=l * 2 * KF,
                        after=(mem_sums, lambda: spread(S_MEM, MEM)))
                project("kx", KD, mem_rhs, [(mem_lo_done, l * KD + KD), left_bank_0("f1dn")],
                        width=MEM, after=(lambda: y_sums("f1dn"), lambda: spread(S_POST1)))
                project("win", 18, h_rhs, [(act_tiles, l * NAT + KD + RING)], chunk=l * NH + H_PRE2,
                        after=(lambda: x_sums(S_PRE2, 3), lambda: spread(S_PRE2)))

                for t in range(2):
                    for c in range(QB):
                        mm = pe.transpose(ps[:, 4 + t, c * P:(c + 1) * P], vt[:, t, c * P:(c + 1) * P], ident)
                    mm.then_inc(v_tr, 1)
                pe.wait_ge(u_ready, l + 1)
                pe.wait_ge(dve_tiles, l * NDT + DT["win"] + 18 + RING)
                for t in range(2):
                    mm = pe.matmul(ps[:, 0, :], mean256[:, :], u[:, t, :], start=(t == 0), stop=(t == 1))
                mm.then_inc(mu_done, 1)

                def scores(n):
                    qb, h = n // DIFF_H, n % DIFF_H
                    keys = (qb + 1) * P
                    if n == 0:
                        pe.wait_ge(r_ready, l * NSTAT + S_PRE2 + 1)
                        pe.wait_ge(v_tok, l * 2 + 2)
                        pe.wait_ge(qk_ready, l * 4 + 4)
                    if n >= 2:
                        pe.wait_ge(a_exp, l * NUNIT + n - 1)
                    for c in range(2):
                        f = (2 * h + c) * DIFF_DK
                        t, r = f // P, f % P
                        bank = 2 + 2 * (n % 2) + c
                        pe.matmul(ps[:, bank, 0:keys], qk[r:r + DIFF_DK, t, qb * P:(qb + 1) * P],
                                  qk[r:r + DIFF_DK, 2 + t, 0:keys], start=True, stop=False)
                        mm = pe.matmul(ps[:, bank, keys - CHUNK:keys], const[r:r + 1, C_ROW:C_ROW + P],
                                       const[r:r + 1, C_ROW + P:C_ROW + P + CHUNK], start=False, stop=True)
                    mm.then_inc(a_s, 1)

                def mix_transpose(n):
                    pe.wait_ge(a_mix, l * NUNIT + n + 1)
                    if n >= 1:
                        pe.wait_ge(a_trc, l * NUNIT + n)
                    for k in range(n // DIFF_H + 1):
                        mm = pe.transpose(ps[:, 6, k * P:(k + 1) * P], amix[:, n % 2, k * P:(k + 1) * P], ident)
                    mm.then_inc(a_tr, 1)

                def values(n):
                    qb, h = n // DIFF_H, n % DIFF_H
                    pe.wait_ge(a_trc, l * NUNIT + n + 1)
                    if h == 0 and qb >= 2:
                        pe.wait_ge(o_out, l * QB + qb - 1)
                    if n == 4:
                        pe.wait_ge(r_ready, l * NSTAT + S_LN + 1)
                    for k in range(qb + 1):
                        mm = pe.matmul(ps[:, (7, 1)[qb % 2], h * DIFF_DV:(h + 1) * DIFF_DV],
                                       amix_t[:, n % 2, k * P:(k + 1) * P], v[:, k, h * DIFF_DV:(h + 1) * DIFF_DV],
                                       start=(k == 0), stop=(k == qb))
                    mm.then_inc(a_pv, 1)

                def out_transpose(qb):
                    pe.wait_ge(o_out, l * QB + qb + 1)
                    if qb >= 1:
                        pe.wait_ge(yc_lo, l * QB + qb)
                    for t in range(2):
                        mm = pe.transpose(ps[:, 0, t * P:(t + 1) * P], oc[:, t * P:(t + 1) * P], ident)
                    mm.then_inc(o_tr, 1)

                for t in range(NUNIT + 5):
                    if t < NUNIT:
                        scores(t)
                    if 2 <= t <= NUNIT + 1:
                        mix_transpose(t - 2)
                    if 3 <= t <= NUNIT + 2:
                        values(t - 3)
                    if t >= 8 and (t - 8) % 4 == 0:
                        if t == NUNIT + 4:
                            keep_warm(5)
                        out_transpose((t - 8) // 4)
                    if t == 4:
                        pe.wait_ge(sq_ready, l * 6 + 4)
                        sums(S_LN, 2, SEQ, lambda m: epi[:, m, :], bank=0)
                    if t == 6:
                        spread(S_LN, bank=1)
                    if t == NUNIT + 1:
                        pe.wait_ge(mixed, l * 2 + 2)
                        pe.wait_ge(poolw_in, l * 16 + 16)
                        pe.wait_ge(a_exp, l * NUNIT + NUNIT - 1)
                        for i in range(2):
                            pe.matmul(ps[:, 2 + i, :], poolw[:, i, :], zb[:, i, PAD:PAD + SEQ], start=True, stop=True)\
                                .then_inc(pool_y, 1)

                project("wo", KD, h_rhs, [(yc_lo, l * QB + QB), (h_lo_done, l * NH + H_MIX + 6)])
                project("vx", KD, mem_rhs, [left_bank_0("wo")], width=MEM,
                        after=(lambda: y_sums("wo"), lambda: spread(S_POST2)))
                project("qx", KD, h_rhs, [(act_tiles, l * NAT + 2 * KD + RING)], chunk=l * NH + H_PRE3,
                        after=(lambda: x_sums(S_PRE3, 5), lambda: spread(S_PRE3)))
                for n in range(4):
                    if n >= 2:
                        pe.wait_ge(vx_tok, l * 4 + n - 1)
                    for f in range(4):
                        mm = pe.transpose(ps[:, 2 + n % 2, f * P:(f + 1) * P],
                                          vxt[:, 4 * (n % 2) + f, (n // 2) * P:(n // 2 + 1) * P], ident)
                    mm.then_inc(vx_tr, 1)

                pe.wait_ge(dve_tiles, l * NDT + DT["qx"] + KD + RING)
                pe.wait_ge(vx_tok, l * 4 + 4)
                pe.wait_ge(r_ready, l * NSTAT + S_PRE3 + 1)
                for t in range(QB + 2):
                    if t < QB:
                        if t >= 2:
                            pe.wait_ge(x_exp, l * QB + t - 1)
                        for h in range(X_H):
                            for c in range(2):
                                mm = pe.matmul(ps[:, 2 + 2 * (t % 2) + h // 2, (h % 2) * MEM:(h % 2 + 1) * MEM],
                                               qx[:, 2 * h + c, t * P:(t + 1) * P], kx[:, 2 * h + c, :],
                                               start=(c == 0), stop=(c == 1))
                        mm.then_inc(x_s, 1)
                    if t >= 2:
                        pe.wait_ge(x_nrm, l * QB + t - 1)
                        if t >= 3:
                            pe.wait_ge(x_trc, l * QB + t - 2)
                        for mc in range(2):
                            for h in range(X_H):
                                mm = pe.transpose(ps[:, 6 + mc, h * P:(h + 1) * P],
                                                  px[:, t % 2, h, mc * P:(mc + 1) * P], ident)
                        mm.then_inc(x_tr, 1)
                pe.wait_ge(x_trc, l * QB + QB)
                for n in range(2 * X_H):
                    if n >= 2:
                        pe.wait_ge(h_lo_done, l * NH + H_OX + n - 1)
                    for mc in range(2):
                        mm = pe.matmul(ps[:, n % 2, :], vx[:, mc, n * P:(n + 1) * P], pxt[:, mc, n // 2, :],
                                       start=(mc == 0), stop=(mc == 1))
                    mm.then_inc(x_pv, 1)
                project("xo", KD, h_rhs, [(h_lo_done, l * NH + H_OX + KD)])
                keep_warm(2)
                y_sums("xo")
                keep_warm(3)
                spread(S_POST3)
                keep_warm(5)
                project("f2gu", 2 * KF, h_rhs, [], chunk=l * NH + H_PRE4,
                        after=(lambda: x_sums(S_PRE4, 6), lambda: spread(S_PRE4)))
                project("f2dn", KD, hid_rhs, [], inputs_kf=l * 2 * KF + KF)
                keep_warm(2)
                y_sums("f2dn")
                keep_warm(3)
                spread(S_POST4)
                keep_warm(5)

        @block.scalar
        def _(act):
            for i in range(2):
                c = slice(i * KD // 2, (i + 1) * KD // 2)
                act.dma_start(x[:, c, :], x_d[:, c, :]).then_inc(x_in[i], 16)
            act.sem_inc(ysq_ready, RING)
            act.wait_ge(lam_arg, 1)
            act.activation(lam_s[:], lam_s[:], ACT.Exp).then_inc(lam_exp, 1)

            with act.Fori(0, DEPTH) as l:
                LB = l * (NB // 2)

                def prep(p, s, kc):
                    act.wait_ge(w_loaded[s], (LB + p + 1) * 16)
                    act.wait_ge(w_used, 2 * (LB + p) + s + 1)
                    act.activation(w_hi[:, s, 0:kc, :], w_in_f32[:, s, 0:kc, :], ACT.Copy).then_inc(w_hi_done, 1)

                def x_hi(no, gain, m):
                    if no in (S_PRE1, S_PRE4) and m >= KD - 2:
                        act.wait_ge(x_ready_p, l * NXP + (1 if no == S_PRE1 else 2))
                    else:
                        act.wait_ge(x_ready, l * NXD + (XD[no] if no != S_PRE1 else XD[no] - NXD) + X0 + m // 2 + 1)
                    act.activation(h_hi[:, m, :], x[:, m, :], ACT.Copy, scale=g(gain, m)).then_inc(h_hi_done, 1)

                def x_squares(n=KD):
                    act.activation(sqx[:, 0:n, :], x[:, 0:n, :], ACT.Square).then_inc(sq_ready, 1)

                def take_r(no, dst, width=SEQ, bank=B_BC):
                    act.wait_ge(stat_bc, l * NSTAT + no + 1)
                    act.activation(dst[:], ps[:, bank, 0:width], ACT.Copy).then_inc(r_ready, 1)

                def y_square(name, m, s):
                    act.wait_ge(dve_tiles, l * NDT + DT[name] + m + 1 + RING)
                    act.wait_ge(ysq_used, (l * 4 + POST[name][1]) * NY + m - 1 + RING)
                    act.activation(epi[:, s, :], ps[:, s, :], ACT.Square).then_inc(ysq_ready, 1)

                def ffn(n, no):
                    base = BASE[f"f{n}gu"] // 2
                    fi = l * 2 * KF + (n - 1) * KF

                    def pair(j, kc, first=False):
                        act.activation(warm[:, 0:1], ident[:, 0:1], ACT.Silu)
                        prep(base + j + 1, 0, kc)
                        if first:
                            prep(base + j + 1, 1, kc)
                            take_r(no, r_pre)
                        act.wait_ge(dve_tiles, l * NDT + DT[f"f{n}gu"] + 2 * j + 1 + RING)
                        act.activation(epi[:, 0, :], epi[:, 0, :], ACT.Silu).then_inc(silu_done, 1)
                        if not first:
                            prep(base + j + 1, 1, kc)
                        act.wait_ge(prod_done, fi + j + 1)
                        act.activation(hid_hi[:, bass.ds(j, 1), :], epi[:, 1, :], ACT.Copy).then_inc(hid_hi_done, 1)

                    pair(0, KD, True)
                    with act.Fori(1, KF - 1) as j:
                        pair(j, KD)
                    pair(KF - 1, KFH)

                def ffn_out(n, fill):
                    base = BASE[f"f{n}dn"] // 2

                    def out_pair(j, kc, fill=()):
                        for s in range(2):
                            for half in range(2):
                                if kc or s == 0:
                                    prep(base + 2 * j + 1 + s, half, KFH if s == 0 else kc)
                                for f in fill[2 * (2 * s + half):2 * (2 * s + half) + 2]:
                                    f()
                            y_square(f"f{n}dn", 2 * j + s, s)

                    if fill:
                        out_pair(0, KFH)
                        for f in fill[0:3]:
                            f()
                        out_pair(1, KFH, fill[3:])
                    with act.Fori(2 if fill else 0, KD // 2 - 1) as j:
                        out_pair(j, KFH)
                    out_pair(KD // 2 - 1, KD if n == 1 else None)

                def out_project(name):
                    with act.Fori(0, KD // 2) as j:
                        for s in range(2):
                            prep(BASE[name] // 2 + j + 1, s, KD)
                            y_square(name, 2 * j + s, s)

                def memory_project(name, dst, post, no, gain):
                    hi_after = {2: (0,), 3: (1,), 4: (2, 3), 5: (4,), 6: (5, 6), 7: (7,)}
                    for m in range(KD):
                        prep(BASE[name] // 2 + m // 2 + 1, m % 2, KD)
                        act.activation(dst[:, m, :], ps[:, m % 2, 0:MEM], ACT.Copy).then_inc(act_tiles, 1)
                        if m == 1:
                            take_r(post, r_post)
                        for c in hi_after.get(m, ()):
                            x_hi(no, gain, c)
                    x_squares()

                act.wait_ge(par_ready, l + 1)
                prep(0, 0, KD)
                prep(0, 1, KD)
                for m in range(KD):
                    x_hi(S_PRE1, "f1_pre_g", m)
                x_squares(KD - 2)
                ffn(1, S_PRE1)
                act.wait_ge(mem_in, l * 16 + 16)
                act.activation(mem_sq[:], mem_f32[:], ACT.Square).then_inc(sq_ready, 1)

                def sines(t):
                    act.wait_ge(trig_arg, l + 1)
                    act.activation(t[:], t[:], ACT.Sin).then_inc(trig_done, 1)

                def mem_hi_of(m):
                    act.wait_ge(mem_n, l + 1)
                    act.activation(mem_hi[:, m, :], mem_f32[:, m, :], ACT.Copy, scale=g("x_mem_g", m)).then_inc(mem_hi_done, 1)

                ffn_out(1, [lambda: take_r(S_MEM, r_mem, MEM), lambda: sines(sin_t), lambda: sines(cos_t)]
                        + [lambda m=m: mem_hi_of(m) for m in range(KD)])
                memory_project("kx", kx, S_POST1, S_PRE2, "mix_pre_g")

                for j in range(9):
                    prep(BASE["win"] // 2 + j + 1, 0, KD)
                    prep(BASE["win"] // 2 + j + 1, 1, KD)
                    if j == 0:
                        take_r(S_PRE2, r_pre)
                    if j == 2:
                        act.wait_ge(dve_tiles, l * NDT + DT["win"] + 4 + RING)
                        act.activation(gg[:], gg[:], ACT.Tanh, scale=0.5).then_inc(tanh_done, 1)
                for t in range(2):
                    act.wait_ge(v_tr, l * 2 + t + 1)
                    act.activation(v[:, :, t * P:(t + 1) * P],
                                   ps[:, 4 + t, :].rearrange("p (c n) -> p c n", c=QB), ACT.Copy).then_inc(v_tok, 1)

                for t in range(NUNIT + 5):
                    if t < NUNIT:
                        act.wait_ge(a_max, l * NUNIT + t + 1)
                        if t >= 2:
                            act.wait_ge(a_mix, l * NUNIT + t - 1)
                        keys = (t // DIFF_H + 1) * P
                        for c in range(2):
                            e = act.activation(prob[:, t % 2, c, 0:keys], ps[:, 2 + 2 * (t % 2) + c, 0:keys], ACT.Exp,
                                               bias=att_s[:, t % 2, 0, c:c + 1], scale=DIFF_SCALE,
                                               accum_out=att_s[:, t % 2, 1, c:c + 1])
                        e.then_inc(a_exp, 1)
                    if 2 <= t <= NUNIT + 1:
                        n = t - 2
                        keys = (n // DIFF_H + 1) * P
                        act.wait_ge(a_tr, l * NUNIT + n + 1)
                        if n >= 2:
                            act.wait_ge(a_pv, l * NUNIT + n - 1)
                        act.activation(amix_t[:, n % 2, 0:keys], ps[:, 6, 0:keys], ACT.Copy).then_inc(a_trc, 1)
                    if t >= 7 and (t - 7) % 4 == 0:
                        qb = (t - 7) // 4
                        act.wait_ge(a_pv, l * NUNIT + 4 * qb + 4)
                        if qb >= 1:
                            act.wait_ge(o_out, l * QB + qb)
                        for h in range(DIFF_H):
                            e = act.activation(junk[:, h, :], ps[:, (7, 1)[qb % 2], h * DIFF_DV:(h + 1) * DIFF_DV],
                                               ACT.Square, accum_out=stat[:, 3, h:h + 1])
                        e.then_inc(o_sq, 1)
                    if t >= 8 and (t - 8) % 4 == 0:
                        qb = (t - 8) // 4
                        act.wait_ge(o_tr, l * QB + qb + 1)
                        for f in range(2):
                            e = act.activation(h_hi[:, 4 + f, qb * P:(qb + 1) * P], ps[:, 0, f * P:(f + 1) * P],
                                               ACT.Copy, scale=g("subln"))
                        e.then_inc(yc_hi, 1)
                    if t == 3:
                        act.wait_ge(xc_ready, l * 2 + 2)
                        for i in range(2):
                            e = act.activation(epi[:, i, :], u[:, i, :], ACT.Square)
                        e.then_inc(sq_ready, 1)
                    if t == 6:
                        take_r(S_LN, r_post, bank=1)
                        act.wait_ge(yb_ready, l + 1)
                        for i in range(2):
                            act.activation(h_hi[:, 2 + i, :], bg[:, i, :], ACT.Copy).then_inc(h_hi_done, 1)
                    if t == NUNIT + 1:
                        act.wait_ge(ln_ready, l + 1)
                        for i in range(2):
                            act.activation(u[:, i, :], u[:, i, :], ACT.Silu, bias=g("ln_b", i)).then_inc(yd_ready, 1)
                    if t == NUNIT + 2:
                        for i in range(2):
                            act.wait_ge(pool_y, l * 2 + i + 1)
                            act.activation(h_hi[:, i, :], ps[:, 2 + i, :], ACT.Copy, scale=g("pool_scale", i)).then_inc(h_hi_done, 1)
                        for i in range(2):
                            act.wait_ge(yd_ready, l * 2 + i + 1)
                            act.activation(h_hi[:, 6 + i, :], u[:, i, :], ACT.Copy).then_inc(h_hi_done, 1)

                out_project("wo")
                memory_project("vx", vxt, S_POST2, S_PRE3, "x_pre_g")
                for j in range(KD // 2):
                    prep(BASE["qx"] // 2 + j + 1, 0, KD)
                    prep(BASE["qx"] // 2 + j + 1, 1, KD)
                    if j == 0:
                        take_r(S_PRE3, r_pre)
                for n in range(4):
                    act.wait_ge(vx_tr, l * 4 + n + 1)
                    act.activation(vx[:, n // 2, (n % 2) * SEQ:(n % 2 + 1) * SEQ], ps[:, 2 + n % 2, :], ACT.Copy)\
                        .then_inc(vx_tok, 1)
                for t in range(QB + 2):
                    if t < QB:
                        act.wait_ge(x_max, l * QB + t + 1)
                        if t >= 2:
                            act.wait_ge(x_tr, l * QB + t - 1)
                        for h in range(X_H):
                            e = act.activation(px[:, t % 2, h, :],
                                               ps[:, 2 + 2 * (t % 2) + h // 2, (h % 2) * MEM:(h % 2 + 1) * MEM], ACT.Exp,
                                               bias=att_s[:, t % 2, 0, h:h + 1], scale=X_SCALE,
                                               accum_out=att_s[:, t % 2, 1, h:h + 1])
                        e.then_inc(x_exp, 1)
                    if t >= 2:
                        act.wait_ge(x_tr, l * QB + t - 1)
                        for mc in range(2):
                            e = act.activation(pxt[:, mc, :, (t - 2) * P:(t - 1) * P],
                                               ps[:, 6 + mc, :].rearrange("p (h n) -> p h n", h=X_H), ACT.Copy)
                        e.then_inc(x_trc, 1)
                for n in range(2 * X_H):
                    act.wait_ge(x_pv, l * 2 * X_H + n + 1)
                    act.activation(h_hi[:, n, :], ps[:, n % 2, :], ACT.Copy).then_inc(h_hi_done, 1)
                out_project("xo")
                take_r(S_POST3, r_post)
                for m in range(KD):
                    x_hi(S_PRE4, "f2_pre_g", m)
                x_squares(KD - 2)
                ffn(2, S_PRE4)
                ffn_out(2, [])
                take_r(S_POST4, r_post)

        @block.gpsimd
        def _(pool):
            pool.memset(ones[:], 1.0)
            pool.memset(mean256[:], 1.0 / (2 * P))
            pool.drain()
            pool.sem_inc(setup_p, 1)
            pool.sem_inc(w_lo_done, RING)
            pool.sem_inc(ysq_used, RING)

            with pool.Fori(0, DEPTH) as l:
                LB = l * (NB // 2)

                def prep(p, s, kc):
                    pool.wait_ge(w_hi_done, 2 * (LB + p) + s + 1)
                    pool.tensor_tensor(w_lo[:, s, 0:kc, :], w_in_f32[:, s, 0:kc, :],
                                       w_hi[:, s, 0:kc, :].bitcast(F32), ALU.subtract).then_inc(w_lo_done, 1)

                def add_square(name, m, s):
                    first = isinstance(m, int) and m == 1
                    pool.wait_ge(ysq_ready, (l * 4 + POST[name][1]) * KD + m + 1 + RING)
                    pool.tensor_tensor(acc[:], epi[:, 0, :] if first else acc[:], epi[:, s, :], ALU.add)
                    pool.drain()
                    pool.sem_inc(ysq_used, 2 if first else 1)

                def ffn(n):
                    base = BASE[f"f{n}gu"] // 2
                    with pool.Fori(0, KF - 1) as j:
                        prep(base + j + 1, 0, KD)
                        prep(base + j + 1, 1, KD)
                    prep(base + KF, 0, KFH)
                    prep(base + KF, 1, KFH)
                    name = f"f{n}dn"
                    base = BASE[name] // 2

                    def out_pair(j, kc, first=False, last=False):
                        for s in range(2):
                            if kc or s == 0:
                                prep(base + 2 * j + 1 + s, 0, KFH if s == 0 else kc)
                                prep(base + 2 * j + 1 + s, 1, KFH if s == 0 else kc)
                            if not (first and s == 0 or last and s == 1):
                                add_square(name, 2 * j + s, s)

                    out_pair(0, KFH, first=True)
                    with pool.Fori(1, KD // 2 - 1) as j:
                        out_pair(j, KFH)
                    out_pair(KD // 2 - 1, KD if n == 1 else None, last=True)

                def out_project(name):
                    def pair(j, first=False, last=False):
                        for s in range(2):
                            prep(BASE[name] // 2 + j + 1, s, KD)
                            if not (first and s == 0 or last and s == 1):
                                add_square(name, 2 * j + s, s)

                    pair(0, first=True)
                    with pool.Fori(1, KD // 2 - 1) as j:
                        pair(j)
                    pair(KD // 2 - 1, last=True)

                def update_x(no, y):
                    pool.wait_ge(r_ready, l * NSTAT + no + 1)
                    last = y[:, KD - 2:KD, :]
                    pool.tensor_tensor(last, last, r_post[:].rearrange("p (o n) -> p o n", o=1)
                                       .to_broadcast([P, 2, SEQ]), ALU.mult)
                    pool.drain()
                    pool.tensor_tensor(x[:, KD - 2:KD, :], x[:, KD - 2:KD, :], last, ALU.add).then_inc(x_ready_p, 1)
                    pool.drain()

                def x_squares():
                    last = x[:, KD - 2:KD, :]
                    pool.tensor_tensor(sqx[:, KD - 2:KD, :], last, last, ALU.mult).then_inc(sq_ready_p, 1)

                prep(0, 0, KD)
                prep(0, 1, KD)
                pool.wait_ge(x_ready_p, l * NXP + 1)
                x_squares()
                ffn(1)
                for m in range(KD):
                    prep(BASE["kx"] // 2 + m // 2 + 1, m % 2, KD)
                pool.memset(za[:, :, 0:PAD], 0.0)
                pool.memset(zb[:, :, 0:PAD], 0.0)
                pool.memset(zc[:, :, 0:PAD], 0.0)
                pool.memset(cpad[:, :, 0:SCW - 1], 0.0)
                pool.memset(upad[:, :, 0:CFW - 1], 0.0)
                pool.drain()
                pool.sem_inc(pads_done, 1)
                for j in range(9):
                    prep(BASE["win"] // 2 + j + 1, 0, KD)
                    prep(BASE["win"] // 2 + j + 1, 1, KD)
                    if j in (5, 6):
                        for i in (0, 1) if j == 5 else (2, 3):
                            pool.wait_ge(rope_shuf, l * 4 + i + 1)
                            pool.tensor_tensor(rope[:, i, :], rope[:, i, :], sin_t[:], ALU.mult)
                            pool.tensor_tensor(qk[:, i, :], qk[:, i, :], cos_t[:], ALU.mult)
                            pool.drain()
                            pool.sem_inc(rope_mul, 1)
                    if j == 7:
                        pool.wait_ge(dve_tiles, l * NDT + DT["win"] + 14 + RING)
                        pool.tensor_tensor(cpad[:, :, SCW - 1:], cg[:], xs[:], ALU.mult).then_inc(c_done, 1)
                pool.wait_ge(dve_tiles, l * NDT + DT["win"] + 18 + RING)

                def shifted(t, part, tile, by):
                    return t[part, tile, PAD - by:PAD - by + SEQ]
                every, upper = slice(0, P), slice(P // 2, P)
                for src, dst, part, t, by in (
                        (za, zb, every, 0, 1), (za, zb, every, 1, 1),
                        (zb, zc, every, 1, 2), (zb, zc, upper, 0, 2),
                        (zc, zb, every, 1, 4),
                        (zb, zc, upper, 1, 8)):
                    if (t, by) != (0, 1):
                        pool.drain()
                    pool.tensor_tensor(shifted(dst, part, t, 0), shifted(src, part, t, 0),
                                       shifted(src, part, t, by), ALU.add)
                for t in range(2):
                    pool.drain()
                    pool.tensor_copy(shifted(zb, upper, t, 0), shifted(zc, upper, t, 0))
                pool.drain()
                pool.sem_inc(pool_sums, 1)
                out_project("wo")
                for m in range(KD):
                    prep(BASE["vx"] // 2 + m // 2 + 1, m % 2, KD)
                with pool.Fori(0, KD // 2) as j:
                    prep(BASE["qx"] // 2 + j + 1, 0, KD)
                    prep(BASE["qx"] // 2 + j + 1, 1, KD)
                out_project("xo")
                update_x(S_POST3, y_r)
                x_squares()
                ffn(2)
                update_x(S_POST4, y)

        @block.vector
        def _(dve):
            stt = dve.scalar_tensor_tensor

            def rsqrt(src, n, count):
                hv, r, w = stat[:, 0, 0:n], stat[:, 1, 0:n], stat[:, 2, 0:n]
                dve.tensor_scalar(w, src, 1.0 / count, EPS, ALU.mult, ALU.add)
                dve.drain()
                dve.tensor_scalar(hv, w, -0.5, None, ALU.mult)
                dve.tensor_scalar(r.bitcast(I32), w.bitcast(I32), -0.5, float(0x5F3759DF), ALU.mult, ALU.add)
                dve.drain()
                for _ in range(3):
                    dve.tensor_tensor(w, r, r, ALU.mult)
                    dve.drain()
                    dve.tensor_tensor(w, w, hv, ALU.mult)
                    dve.drain()
                    stt(r, w, 1.5, r, ALU.add, ALU.mult)
                    dve.drain()

            dve.sem_inc(dve_tiles, RING)
            dve.sem_inc(act_tiles, RING)
            dve.wait_ge(consts_in, 48)
            for a in range(2):
                dve.tensor_tensor(lam_p[:, :, a, :], lam_in[:, :, 2 * a, :], lam_in[:, :, 2 * a + 1, :], ALU.mult)
            dve.drain()
            dve.tensor_reduce(lam_s[:], lam_p[:], AX.X, ALU.add)
            dve.drain()
            dve.sem_inc(lam_arg, 1)
            for l in range(DEPTH):
                for name in ("f1_post_g", "f2_post_g"):
                    c = par_all[:, l, PAR[name]:PAR[name] + KD]
                    dve.tensor_scalar(c, c, 0.5, None, ALU.mult)
                c = par_all[:, l, PAR["conf_w"]:PAR["conf_w"] + 2 * CFW]
                dve.tensor_scalar(c, c, 0.5, None, ALU.mult)
                c = par_all[:, l, PAR["subln"]:PAR["subln"] + 1]
                dve.tensor_scalar(c, c, 1.0 - (0.8 - 0.6 * math.exp(-0.3 * l)), None, ALU.mult)
            dve.wait_ge(lam_exp, 1)
            for l in range(DEPTH):
                stt(neg_lam[:, l:l + 1], lam_s[:, 2 * l + 1:2 * l + 2], -(0.8 - 0.6 * math.exp(-0.3 * l)),
                    lam_s[:, 2 * l:2 * l + 1], ALU.add, ALU.subtract)
            dve.drain()
            dve.tensor_copy(par_all[:, DEPTH, :], par_all[:, 0, :])
            dve.tensor_copy(par[:], par_all[:, 0, :])
            dve.drain()
            dve.sem_inc(par_ready, 1)
            dve.wait_ge(x_in[0], 16)
            dve.sem_inc(x_ready, KD // 4)
            dve.wait_ge(x_in[1], 16)
            dve.sem_inc(x_ready, X0 - KD // 4)
            dve.sem_inc(x_ready_p, 1)

            with dve.Fori(0, DEPTH) as l:
                def lo_of(m_dst, in0, gain=None):
                    hi = h_hi[:, m_dst, :].bitcast(F32)
                    if gain is None:
                        dve.tensor_tensor(h_lo[:, m_dst, :], in0, hi, ALU.subtract).then_inc(h_lo_done, 1)
                    else:
                        stt(h_lo[:, m_dst, :], in0, gain, hi, ALU.mult, ALU.subtract).then_inc(h_lo_done, 1)

                def factors(no, width, count, bank=B_STAT):
                    n = width // P
                    dve.wait_ge(stat_sum, l * NSTAT + no + 1)
                    rsqrt(ps[:, bank, 0:n], n, count)
                    dve.tensor_tensor(diag[:, 0:n, :], ident.rearrange("p (o n) -> p o n", o=1).to_broadcast([P, n, P]),
                                      stat[:, 1, 0:n].rearrange("p (n o) -> p n o", o=1).to_broadcast([P, n, P]),
                                      ALU.mult).then_inc(stat_diag, 1)

                def x_lo(first_h, gain, m):
                    dve.wait_ge(h_hi_done, l * NH + first_h + m + 1)
                    lo_of(m, x[:, m, :], g(gain, m))

                def pre_norm(no, first_h, gain):
                    for m in range(KD):
                        x_lo(first_h, gain, m)
                    factors(no, SEQ, D)

                def update_x(y, i):
                    c = slice(2 * i, 2 * i + 2)
                    dve.tensor_tensor(y[:, c, :], y[:, c, :], r_post[:].rearrange("p (o n) -> p o n", o=1)
                                      .to_broadcast([P, 2, SEQ]), ALU.mult)
                    dve.drain()
                    dve.tensor_tensor(x[:, c, :], x[:, c, :], y[:, c, :], ALU.add).then_inc(x_ready, 1)

                def post_norm(name, y, pairs=KD // 2):
                    no = POST[name][0]
                    factors(no, SEQ, D)
                    if name == "f2dn":
                        dve.tensor_copy(par[:], par_all[:, bass.ds(l + 1, 1), :])
                        dve.drain()
                        dve.sem_inc(par_ready, 1)
                    dve.wait_ge(r_ready, l * NSTAT + no + 1)
                    for i in range(pairs):
                        update_x(y, i)

                def take_y(name, j, s, gain, y, kf=False):
                    dve.wait_ge(w_used, l * NB + BASE[name] + (4 * j + 2 * s + 2 if kf else 2 * j + s + 1) + RING)
                    dve.tensor_scalar(y[:, bass.ds(2 * j + s, 1), :], ps[:, s, :],
                                      par[:, bass.ds(PAR[gain] + 2 * j + s, 1)], None, ALU.mult).then_inc(dve_tiles, 1)

                def ffn_in(n):
                    tile0 = l * NB + BASE[f"f{n}gu"]
                    fi = l * 2 * KF + (n - 1) * KF
                    with dve.Fori(0, KF) as j:
                        dve.wait_ge(r_ready, l * NSTAT + (S_PRE1, S_PRE4)[n - 1] + 1)
                        dve.wait_ge(w_used, tile0 + 2 * j + 1 + RING)
                        dve.tensor_tensor(epi[:, 0, :], ps[:, 0, :], r_pre[:], ALU.mult).then_inc(dve_tiles, 1)
                        dve.wait_ge(w_used, tile0 + 2 * j + 2 + RING)
                        dve.tensor_tensor(epi[:, 1, :], ps[:, 1, :], r_pre[:], ALU.mult).then_inc(dve_tiles, 1)
                        dve.drain()
                        dve.wait_ge(silu_done, fi + j + 1)
                        dve.tensor_tensor(epi[:, 1, :], epi[:, 1, :], epi[:, 0, :], ALU.mult).then_inc(prod_done, 1)
                        dve.drain()
                        dve.wait_ge(hid_hi_done, fi + j + 1)
                        dve.tensor_tensor(hid_lo[:, bass.ds(j, 1), :], epi[:, 1, :],
                                          hid_hi[:, bass.ds(j, 1), :].bitcast(F32), ALU.subtract).then_inc(hid_lo_done, 1)
                        dve.drain()

                def out_project(name, gain):
                    with dve.Fori(0, KD // 2) as j:
                        for s in range(2):
                            take_y(name, j, s, gain, y_r)
                    dve.drain()

                pre_norm(S_PRE1, H_PRE1, "f1_pre_g")
                dve.tensor_copy(neg_lam_l[:], neg_lam[:, bass.ds(l, 1)])
                ffn_in(1)

                ang_, k, kh, kl = ang[:, 0, :], ang[:, 1, :], ang[:, 2, :], ang[:, 3, :]
                two_pi = 2 * math.pi
                c1 = math.floor(two_pi * 2 ** 9) / 2 ** 9
                c2 = math.floor((two_pi - c1) * 2 ** 22) / 2 ** 22
                c3 = two_pi - c1 - c2
                dve.wait_ge(pos_in, l * 16 + 16)
                dve.tensor_copy(ang_, pos_i[:])
                dve.drain()
                dve.tensor_scalar(ang_, ang_, const[:, C_FREQ:C_FREQ + 1], None, ALU.mult)
                dve.drain()
                dve.tensor_scalar(k, ang_, 1 / two_pi, 1.5 * 2 ** 23, ALU.mult, ALU.add)
                dve.drain()
                dve.tensor_scalar(k, k, 1.5 * 2 ** 23, None, ALU.subtract)
                dve.drain()
                dve.tensor_scalar(kh, k, 1.5 * 2 ** 35, None, ALU.add)
                dve.drain()
                dve.tensor_scalar(kh, kh, 1.5 * 2 ** 35, None, ALU.subtract)
                dve.drain()
                dve.tensor_tensor(kl, k, kh, ALU.subtract)
                dve.drain()
                for part in (c1, c2):
                    for kk in (kh, kl):
                        stt(ang_, kk, -part, ang_, ALU.mult, ALU.add)
                        dve.drain()
                stt(ang_, k, -c3, ang_, ALU.mult, ALU.add)
                dve.drain()
                dve.tensor_scalar(sin_t[:], ang_, 3.1415925, -3.1415925, ALU.min, ALU.max)
                dve.tensor_scalar(kh, ang_, -1.0, None, ALU.mult)
                dve.drain()
                dve.tensor_tensor(kh, kh, ang_, ALU.max)
                dve.drain()
                dve.tensor_scalar(cos_t[:], kh, -1.0, math.pi / 2, ALU.mult, ALU.add)
                dve.drain()
                dve.sem_inc(trig_arg, 1)

                take_y("f1dn", 0, 0, "f1_post_g", y, True)
                factors(S_MEM, MEM, D)
                take_y("f1dn", 0, 1, "f1_post_g", y, True)
                dve.wait_ge(r_ready, l * NSTAT + S_MEM + 1)
                dve.tensor_tensor(mem_f32[:], mem_f32[:],
                                  r_mem[:].rearrange("p (o n) -> p o n", o=1).to_broadcast([P, KD, MEM]), ALU.mult)
                dve.drain()
                dve.sem_inc(mem_n, 1)
                for m in range(KD):
                    dve.wait_ge(mem_hi_done, l * KD + m + 1)
                    stt(mem_lo[:, m, :], mem_f32[:, m, :], g("x_mem_g", m), mem_hi[:, m, :].bitcast(F32),
                        ALU.mult, ALU.subtract).then_inc(mem_lo_done, 1)
                    if m % (KD // 2) == KD // 2 - 1:
                        take_y("f1dn", 1, m // (KD // 2), "f1_post_g", y, True)
                dve.wait_ge(trig_done, l * 2 + 2)
                dve.tensor_scalar(sin_t[:], sin_t[:], const[:, C_SIGN:C_SIGN + 1], None, ALU.mult)
                with dve.Fori(2, KD // 2) as j:
                    for s in range(2):
                        take_y("f1dn", j, s, "f1_post_g", y, True)
                dve.drain()
                post_norm("f1dn", y)
                pre_norm(S_PRE2, H_PRE2, "mix_pre_g")

                dve.wait_ge(pads_done, l + 1)
                dve.wait_ge(r_ready, l * NSTAT + S_PRE2 + 1)
                dests = ([ga[:, t, :] for t in range(2)] + [gg[:, t, :] for t in range(2)] + [qk[:, t, :] for t in range(4)]
                         + [vt[:, t, :] for t in range(2)] + [xs[:, t, :] for t in range(2)]
                         + [cg[:, t, :] for t in range(2)] + [bg[:, t, :] for t in range(2)]
                         + [za[:, t, PAD:PAD + SEQ] for t in range(2)])
                half = ROT // 2
                swap = [i + half if i < half else i - half if i < ROT else i for i in range(32)]
                per_tile = -(-(CFW - 1) // 13)
                done_taps = 0
                for i in range(18):
                    dve.wait_ge(w_used, l * NB + BASE["win"] + i + 1 + RING)
                    dve.tensor_tensor(dests[i], ps[:, i % 2, :], r_pre[:], ALU.mult).then_inc(dve_tiles, 1)
                    if i == 4:
                        dve.wait_ge(tanh_done, l + 1)
                        stt(upad[:, :, CFW - 1:], gg[:], 1.0, ga[:], ALU.add, ALU.mult)
                        dve.drain()
                        for t in range(2):
                            dve.tensor_scalar(u[:, t, :], upad[:, t, CFW - 1:CFW - 1 + SEQ], g("conf_w", 2 * (CFW - 1) + t),
                                              g("conf_b", t), ALU.mult, ALU.add)
                        dve.drain()
                    if i == 7:
                        dve.drain()
                        for r in range(4):
                            dve.stream_shuffle(rope[:, r, :], qk[:, r, :], swap).then_inc(rope_shuf, 1)
                    if i >= 5:
                        n = min(per_tile, CFW - 1 - done_taps)
                        if n > 0:
                            for tap in range(done_taps, done_taps + n):
                                for t in range(2):
                                    stt(u[:, t, :], upad[:, t, tap:tap + SEQ], g("conf_w", 2 * tap + t), u[:, t, :],
                                        ALU.mult, ALU.add)
                                dve.drain()
                            done_taps += n
                            if done_taps == CFW - 1:
                                dve.sem_inc(u_ready, 1)
                    if i == 16:
                        for r in range(4):
                            dve.wait_ge(rope_mul, l * 4 + r + 1)
                            dve.tensor_tensor(qk[:, r, :], qk[:, r, :], rope[:, r, :], ALU.add).then_inc(qk_ready, 1)
                assert done_taps == CFW - 1

                def short_conv(k_):
                    if k_ == 0:
                        dve.wait_ge(c_done, l + 1)
                    for t in range(2):
                        if k_ == 0:
                            dve.tensor_scalar(xs[:, t, :], cpad[:, t, 0:SEQ], g("sconv_w", t), None, ALU.mult)
                        else:
                            stt(xs[:, t, :], cpad[:, t, k_:k_ + SEQ], g("sconv_w", 2 * k_ + t), xs[:, t, :], ALU.mult, ALU.add)
                    dve.drain()
                    if k_ == SCW - 1:
                        dve.tensor_tensor(bg[:], bg[:], xs[:], ALU.mult).then_inc(yb_ready, 1)

                def pooled(t):
                    dve.wait_ge(pool_sums, l + 1)
                    edge = zc[:, t, PAD:2 * PAD]
                    dve.tensor_tensor(edge, zb[:, t, PAD:2 * PAD], const[:, C_EDGE + t * PAD:C_EDGE + (t + 1) * PAD], ALU.mult)
                    dve.drain()
                    stt(zb[:, t, PAD:PAD + SEQ], zb[:, t, PAD:PAD + SEQ], const[:, C_INVW + t:C_INVW + t + 1],
                        za[:, t, PAD:PAD + SEQ], ALU.mult, ALU.subtract)
                    dve.drain()
                    dve.tensor_tensor(zb[:, t, PAD:2 * PAD], edge, za[:, t, PAD:2 * PAD], ALU.subtract).then_inc(mixed, 1)

                for t in range(NUNIT + 5):
                    if t < NUNIT:
                        keys = (t // DIFF_H + 1) * P
                        dve.wait_ge(a_s, l * NUNIT + t + 1)
                        b = 2 + 2 * (t % 2)
                        dve.tensor_reduce(att_s[:, t % 2, 0, 0:2], ps[:, b:b + 2, 0:keys], AX.X, ALU.max, negate=True)
                        dve.drain()
                        m_ = att_s[:, t % 2, 0, 0:2]
                        dve.tensor_scalar(m_, m_, DIFF_SCALE, None, ALU.mult).then_inc(a_max, 1)
                    if 1 <= t <= NUNIT:
                        n = t - 1
                        keys = (n // DIFF_H + 1) * P
                        r = att_s[:, n % 2, 2, 0:2]
                        dve.wait_ge(a_exp, l * NUNIT + n + 1)
                        if n >= 2:
                            dve.wait_ge(a_tr, l * NUNIT + n - 1)
                        dve.reciprocal(r, att_s[:, n % 2, 1, 0:2])
                        dve.drain()
                        dve.tensor_scalar(r[:, 1:2], r[:, 1:2], neg_lam_l[:], None, ALU.mult)
                        dve.tensor_scalar(amix[:, n % 2, 0:keys], prob[:, n % 2, 0, 0:keys], r[:, 0:1], None, ALU.mult)
                        dve.drain()
                        stt(amix[:, n % 2, 0:keys], prob[:, n % 2, 1, 0:keys], r[:, 1:2], amix[:, n % 2, 0:keys],
                            ALU.mult, ALU.add).then_inc(a_mix, 1)
                    if t >= 7 and (t - 7) % 4 == 0:
                        qb = (t - 7) // 4
                        dve.wait_ge(o_sq, l * QB + qb + 1)
                        rsqrt(stat[:, 3, :], DIFF_H, DIFF_DV)
                        if qb >= 1:
                            dve.wait_ge(o_tr, l * QB + qb)
                        dve.tensor_tensor(oc[:].rearrange("p (h n) -> p h n", h=DIFF_H),
                                          ps[:, (7, 1)[qb % 2], 0:2 * P].rearrange("p (h n) -> p h n", h=DIFF_H),
                                          stat[:, 1, 0:DIFF_H].rearrange("p (h o) -> p h o", o=1)
                                          .to_broadcast([P, DIFF_H, DIFF_DV]), ALU.mult).then_inc(o_out, 1)
                    if t >= 8 and (t - 8) % 4 == 0:
                        qb = (t - 8) // 4
                        dve.wait_ge(yc_hi, l * QB + qb + 1)
                        for f in range(2):
                            e = stt(h_lo[:, 4 + f, qb * P:(qb + 1) * P], ps[:, 0, f * P:(f + 1) * P], g("subln"),
                                    h_hi[:, 4 + f, qb * P:(qb + 1) * P].bitcast(F32), ALU.mult, ALU.subtract)
                        e.then_inc(yc_lo, 1)
                    if t == 2:
                        dve.wait_ge(mu_done, l + 1)
                        for i in range(2):
                            dve.tensor_tensor(u[:, i, :], u[:, i, :], ps[:, 0, :], ALU.subtract).then_inc(xc_ready, 1)
                    if t in (1, 3, 4):
                        short_conv((1, 3, 4).index(t))
                    if t == 5:
                        factors(S_LN, SEQ, 2 * P, bank=0)
                    if t == 6:
                        dve.wait_ge(r_ready, l * NSTAT + S_LN + 1)
                        for i in range(2):
                            e = stt(u[:, i, :], u[:, i, :], g("ln_g", i), r_post[:], ALU.mult, ALU.mult)
                        e.then_inc(ln_ready, 1)
                    if t == 9:
                        for i in range(2):
                            dve.wait_ge(h_hi_done, l * NH + H_MIX + i + 1)
                            lo_of(2 + i, bg[:, i, :])
                    if t in (10, 13):
                        pooled((10, 13).index(t))
                    if t == NUNIT + 2:
                        for i in range(2):
                            dve.wait_ge(h_hi_done, l * NH + H_MIX + 2 + i + 1)
                            lo_of(i, ps[:, 2 + i, :], g("pool_scale", i))
                        for i in range(2):
                            dve.wait_ge(h_hi_done, l * NH + H_MIX + 4 + i + 1)
                            lo_of(6 + i, u[:, i, :])

                out_project("wo", "mix_post_g")
                post_norm("wo", y_r)
                pre_norm(S_PRE3, H_PRE3, "x_pre_g")
                with dve.Fori(0, KD // 2) as j:
                    for s in range(2):
                        dve.wait_ge(r_ready, l * NSTAT + S_PRE3 + 1)
                        dve.wait_ge(w_used, l * NB + BASE["qx"] + 2 * j + s + 1 + RING)
                        dve.tensor_tensor(qx[:, bass.ds(2 * j + s, 1), :], ps[:, s, :], r_pre[:], ALU.mult).then_inc(dve_tiles, 1)
                dve.drain()
                for t in range(QB + 1):
                    if t < QB:
                        b = 2 + 2 * (t % 2)
                        m_ = att_s[:, t % 2, 0, :]
                        dve.wait_ge(x_s, l * QB + t + 1)
                        dve.tensor_reduce(m_, ps[:, b:b + 2, :].rearrange("p b (h n) -> p (b h) n", h=2), AX.X, ALU.max, negate=True)
                        dve.drain()
                        dve.tensor_scalar(m_, m_, X_SCALE, None, ALU.mult).then_inc(x_max, 1)
                    if t >= 1:
                        n = t - 1
                        dve.wait_ge(x_exp, l * QB + n + 1)
                        dve.reciprocal(att_s[:, n % 2, 2, :], att_s[:, n % 2, 1, :])
                        dve.drain()
                        for h in range(X_H):
                            e = dve.tensor_scalar(px[:, n % 2, h, :], px[:, n % 2, h, :], att_s[:, n % 2, 2, h:h + 1], None, ALU.mult)
                        e.then_inc(x_nrm, 1)
                for n in range(2 * X_H):
                    dve.wait_ge(h_hi_done, l * NH + H_OX + n + 1)
                    lo_of(n, ps[:, n % 2, :])
                dve.drain()
                out_project("xo", "x_post_g")
                post_norm("xo", y_r, 2)
                for m in range(KD):
                    x_lo(H_PRE4, "f2_pre_g", m)
                    if m == 1:
                        update_x(y_r, 2)
                factors(S_PRE4, SEQ, D)
                ffn_in(2)
                with dve.Fori(0, KD // 2) as j:
                    for s in range(2):
                        take_y("f2dn", j, s, "f2_post_g", y, True)
                dve.drain()
                post_norm("f2dn", y, KD // 2 - 1)


def _blocks(w, kc):
    L, K, N = w.shape
    w = w.reshape(L, K // (kc * P), kc, P, N // P, P)
    return w.transpose(0, 4, 1, 3, 2, 5).reshape(L, -1, P, kc * P)


def _columns(a):
    a = np.asarray(a)
    L = a.shape[0]
    return a.reshape(L, -1, P).transpose(2, 0, 1)


def _constants():
    c = np.zeros((P, NCONST), np.float32)
    c[:, C_ID:C_ID + P] = np.eye(P, dtype=np.float32)
    inv = np.float32(THETA) ** (-np.arange(0, ROT, 2, dtype=np.float32) / np.float32(ROT))
    for p in range(P):
        d = p % DIFF_DK
        if d < ROT:
            c[p, C_FREQ] = inv[d % (ROT // 2)]
            c[p, C_SIGN] = -1.0 if d < ROT // 2 else 1.0
        for t in range(2):
            w = POOL_WINDOWS[2 * t + p // 64]
            c[p, C_INVW + t] = 1.0 / w
            for i in range(POOL_WINDOWS[-1]):
                c[p, C_EDGE + t * POOL_WINDOWS[-1] + i] = 1.0 / min(i + 1, w)
    c[::DIFF_DK, C_ROW:C_ROW + CHUNK] = 1.0
    c[::DIFF_DK, C_ROW + P:] = -1e30
    return c


def kernel(**a):
    import concourse.bacc as bacc
    from concourse.bass_utils import run_bass_kernel_spmd as run

    a = {k: np.asarray(v) for k, v in a.items()}
    win = a["w_in"]
    G = 2 * P
    win = np.concatenate([win[:, :, i * G:(i + 1) * G] for i in (7, 8, 4, 5, 6, 1, 3, 2, 0)], axis=2)

    def gate_up(n):
        gt, up = _blocks(a[f"f{n}_w_gate"], KD), _blocks(a[f"f{n}_w_up"], KD)
        return np.stack([gt, up], axis=2).reshape(DEPTH, 2 * KF, P, KD * P)

    w8 = np.concatenate([gate_up(1)] + [_blocks(w, KD) for w in (a["x_wk"], win, a["w_o"], a["x_wv"], a["x_wq"], a["x_wo"])]
                        + [gate_up(2)], axis=1)
    wd = np.concatenate([_blocks(a["f1_w_down"], KFH), _blocks(a["f2_w_down"], KFH)], axis=1)
    par = np.concatenate([_columns(a[n]) for n in ("f1_pre_g", "f1_post_g", "mix_pre_g", "mix_post_g", "x_pre_g", "x_mem_g",
                                                   "x_post_g", "f2_pre_g", "f2_post_g", "pool_scale", "sconv_w")]
                         + [np.tile(a["diff_subln_g"], (1, 2)).T.reshape(P, DEPTH, 1)]
                         + [_columns(a[n]) for n in ("conf_dw_w", "conf_dw_b", "conf_ln_g", "conf_ln_b")], axis=2)
    poolw = np.zeros((DEPTH, P, 2, P), np.float32)
    for t in range(2):
        for s in range(2):
            poolw[:, 64 * s:64 * s + 64, t, 64 * s:64 * s + 64] = a["pool_w"][:, 2 * t + s]
    lam = np.stack([a["lam_q1"], a["lam_k1"], a["lam_q2"], a["lam_k2"]], axis=1).reshape(1, -1)
    ins = {
        "xT": a["x"][0].T.reshape(KD, P, SEQ).transpose(1, 0, 2),
        "memT": a["mem"][0].T.reshape(KD, P, MEM).transpose(1, 0, 2),
        "pos": a["positions"].reshape(1, SEQ),
        "w8": w8.reshape(-1, P, KD * P), "wd": wd.reshape(-1, P, KFH * P),
        "par": par, "poolw": poolw, "lam": lam, "const": _constants(),
    }
    ins = {k: np.ascontiguousarray(v) for k, v in ins.items()}
    nc = bacc.Bacc("TRN2", target_bir_lowering=False, num_devices=1)
    aps = [nc.dram_tensor(k, v.shape, mybir.dt.from_np(v.dtype), kind="ExternalInput").ap() for k, v in ins.items()]
    out = nc.dram_tensor("out", (P, KD, SEQ), F32, kind="ExternalOutput").ap()
    build(nc, *aps, out)
    got = run(nc, [ins], core_ids=[0]).results[0]["out"]
    return np.ascontiguousarray(got.transpose(1, 0, 2).reshape(D, SEQ).T)[None]
```

```python
import math
from contextlib import ExitStack

import numpy as np

import concourse.bass as bass
from concourse import mybir

F32, F32R, I32 = mybir.dt.float32, mybir.dt.float32r, mybir.dt.int32
ALU, ACT, AX = mybir.AluOpType, mybir.ActivationFunctionType, mybir.AxisListType

P, D, SEQ, DEPTH, MEM, FF = 128, 1024, 512, 2, 256, 2816
KD, KF, KFH = D // P, FF // P, FF // P // 2
EPS = 1e-6
POOL_WINDOWS = (2, 4, 8, 16)
SCW, CFW = 3, 31
DIFF_DK, DIFF_DV, DIFF_H, X_H, X_HD, CHUNK = 32, 64, 4, 4, 256, 64
ROT, THETA = DIFF_DK // 4, 500000.0
QB = SEQ // P

SIZES = (("f1gu", 2 * KF), ("f1dn", 2 * KD), ("kx", KD), ("win", 18), ("wo", KD), ("vx", KD),
         ("qx", KD), ("xo", KD), ("f2gu", 2 * KF), ("f2dn", 2 * KD))
BASE, NB = {}, 0
for _n, _k in SIZES:
    BASE[_n] = NB
    NB += _k
DT, NDT = {}, 0
for _n, _k in (("f1gu", 2 * KF), ("f1dn", KD), ("win", 18), ("wo", KD), ("qx", KD), ("xo", KD),
               ("f2gu", 2 * KF), ("f2dn", KD)):
    DT[_n] = NDT
    NDT += _k
NAT = 2 * KD
RING = 2
WARM_UP = 6

PAR, NPAR = {}, 0
for _n, _k in (("f1_pre_g", KD), ("f1_post_g", KD), ("mix_pre_g", KD), ("mix_post_g", KD),
               ("x_pre_g", KD), ("x_mem_g", KD), ("x_post_g", KD), ("f2_pre_g", KD),
               ("f2_post_g", KD), ("pool_scale", 2), ("sconv_w", 2 * SCW), ("subln", 1),
               ("conf_w", 2 * CFW), ("conf_b", 2), ("ln_g", 2), ("ln_b", 2)):
    PAR[_n] = NPAR
    NPAR += _k
C_ID, C_FREQ, C_SIGN, C_INVW, C_EDGE, C_ROW = 0, 128, 129, 130, 132, 164
NCONST = C_ROW + 128 + CHUNK

NTH, NSQ = {"PRE1": 1, "MEM": 2, "PRE2": 3, "LN": 4, "PRE3": 5, "PRE4": 6}, 6
(S_PRE1, S_MEM, S_POST1, S_PRE2, S_LN, S_POST2, S_PRE3, S_POST3, S_PRE4, S_POST4), NSTAT = range(10), 10
MIX_ORDER = (2, 3, 6, 7, 0, 1, 4, 5)
H_PRE1, H_PRE2, H_MIX, H_PRE3, H_OX, H_PRE4, NH = 0, 8, 16, 22, 30, 38, 46
POST = {"f1dn": (S_POST1, 0), "wo": (S_POST2, 1), "xo": (S_POST3, 2), "f2dn": (S_POST4, 3)}
NY = KD - 1
XD = {S_PRE2: 0, S_PRE3: 4, S_PRE4: 8, S_PRE1: 10}
NXD, NXP, X0 = 12, 4, 2
NUNIT = QB * DIFF_H
DIFF_SCALE, X_SCALE = DIFF_DK ** -0.5, X_HD ** -0.5


def build(nc, x_d, mem_d, pos_d, w8_d, wd_d, par_d, poolw_d, lam_d, const_d, out_d):
    ctx = ExitStack()
    with ctx:
        place = [(nc.sbuf_base + 63) // 64 * 64]

        def at(name, shape, dt, where=None):
            n = int(np.prod(shape[1:])) * 4
            off = place[0] if where is None else where
            t = nc.alloc_sbuf_tensor_at(name, shape, dt, offset=off)
            if where is None:
                place[0] += (n + 31) // 32 * 32
            return t

        x = at("x", [P, KD, SEQ], F32)
        y_at = place[0]
        h_hi = at("h_hi", [P, KD, SEQ], F32R)
        y = at("y", [P, KD, SEQ], F32, y_at)
        h_lo = at("h_lo", [P, KD, SEQ], F32R)
        w_in_f32 = at("w_stage", [P, RING, KFH, P], F32)
        w_hi = at("w_hi", [P, RING, KFH, P], F32R)
        w_lo = at("w_lo", [P, RING, KFH, P], F32R)
        mem_hi = at("mem_hi", [P, KD, MEM], F32R)
        mem_lo = at("mem_lo", [P, KD, MEM], F32R)
        const = at("const", [P, NCONST], F32)
        ones = at("ones", [P, P], F32)
        mean256 = at("mean256", [P, P], F32)
        cos_t = at("cos_t", [P, SEQ], F32)
        sin_t = at("sin_t", [P, SEQ], F32)
        par_all = at("par_all", [P, DEPTH + 1, NPAR], F32)
        par = at("par", [P, NPAR], F32)
        neg_lam = at("neg_lam", [P, DEPTH], F32)
        neg_lam_l = at("neg_lam_l", [P, 1], F32)
        r_mem = at("r_mem", [P, MEM], F32)
        r_pre = at("r_pre", [P, SEQ], F32)
        r_post = at("r_post", [P, SEQ], F32)
        e0_at = place[0]
        epi = at("epi", [P, 2, SEQ], F32)
        acc_at = place[0]
        acc = at("acc", [P, SEQ], F32)
        poolw = at("poolw", [P, 2, P], F32, acc_at)
        diag = at("diag", [P, QB, P], F32)
        warm = at("warm", [P, 1], F32)
        mask = at("mask", [P, P + CHUNK], F32R)
        stat = at("stat", [P, 4, 4], F32)
        att_s = at("att_s", [P, 2, 3, 4], F32)
        ident = const[:, C_ID:C_ID + P]

        r_at = place[0]
        hid_hi = at("hid_hi", [P, KF, SEQ], F32R)
        hid_lo = at("hid_lo", [P, KF, SEQ], F32R)
        assert place[0] <= nc.sbuf_usable_end, place[0]
        h_lo_at = y_at + KD * SEQ * 4
        mem_f32 = at("mem_f32", [P, KD, MEM], F32, h_lo_at)
        ang = at("ang", [P, 4, SEQ], F32, h_lo_at + KD * MEM * 4)
        mem_sq = at("mem_sq", [P, KD, MEM], F32, y_at + KD // 2 * SEQ * 4)
        pos_i = at("pos_i", [P, SEQ], I32, y_at + (KD // 2 - 1) * SEQ * 4)
        rp = [r_at]

        def r_alloc(name, shape):
            t = at(name, shape, F32, rp[0])
            rp[0] += (int(np.prod(shape[1:])) * 4 + 31) // 32 * 32
            return t

        kx = r_alloc("kx", [P, KD, MEM])
        vx_at = rp[0]
        xs = r_alloc("xs", [P, 2, SEQ])
        cg = r_alloc("cg", [P, 2, SEQ])
        vx = at("vx", [P, MEM // P, D], F32, vx_at)
        vxt_at = rp[0]
        ga = r_alloc("ga", [P, 2, SEQ])
        gg = r_alloc("gg", [P, 2, SEQ])
        vxt = at("vxt", [P, KD, MEM], F32, vxt_at)
        qk_hi = at("qk_hi", [P, 4, SEQ], F32R, vxt_at)
        cross_at = rp[0]
        bg = r_alloc("bg", [P, 2, SEQ])
        PAD = POOL_WINDOWS[-1]
        za = r_alloc("za", [P, 2, PAD + SEQ])
        zb = r_alloc("zb", [P, 2, PAD + SEQ])
        zc = r_alloc("zc", [P, 2, PAD + SEQ])
        qk_at = rp[0]
        qk = r_alloc("qk", [P, 4, SEQ])
        qk_lo = at("qk_lo", [P, 4, SEQ], F32R, qk_at)
        vt = r_alloc("vt", [P, 2, SEQ])
        v = r_alloc("v", [P, QB, 2 * P])
        cpad = r_alloc("cpad", [P, 2, SCW - 1 + SEQ])
        upad = r_alloc("upad", [P, 2, CFW - 1 + SEQ])
        u = r_alloc("u", [P, 2, SEQ])
        p_at = rp[0]
        prob = r_alloc("prob", [P, 2, 2, SEQ])
        rope = at("rope", [P, 4, SEQ], F32, p_at)
        sqx = at("sqx", [P, KD, SEQ], F32, p_at)
        amix = r_alloc("amix", [P, 2, SEQ])
        amix_t = r_alloc("amix_t", [P, 2, SEQ])
        oc = r_alloc("oc", [P, 2 * P])
        junk = r_alloc("junk", [P, DIFF_H, DIFF_DV])
        assert rp[0] <= place[0], (rp[0], place[0])
        rp[0] = cross_at
        qx = r_alloc("qx", [P, KD, SEQ])
        y_r = at("y_r", [P, KD, SEQ], F32, cross_at)
        px = r_alloc("px", [P, 2, X_H, MEM])
        pxt = r_alloc("pxt", [P, 2, X_H, SEQ])
        assert rp[0] <= place[0]
        lam_in = at("lam_in", [P, DEPTH, 4, DIFF_DK], F32, r_at)
        lam_s = at("lam_s", [P, 2 * DEPTH], F32, r_at + SEQ * 4)
        lam_p = at("lam_p", [P, DEPTH, 2, DIFF_DK], F32, r_at + SEQ * 4 + 64)

        ps = ctx.enter_context(nc.psum_tensor("ps", [P, 8, 512], F32))
        B_STAT, B_BC = 6, 7
        O_BANK = [0] * (QB - 1) + [6]

        def sem(name):
            return ctx.enter_context(nc.semaphore(name))

        w_loaded = [sem("w_loaded0"), sem("w_loaded1")]
        w_hi_done, w_lo_done, w_used = sem("w_hi_done"), sem("w_lo_done"), sem("w_used")
        dve_tiles, act_tiles = sem("dve_tiles"), sem("act_tiles")
        h_hi_done, h_lo_done = sem("h_hi_done"), sem("h_lo_done")
        sq_ready, sq_ready_p, sq_summed, r_ready = sem("sq_ready"), sem("sq_ready_p"), sem("sq_summed"), sem("r_ready")
        ysq_ready, ysq_used, y_summed = sem("ysq_ready"), sem("ysq_used"), sem("y_summed")
        stat_sum, stat_diag, stat_bc = sem("stat_sum"), sem("stat_diag"), sem("stat_bc")
        x_ready, x_ready_p = sem("x_ready"), sem("x_ready_p")
        silu_done, prod_done = sem("silu_done"), sem("prod_done")
        hid_hi_done, hid_lo_done = sem("hid_hi_done"), sem("hid_lo_done")
        consts_in, x_in, poolw_in = sem("consts_in"), [sem("x_in0"), sem("x_in1")], sem("poolw_in")
        mem_in, pos_in, mem_n, mem_hi_done, mem_lo_done = sem("mem_in"), sem("pos_in"), sem("mem_n"), sem("mem_hi_done"), sem("mem_lo_done")
        par_ready, setup_p, trig_arg, trig_done = (sem(n) for n in ("par_ready", "setup_p", "trig_arg", "trig_done"))
        lam_arg, lam_exp = sem("lam_arg"), sem("lam_exp")
        tanh_done, c_done, pads_done = sem("tanh_done"), sem("c_done"), sem("pads_done")
        pool_sums, mixed, pool_y = (sem(n) for n in ("pool_sums", "mixed", "pool_y"))
        yb_ready, u_ready, mu_done, xc_ready = sem("yb_ready"), sem("u_ready"), sem("mu_done"), sem("xc_ready")
        ln_ready, yd_ready = sem("ln_ready"), sem("yd_ready")
        rope_shuf, rope_mul, qk_ready = sem("rope_shuf"), sem("rope_mul"), sem("qk_ready")
        qk_hi_done, qk_lo_done = sem("qk_hi_done"), sem("qk_lo_done")
        v_tr, v_tok, vx_tr, vx_tok = sem("v_tr"), sem("v_tok"), sem("vx_tr"), sem("vx_tok")
        a_s, a_max, a_exp, a_mix, a_tr, a_trc, a_pv = (sem(n) for n in ("a_s", "a_max", "a_exp", "a_mix", "a_tr", "a_trc", "a_pv"))
        o_sq, o_out, o_tr, yc_hi, yc_lo = (sem(n) for n in ("o_sq", "o_out", "o_tr", "yc_hi", "yc_lo"))
        x_s, x_max, x_exp, x_nrm, x_tr, x_trc, x_pv = (sem(n) for n in ("x_s", "x_max", "x_exp", "x_nrm", "x_tr", "x_trc", "x_pv"))
        stored = sem("stored")

        def g(name, i=0):
            return par[:, PAR[name] + i:PAR[name] + i + 1]

        block = ctx.enter_context(nc.Block())

        @block.sync
        def _(sp):
            sp.dma_start(par_all[:, 0:DEPTH, :], par_d).then_inc(consts_in, 16)
            sp.dma_start(const[:], const_d).then_inc(consts_in, 16)
            sp.dma_start(lam_in[:], lam_d.to_broadcast([P, DEPTH * 4 * DIFF_DK])
                         .rearrange("p (l a k) -> p l a k", l=DEPTH, a=4)).then_inc(consts_in, 16)
            sp.dma_start(x[:, 0:KD // 2, :], x_d[:, 0:KD // 2, :]).then_inc(x_in[0], 16)
            with sp.Fori(0, DEPTH) as l:
                def load(p, s, kc, src):
                    sp.wait_ge(w_lo_done, 2 * p + s + 1)
                    sp.dma_start(w_in_f32[:, s, 0:kc, :], src.rearrange("p (k m) -> p k m", k=kc))\
                        .then_inc(w_loaded[s], 16)

                def loads(lo, n, kc, dram, first):
                    with sp.Fori(0, n // 2) as j:
                        for s in range(2):
                            load(l * (NB // 2) + lo // 2 + j, s, kc,
                                 dram[bass.ds(l * (NB - 4 * KD if kc == KD else 4 * KD) + first + 2 * j + s, 1), :, :]
                                 .rearrange("a p n -> (a p) n"))

                loads(BASE["f1gu"], 2 * KF, KD, w8_d, 0)
                for s in range(2):
                    load(l * (NB // 2) + BASE["f1dn"] // 2, s, KFH,
                         wd_d[bass.ds(l * 4 * KD + s, 1), :, :].rearrange("a p n -> (a p) n"))
                sp.wait_ge(w_used, l * NB + 2 * KF + RING)
                sp.dma_start(mem_f32[:], mem_d).then_inc(mem_in, 16)
                sp.dma_start(pos_i[:], pos_d.to_broadcast([P, SEQ])).then_inc(pos_in, 16)
                loads(BASE["f1dn"] + 2, 2 * KD - 2, KFH, wd_d, 2)
                loads(BASE["kx"], KD, KD, w8_d, 2 * KF)
                sp.wait_ge(stat_sum, l * NSTAT + S_POST1 + 1)
                sp.dma_start(poolw[:], poolw_d[bass.ds(l, 1), :, :, :].rearrange("a p t n -> (a p) t n"))\
                    .then_inc(poolw_in, 16)
                loads(BASE["win"], BASE["f2dn"] - BASE["win"], KD, w8_d, 2 * KF + KD)
                loads(BASE["f2dn"], 2 * KD, KFH, wd_d, 2 * KD)
            for i in range(KD // 2):
                if i >= 2:
                    sp.wait_ge(x_ready_p, DEPTH * NXP + i - 1)
                else:
                    sp.wait_ge(x_ready, (DEPTH - 1) * NXD + XD[S_PRE1] + X0 + i + 1)
                sp.dma_start(out_d[:, 2 * i:2 * i + 2, :], x[:, 2 * i:2 * i + 2, :]).then_inc(stored, 16)
            sp.wait_ge(stored, 16 * (KD // 2))

        @block.tensor
        def _(pe):
            pe.sem_inc(w_used, RING)
            pe.wait_ge(setup_p, 1)
            for _ in range(WARM_UP):
                pe.matmul(ps[:, 5, :], ones[:, :], ones[:].rearrange("p (o n) -> p o n", o=1)
                          .to_broadcast([P, SEQ // P, P]), start=True, stop=True)

            with pe.Fori(0, DEPTH) as l:
                def product(bank, width, p, kcs, rhs, first, last, chunk=None, order=None, at_chunk=None):
                    s = p[1]
                    n_k = kcs[1] - kcs[0]
                    pe.wait_ge(w_hi_done, 2 * p[0] + s + 1)
                    for i, k in enumerate(order or range(n_k)):
                        if chunk is not None:
                            pe.wait_ge(h_lo_done, chunk + k + 1)
                        if at_chunk is not None:
                            at_chunk(k)
                        for n, operand in enumerate(rhs(kcs[0] + k)):
                            pe.matmul(ps[:, bank, 0:width], w_hi[:, s, k, :], operand,
                                      start=(first and i == 0 and n == 0), stop=False)
                    pe.wait_ge(w_lo_done, 2 * p[0] + s + 1 + RING)
                    for k in range(n_k):
                        mm = pe.matmul(ps[:, bank, 0:width], w_lo[:, s, k, :], rhs(kcs[0] + k)[0],
                                       start=False, stop=(last and k == n_k - 1))
                    mm.then_inc(w_used, 1)

                def keep_warm(n):
                    for _ in range(n):
                        pe.matmul(ps[:, 5, :], ones[:, :], ones[:].rearrange("p (o n) -> p o n", o=1)
                                  .to_broadcast([P, SEQ // P, P]), start=True, stop=True)

                def project(name, n_tiles, rhs, inputs, width=SEQ, inputs_kf=None, chunk=None, after=(None, None),
                            order=None, at_chunk=None):
                    by_act = name in ("kx", "vx")
                    peel = after != (None, None) or at_chunk is not None

                    def tile(j, s, chunk=None, bank=None):
                        bank = s if bank is None else bank
                        if isinstance(bank, int) and bank >= 2:
                            pass
                        elif by_act:
                            pe.wait_ge(act_tiles, l * NAT + (KD if name == "vx" else 0) + 2 * j + s + 1)
                        else:
                            pe.wait_ge(dve_tiles, l * NDT + DT[name] + 2 * j + s + 1)
                        if name in POST:
                            pe.wait_ge(ysq_ready, (l * 4 + POST[name][1]) * KD + 2 * j + s + 1)
                        if inputs_kf is not None:
                            for half in range(2):
                                pe.wait_ge(hid_lo_done, inputs_kf + half * KFH + KFH)
                                product(bank, width, (l * (NB // 2) + BASE[name] // 2 + 2 * j + s, half),
                                        (half * KFH, half * KFH + KFH), rhs, half == 0, half == 1)
                        else:
                            product(bank, width, (l * (NB // 2) + BASE[name] // 2 + j, s), (0, KD), rhs, True, True, chunk, order,
                                    at_chunk if isinstance(j, int) and j + s == 0 else None)

                    if peel:
                        for sem_, value in inputs:
                            pe.wait_ge(sem_, value)
                        for t in range(len(after)):
                            tile(t // 2, t % 2, chunk if t == 0 else None, t)
                            if after[t]:
                                after[t]()
                    with pe.Fori(len(after) // 2 if peel else 0, n_tiles // 2) as j:
                        if not peel:
                            for sem_, value in inputs:
                                pe.wait_ge(sem_, value)
                        for s in range(2):
                            tile(j, s)

                def h_rhs(k):
                    return h_hi[:, k, :], h_lo[:, k, :]

                def hid_rhs(k):
                    return hid_hi[:, k, :], hid_lo[:, k, :]

                def mem_rhs(k):
                    return mem_hi[:, k, :], mem_lo[:, k, :]

                def sums(no, n, width, tiles, bank=B_STAT):
                    for m in range(n):
                        for c in range(width // P):
                            mm = pe.matmul(ps[:, bank, c:c + 1], tiles(m)[:, c * P:(c + 1) * P], ones[:, 0:1],
                                           start=(m == 0 and c == 0), stop=(m == n - 1), skip_group_check=True)
                    mm.then_inc(stat_sum, 1)

                def spread(no, width=SEQ, bank=B_BC):
                    pe.wait_ge(stat_diag, l * NSTAT + no + 1)
                    pe.matmul(ps[:, bank, 0:width], ones[:, :], diag[:, 0:width // P, :], start=True, stop=True)\
                        .then_inc(stat_bc, 1)

                def x_sums(no, name):
                    pe.wait_ge(sq_summed, l * NSQ + NTH[name])
                    sums(no, 1, SEQ, lambda m: sqx[:, m, :])

                def y_sums(name):
                    no, nth = POST[name]
                    pe.wait_ge(y_summed, l * 4 + nth + 1)
                    sums(no, 1, SEQ, lambda m: acc[:, :])

                def left_bank_0(name):
                    return ysq_ready, (l * 4 + POST[name][1]) * KD + KD - 1 + RING

                def mem_sums():
                    pe.wait_ge(sq_summed, l * NSQ + NTH["MEM"])
                    sums(S_MEM, 1, MEM, lambda m: mem_sq[:, m, :])

                project("f1gu", 2 * KF, h_rhs, [], chunk=l * NH + H_PRE1,
                        after=(None, lambda: x_sums(S_PRE1, "PRE1"), lambda: spread(S_PRE1), None))
                project("f1dn", KD, hid_rhs, [], inputs_kf=l * 2 * KF,
                        after=(mem_sums, lambda: spread(S_MEM, MEM)))
                project("kx", KD, mem_rhs, [(mem_lo_done, l * KD + KD), left_bank_0("f1dn")],
                        width=MEM, after=(lambda: y_sums("f1dn"), lambda: spread(S_POST1)))
                project("win", 18, h_rhs, [(act_tiles, l * NAT + KD - 1 + RING)], chunk=l * NH + H_PRE2,
                        after=(lambda: pe.wait_ge(act_tiles, l * NAT + KD + RING), lambda: x_sums(S_PRE2, "PRE2"), lambda: spread(S_PRE2), None))

                for t in range(2):
                    for c in range(QB):
                        mm = pe.transpose(ps[:, 4 + t, c * P:(c + 1) * P], vt[:, t, c * P:(c + 1) * P], ident)
                    mm.then_inc(v_tr, 1)
                pe.wait_ge(u_ready, l + 1)
                pe.wait_ge(dve_tiles, l * NDT + DT["win"] + 18 + RING)
                for t in range(2):
                    mm = pe.matmul(ps[:, 0, :], mean256[:, :], u[:, t, :], start=(t == 0), stop=(t == 1))
                mm.then_inc(mu_done, 1)

                def scores(n):
                    qb, h = n // DIFF_H, n % DIFF_H
                    keys = (qb + 1) * P
                    if n == 0:
                        pe.wait_ge(r_ready, l * NSTAT + S_PRE2 + 1)
                        pe.wait_ge(v_tok, l * 2 + 2)
                        pe.wait_ge(qk_lo_done, l + 1)
                    if n >= 2:
                        pe.wait_ge(a_exp, l * NUNIT + n - 1)
                    for c in range(2):
                        f = (2 * h + c) * DIFF_DK
                        t, r = f // P, f % P
                        bank = 2 + 2 * (n % 2) + c
                        for i, (a, b) in enumerate(((qk_hi, qk_hi), (qk_hi, qk_lo), (qk_lo, qk_hi))):
                            pe.matmul(ps[:, bank, 0:keys], a[r:r + DIFF_DK, t, qb * P:(qb + 1) * P],
                                      b[r:r + DIFF_DK, 2 + t, 0:keys], start=(i == 0), stop=False)
                        mm = pe.matmul(ps[:, bank, keys - CHUNK:keys], mask[r:r + 1, 0:P],
                                       mask[r:r + 1, P:P + CHUNK], start=False, stop=True)
                    mm.then_inc(a_s, 1)

                def mix_transpose(n):
                    pe.wait_ge(a_mix, l * NUNIT + n + 1)
                    if n >= 1:
                        pe.wait_ge(a_trc, l * NUNIT + n)
                    for k in range(n // DIFF_H + 1):
                        mm = pe.transpose(ps[:, 6, k * P:(k + 1) * P], amix[:, n % 2, k * P:(k + 1) * P], ident)
                    mm.then_inc(a_tr, 1)

                def values(n):
                    qb, h = n // DIFF_H, n % DIFF_H
                    pe.wait_ge(a_trc, l * NUNIT + n + 1)
                    if h == 0 and qb >= 2:
                        pe.wait_ge(o_out, l * QB + qb - 1)
                    if n == 4:
                        pe.wait_ge(r_ready, l * NSTAT + S_LN + 1)
                    for k in range(qb + 1):
                        mm = pe.matmul(ps[:, (7, 1)[qb % 2], h * DIFF_DV:(h + 1) * DIFF_DV],
                                       amix_t[:, n % 2, k * P:(k + 1) * P], v[:, k, h * DIFF_DV:(h + 1) * DIFF_DV],
                                       start=(k == 0), stop=(k == qb))
                    mm.then_inc(a_pv, 1)

                def out_transpose(qb):
                    pe.wait_ge(o_out, l * QB + qb + 1)
                    if 1 <= qb < QB - 1:
                        pe.wait_ge(yc_lo, l * QB + qb)
                    for t in range(2):
                        mm = pe.transpose(ps[:, O_BANK[qb], t * P:(t + 1) * P], oc[:, t * P:(t + 1) * P], ident)
                    mm.then_inc(o_tr, 1)

                for t in range(NUNIT + 3):
                    if t < NUNIT:
                        scores(t)
                    if 2 <= t <= NUNIT + 1:
                        mix_transpose(t - 2)
                    if 3 <= t <= NUNIT + 2:
                        values(t - 3)
                    if t >= 9 and (t - 9) % 4 == 0:
                        out_transpose((t - 9) // 4)
                    if t == 5:
                        pe.wait_ge(sq_summed, l * NSQ + NTH["LN"])
                        sums(S_LN, 1, SEQ, lambda m: epi[:, m, :], bank=0)
                    if t == 6:
                        spread(S_LN, bank=1)
                    if t == NUNIT + 2:
                        pe.wait_ge(mixed, l * 2 + 2)
                        pe.wait_ge(poolw_in, l * 16 + 16)
                        pe.wait_ge(a_exp, l * NUNIT + NUNIT - 1)
                        for i in range(2):
                            pe.matmul(ps[:, 2 + i, :], poolw[:, i, :], zb[:, i, PAD:PAD + SEQ], start=True, stop=True)\
                                .then_inc(pool_y, 1)


                def mixed_chunk(k):
                    if k == MIX_ORDER[2]:
                        out_transpose(QB - 1)
                    if k in MIX_ORDER[:6]:
                        pe.wait_ge(h_lo_done, l * NH + H_MIX + MIX_ORDER.index(k) + 1)
                    else:
                        pe.wait_ge(yc_lo, l * QB + QB)

                project("wo", KD, h_rhs, [(yc_lo, l * QB + QB - 1)], order=MIX_ORDER, at_chunk=mixed_chunk)
                project("vx", KD, mem_rhs, [left_bank_0("wo")], width=MEM,
                        after=(lambda: y_sums("wo"), lambda: spread(S_POST2)))
                project("qx", KD, h_rhs, [(act_tiles, l * NAT + 2 * KD - 1 + RING)], chunk=l * NH + H_PRE3,
                        after=(lambda: pe.wait_ge(act_tiles, l * NAT + 2 * KD + RING), lambda: x_sums(S_PRE3, "PRE3"), lambda: spread(S_PRE3), None))
                def vx_transpose(n):
                    if n >= 2:
                        pe.wait_ge(vx_tok, l * 4 + n - 1)
                    for f in range(4):
                        mm = pe.transpose(ps[:, n % 2, f * P:(f + 1) * P],
                                          vxt[:, 4 * (n % 2) + f, (n // 2) * P:(n // 2 + 1) * P], ident)
                    mm.then_inc(vx_tr, 1)

                pe.wait_ge(dve_tiles, l * NDT + DT["qx"] + KD + RING)
                pe.wait_ge(r_ready, l * NSTAT + S_PRE3 + 1)
                for t in range(QB + 2):
                    if t < QB:
                        if t >= 2:
                            pe.wait_ge(x_exp, l * QB + t - 1)
                        for h in range(X_H):
                            for c in range(2):
                                mm = pe.matmul(ps[:, 2 + 2 * (t % 2) + h // 2, (h % 2) * MEM:(h % 2 + 1) * MEM],
                                               qx[:, 2 * h + c, t * P:(t + 1) * P], kx[:, 2 * h + c, :],
                                               start=(c == 0), stop=(c == 1))
                        mm.then_inc(x_s, 1)
                    if t >= QB:
                        vx_transpose(2 * (t - QB))
                        vx_transpose(2 * (t - QB) + 1)
                    if t >= 2:
                        pe.wait_ge(x_nrm, l * QB + t - 1)
                        if t >= 3:
                            pe.wait_ge(x_trc, l * QB + t - 2)
                        for mc in range(2):
                            for h in range(X_H):
                                mm = pe.transpose(ps[:, 6 + mc, h * P:(h + 1) * P],
                                                  px[:, t % 2, h, mc * P:(mc + 1) * P], ident)
                        mm.then_inc(x_tr, 1)
                pe.wait_ge(x_trc, l * QB + QB)
                pe.wait_ge(vx_tok, l * 4 + 4)
                for n in range(2 * X_H):
                    if n >= 4:
                        pe.wait_ge(h_lo_done, l * NH + H_OX + n - 3)
                    for mc in range(2):
                        mm = pe.matmul(ps[:, 2 + n % 4, :], vx[:, mc, n * P:(n + 1) * P], pxt[:, mc, n // 2, :],
                                       start=(mc == 0), stop=(mc == 1))
                    mm.then_inc(x_pv, 1)
                project("xo", KD, h_rhs, [], at_chunk=lambda k: pe.wait_ge(h_lo_done, l * NH + H_OX + k + 1))
                keep_warm(2)
                y_sums("xo")
                keep_warm(3)
                spread(S_POST3)
                keep_warm(5)
                project("f2gu", 2 * KF, h_rhs, [], chunk=l * NH + H_PRE4,
                        after=(None, lambda: x_sums(S_PRE4, "PRE4"), lambda: spread(S_PRE4), None))
                project("f2dn", KD, hid_rhs, [], inputs_kf=l * 2 * KF + KF)
                keep_warm(2)
                y_sums("f2dn")
                keep_warm(3)
                spread(S_POST4)
                keep_warm(5)

        @block.scalar
        def _(act):
            act.wait_ge(consts_in, 48)
            act.dma_start(x[:, KD // 2:, :], x_d[:, KD // 2:, :]).then_inc(x_in[1], 16)
            act.sem_inc(ysq_ready, RING)
            act.wait_ge(lam_arg, 1)
            act.activation(lam_s[:], lam_s[:], ACT.Exp).then_inc(lam_exp, 1)

            with act.Fori(0, DEPTH) as l:
                LB = l * (NB // 2)

                def prep(p, s, kc):
                    act.wait_ge(w_loaded[s], (LB + p + 1) * 16)
                    act.wait_ge(w_used, 2 * (LB + p) + s + 1)
                    act.activation(w_hi[:, s, 0:kc, :], w_in_f32[:, s, 0:kc, :], ACT.Copy).then_inc(w_hi_done, 1)

                def x_hi(no, gain, m):
                    if no in (S_PRE1, S_PRE4) and m >= KD // 2:
                        act.wait_ge(x_ready_p, l * NXP + (0 if no == S_PRE1 else 2) + m // 2 - 1)
                    else:
                        act.wait_ge(x_ready, l * NXD + (XD[no] if no != S_PRE1 else XD[no] - NXD) + X0 + m // 2 + 1)
                    act.activation(h_hi[:, m, :], x[:, m, :], ACT.Copy, scale=g(gain, m)).then_inc(h_hi_done, 1)

                def x_squares(n=KD):
                    act.activation(sqx[:, 0:n, :], x[:, 0:n, :], ACT.Square).then_inc(sq_ready, 1)

                def take_r(no, dst, width=SEQ, bank=B_BC):
                    act.wait_ge(stat_bc, l * NSTAT + no + 1)
                    act.activation(dst[:], ps[:, bank, 0:width], ACT.Copy).then_inc(r_ready, 1)

                def y_square(name, m, s):
                    act.wait_ge(dve_tiles, l * NDT + DT[name] + m + 1 + RING)
                    act.wait_ge(ysq_used, (l * 4 + POST[name][1]) * NY + m - 1 + RING)
                    act.activation(epi[:, s, :], ps[:, s, :], ACT.Square).then_inc(ysq_ready, 1)

                def ffn(n, no):
                    base = BASE[f"f{n}gu"] // 2
                    fi = l * 2 * KF + (n - 1) * KF

                    def pair(j, kc, first=False, second=False):
                        act.activation(warm[:, 0:1], ident[:, 0:1], ACT.Silu)
                        if not second:
                            prep(base + j + 1, 0, kc)
                        if first:
                            prep(base + j + 1, 1, kc)
                            prep(base + j + 2, 0, kc)
                            take_r(no, r_pre)
                        act.wait_ge(dve_tiles, l * NDT + DT[f"f{n}gu"] + 2 * j + 1 + RING)
                        act.activation(epi[:, 0, :], epi[:, 0, :], ACT.Silu).then_inc(silu_done, 1)
                        if not first:
                            prep(base + j + 1, 1, kc)
                        act.wait_ge(prod_done, fi + j + 1)
                        act.activation(hid_hi[:, bass.ds(j, 1), :], epi[:, 1, :], ACT.Copy).then_inc(hid_hi_done, 1)

                    pair(0, KD, first=True)
                    pair(1, KD, second=True)
                    with act.Fori(2, KF - 1) as j:
                        pair(j, KD)
                    pair(KF - 1, KFH)

                def ffn_out(n, fill):
                    base = BASE[f"f{n}dn"] // 2

                    def out_pair(j, kc, fill=()):
                        for s in range(2):
                            for half in range(2):
                                if kc or s == 0:
                                    prep(base + 2 * j + 1 + s, half, KFH if s == 0 else kc)
                                for f in fill[2 * (2 * s + half):2 * (2 * s + half) + 2]:
                                    f()
                            y_square(f"f{n}dn", 2 * j + s, s)

                    if fill:
                        out_pair(0, KFH)
                        for f in fill[0:3]:
                            f()
                        out_pair(1, KFH, fill[3:])
                    with act.Fori(2 if fill else 0, KD // 2 - 1) as j:
                        out_pair(j, KFH)
                    out_pair(KD // 2 - 1, KD if n == 1 else None)

                def out_project(name):
                    with act.Fori(0, KD // 2) as j:
                        for s in range(2):
                            prep(BASE[name] // 2 + j + 1, s, KD)
                            y_square(name, 2 * j + s, s)

                def memory_project(name, dst, post, no, gain):
                    hi_after = {2: (0, 1), 3: (2, 3), 4: (4, 5), 5: (6, 7)}
                    for m in range(KD):
                        prep(BASE[name] // 2 + m // 2 + 1, m % 2, KD)
                        act.activation(dst[:, m, :], ps[:, m % 2, 0:MEM], ACT.Copy).then_inc(act_tiles, 1)
                        if m == 1:
                            take_r(post, r_post)
                        for c in hi_after.get(m, ()):
                            x_hi(no, gain, c)
                    x_squares()

                act.wait_ge(par_ready, l + 1)
                prep(0, 0, KD)
                prep(0, 1, KD)
                for m in range(KD):
                    x_hi(S_PRE1, "f1_pre_g", m)
                x_squares(KD - 2)
                ffn(1, S_PRE1)
                act.wait_ge(mem_in, l * 16 + 16)
                act.activation(mem_sq[:], mem_f32[:], ACT.Square).then_inc(sq_ready, 1)

                def sines(t):
                    act.wait_ge(trig_arg, l + 1)
                    act.activation(t[:], t[:], ACT.Sin).then_inc(trig_done, 1)

                def mem_hi_of(m):
                    act.wait_ge(mem_n, l + 1)
                    act.activation(mem_hi[:, m, :], mem_f32[:, m, :], ACT.Copy, scale=g("x_mem_g", m)).then_inc(mem_hi_done, 1)

                ffn_out(1, [lambda: take_r(S_MEM, r_mem, MEM), lambda: sines(sin_t), lambda: sines(cos_t)]
                        + [lambda m=m: mem_hi_of(m) for m in range(KD)])
                memory_project("kx", kx, S_POST1, S_PRE2, "mix_pre_g")

                for j in range(9):
                    prep(BASE["win"] // 2 + j + 1, 0, KD)
                    if j == 1:
                        take_r(S_PRE2, r_pre)
                    prep(BASE["win"] // 2 + j + 1, 1, KD)
                    if j == 2:
                        act.wait_ge(dve_tiles, l * NDT + DT["win"] + 4 + RING)
                        act.activation(gg[:], gg[:], ACT.Tanh, scale=0.5).then_inc(tanh_done, 1)
                    if j == 7:
                        act.wait_ge(qk_ready, l * 4 + 4)
                        act.activation(qk_hi[:, 0:2, :], qk[:, 0:2, :], ACT.Copy, scale=DIFF_SCALE)
                        act.activation(qk_hi[:, 2:4, :], qk[:, 2:4, :], ACT.Copy).then_inc(qk_hi_done, 1)
                for t in range(2):
                    act.wait_ge(v_tr, l * 2 + t + 1)
                    act.activation(v[:, :, t * P:(t + 1) * P],
                                   ps[:, 4 + t, :].rearrange("p (c n) -> p c n", c=QB), ACT.Copy).then_inc(v_tok, 1)

                for t in range(NUNIT + 6):
                    if t < NUNIT:
                        act.wait_ge(a_max, l * NUNIT + t + 1)
                        if t >= 2:
                            act.wait_ge(a_mix, l * NUNIT + t - 1)
                        keys = (t // DIFF_H + 1) * P
                        for c in range(2):
                            e = act.activation(prob[:, t % 2, c, 0:keys], ps[:, 2 + 2 * (t % 2) + c, 0:keys], ACT.Exp,
                                               bias=att_s[:, t % 2, 0, c:c + 1],
                                               accum_out=att_s[:, t % 2, 1, c:c + 1])
                        e.then_inc(a_exp, 1)
                    if 2 <= t <= NUNIT + 1:
                        n = t - 2
                        keys = (n // DIFF_H + 1) * P
                        act.wait_ge(a_tr, l * NUNIT + n + 1)
                        if n >= 2:
                            act.wait_ge(a_pv, l * NUNIT + n - 1)
                        act.activation(amix_t[:, n % 2, 0:keys], ps[:, 6, 0:keys], ACT.Copy).then_inc(a_trc, 1)
                    if t >= 7 and (t - 7) % 4 == 0:
                        qb = (t - 7) // 4
                        act.wait_ge(a_pv, l * NUNIT + 4 * qb + 4)
                        if qb >= 1:
                            act.wait_ge(o_out, l * QB + qb)
                        for h in range(DIFF_H):
                            e = act.activation(junk[:, h, :], ps[:, (7, 1)[qb % 2], h * DIFF_DV:(h + 1) * DIFF_DV],
                                               ACT.Square, accum_out=stat[:, 3, h:h + 1])
                        e.then_inc(o_sq, 1)
                    if t >= 9 and (t - 9) % 4 == 0:
                        qb = (t - 9) // 4
                        act.wait_ge(o_tr, l * QB + qb + 1)
                        for f in range(2):
                            e = act.activation(h_hi[:, 4 + f, qb * P:(qb + 1) * P], ps[:, O_BANK[qb], f * P:(f + 1) * P],
                                               ACT.Copy, scale=g("subln"))
                        e.then_inc(yc_hi, 1)
                    if t == 3:
                        act.wait_ge(xc_ready, l * 2 + 2)
                        for i in range(2):
                            e = act.activation(epi[:, i, :], u[:, i, :], ACT.Square)
                        e.then_inc(sq_ready, 1)
                    if t == 6:
                        take_r(S_LN, r_post, bank=1)
                        act.wait_ge(yb_ready, l + 1)
                        for i in range(2):
                            act.activation(h_hi[:, 2 + i, :], bg[:, i, :], ACT.Copy).then_inc(h_hi_done, 1)
                    if t == NUNIT + 3:
                        act.wait_ge(ln_ready, l + 1)
                        for i in range(2):
                            act.activation(u[:, i, :], u[:, i, :], ACT.Silu, bias=g("ln_b", i)).then_inc(yd_ready, 1)
                        for i in range(2):
                            act.wait_ge(yd_ready, l * 2 + i + 1)
                            act.activation(h_hi[:, 6 + i, :], u[:, i, :], ACT.Copy).then_inc(h_hi_done, 1)
                        for i in range(2):
                            act.wait_ge(pool_y, l * 2 + i + 1)
                            act.activation(h_hi[:, i, :], ps[:, 2 + i, :], ACT.Copy, scale=g("pool_scale", i)).then_inc(h_hi_done, 1)

                out_project("wo")
                memory_project("vx", vxt, S_POST2, S_PRE3, "x_pre_g")
                for j in range(KD // 2):
                    prep(BASE["qx"] // 2 + j + 1, 0, KD)
                    if j == 1:
                        take_r(S_PRE3, r_pre)
                    prep(BASE["qx"] // 2 + j + 1, 1, KD)
                for t in range(QB + 2):
                    if t < QB:
                        act.wait_ge(x_max, l * QB + t + 1)
                        if t >= 2:
                            act.wait_ge(x_tr, l * QB + t - 1)
                        for h in range(X_H):
                            e = act.activation(px[:, t % 2, h, :],
                                               ps[:, 2 + 2 * (t % 2) + h // 2, (h % 2) * MEM:(h % 2 + 1) * MEM], ACT.Exp,
                                               bias=att_s[:, t % 2, 0, h:h + 1],
                                               accum_out=att_s[:, t % 2, 1, h:h + 1])
                        e.then_inc(x_exp, 1)
                    if t >= QB:
                        for n in (2 * (t - QB), 2 * (t - QB) + 1):
                            act.wait_ge(vx_tr, l * 4 + n + 1)
                            act.activation(vx[:, n // 2, (n % 2) * SEQ:(n % 2 + 1) * SEQ], ps[:, n % 2, :], ACT.Copy)\
                                .then_inc(vx_tok, 1)
                    if t >= 2:
                        act.wait_ge(x_tr, l * QB + t - 1)
                        for mc in range(2):
                            e = act.activation(pxt[:, mc, :, (t - 2) * P:(t - 1) * P],
                                               ps[:, 6 + mc, :].rearrange("p (h n) -> p h n", h=X_H), ACT.Copy)
                        e.then_inc(x_trc, 1)
                for n in range(2 * X_H):
                    act.wait_ge(x_pv, l * 2 * X_H + n + 1)
                    act.activation(h_hi[:, n, :], ps[:, 2 + n % 4, :], ACT.Copy).then_inc(h_hi_done, 1)
                out_project("xo")
                take_r(S_POST3, r_post)
                for m in range(KD):
                    x_hi(S_PRE4, "f2_pre_g", m)
                x_squares(KD - 2)
                ffn(2, S_PRE4)
                ffn_out(2, [])
                take_r(S_POST4, r_post)

        @block.gpsimd
        def _(pool):
            pool.memset(ones[:], 1.0)
            pool.memset(mean256[:], 1.0 / (2 * P))
            pool.drain()
            pool.sem_inc(setup_p, 1)
            pool.sem_inc(w_lo_done, RING)
            pool.sem_inc(ysq_used, RING)

            with pool.Fori(0, DEPTH) as l:
                LB = l * (NB // 2)

                def prep(p, s, kc):
                    pool.wait_ge(w_hi_done, 2 * (LB + p) + s + 1)
                    pool.tensor_tensor(w_lo[:, s, 0:kc, :], w_in_f32[:, s, 0:kc, :],
                                       w_hi[:, s, 0:kc, :].bitcast(F32), ALU.subtract).then_inc(w_lo_done, 1)

                def add_square(name, m, s):
                    first = isinstance(m, int) and m == 1
                    pool.wait_ge(ysq_ready, (l * 4 + POST[name][1]) * KD + m + 1 + RING)
                    pool.tensor_tensor(acc[:], epi[:, 0, :] if first else acc[:], epi[:, s, :], ALU.add)
                    pool.drain()
                    pool.sem_inc(ysq_used, 2 if first else 1)

                def ffn(n):
                    base = BASE[f"f{n}gu"] // 2
                    with pool.Fori(0, KF - 1) as j:
                        prep(base + j + 1, 0, KD)
                        prep(base + j + 1, 1, KD)
                    prep(base + KF, 0, KFH)
                    prep(base + KF, 1, KFH)
                    name = f"f{n}dn"
                    base = BASE[name] // 2

                    def out_pair(j, kc, first=False, last=False):
                        for s in range(2):
                            if kc or s == 0:
                                prep(base + 2 * j + 1 + s, 0, KFH if s == 0 else kc)
                                prep(base + 2 * j + 1 + s, 1, KFH if s == 0 else kc)
                            if not (first and s == 0 or last and s == 1):
                                add_square(name, 2 * j + s, s)

                    out_pair(0, KFH, first=True)
                    with pool.Fori(1, KD // 2 - 1) as j:
                        out_pair(j, KFH)
                    out_pair(KD // 2 - 1, KD if n == 1 else None, last=True)

                def out_project(name):
                    def pair(j, first=False, last=False):
                        for s in range(2):
                            prep(BASE[name] // 2 + j + 1, s, KD)
                            if not (first and s == 0 or last and s == 1):
                                add_square(name, 2 * j + s, s)

                    pair(0, first=True)
                    with pool.Fori(1, KD // 2 - 1) as j:
                        pair(j)
                    pair(KD // 2 - 1, last=True)

                def update_x(no, y):
                    pool.wait_ge(r_ready, l * NSTAT + no + 1)
                    for i in (2, 3):
                        c = slice(2 * i, 2 * i + 2)
                        pool.tensor_tensor(y[:, c, :], y[:, c, :], r_post[:].rearrange("p (o n) -> p o n", o=1)
                                           .to_broadcast([P, 2, SEQ]), ALU.mult)
                        pool.drain()
                        pool.tensor_tensor(x[:, c, :], x[:, c, :], y[:, c, :], ALU.add).then_inc(x_ready_p, 1)
                    pool.drain()

                def x_squares():
                    last = x[:, KD - 2:KD, :]
                    pool.tensor_tensor(sqx[:, KD - 2:KD, :], last, last, ALU.mult).then_inc(sq_ready_p, 1)

                prep(0, 0, KD)
                prep(0, 1, KD)
                pool.wait_ge(x_ready_p, l * NXP + 2)
                x_squares()
                ffn(1)
                for m in range(KD):
                    prep(BASE["kx"] // 2 + m // 2 + 1, m % 2, KD)
                pool.memset(za[:, :, 0:PAD], 0.0)
                pool.memset(zb[:, :, 0:PAD], 0.0)
                pool.memset(zc[:, :, 0:PAD], 0.0)
                pool.memset(cpad[:, :, 0:SCW - 1], 0.0)
                pool.memset(upad[:, :, 0:CFW - 1], 0.0)
                pool.drain()
                pool.sem_inc(pads_done, 1)
                for j in range(9):
                    prep(BASE["win"] // 2 + j + 1, 0, KD)
                    prep(BASE["win"] // 2 + j + 1, 1, KD)
                    if j in (4, 5):
                        for i in (0, 1) if j == 4 else (2, 3):
                            pool.wait_ge(rope_shuf, l * 4 + i + 1)
                            pool.tensor_tensor(rope[:, i, :], rope[:, i, :], sin_t[:], ALU.mult)
                            pool.tensor_tensor(qk[:, i, :], qk[:, i, :], cos_t[:], ALU.mult)
                            pool.drain()
                            pool.sem_inc(rope_mul, 1)
                    if j == 7:
                        pool.wait_ge(dve_tiles, l * NDT + DT["win"] + 14 + RING)
                        pool.tensor_tensor(cpad[:, :, SCW - 1:], cg[:], xs[:], ALU.mult).then_inc(c_done, 1)
                pool.wait_ge(dve_tiles, l * NDT + DT["win"] + 18 + RING)

                def shifted(t, part, tile, by):
                    return t[part, tile, PAD - by:PAD - by + SEQ]
                every, upper = slice(0, P), slice(P // 2, P)
                for src, dst, part, t, by in (
                        (za, zb, every, 0, 1), (za, zb, every, 1, 1),
                        (zb, zc, every, 1, 2), (zb, zc, upper, 0, 2),
                        (zc, zb, every, 1, 4),
                        (zb, zc, upper, 1, 8)):
                    if (t, by) != (0, 1):
                        pool.drain()
                    pool.tensor_tensor(shifted(dst, part, t, 0), shifted(src, part, t, 0),
                                       shifted(src, part, t, by), ALU.add)
                for t in range(2):
                    pool.drain()
                    pool.tensor_copy(shifted(zb, upper, t, 0), shifted(zc, upper, t, 0))
                pool.drain()
                pool.sem_inc(pool_sums, 1)
                out_project("wo")
                for m in range(KD):
                    prep(BASE["vx"] // 2 + m // 2 + 1, m % 2, KD)
                with pool.Fori(0, KD // 2) as j:
                    prep(BASE["qx"] // 2 + j + 1, 0, KD)
                    prep(BASE["qx"] // 2 + j + 1, 1, KD)
                out_project("xo")
                update_x(S_POST3, y_r)
                x_squares()
                ffn(2)
                update_x(S_POST4, y)

        @block.vector
        def _(dve):
            stt = dve.scalar_tensor_tensor

            def rsqrt(src, n, count):
                hv, r, w = stat[:, 0, 0:n], stat[:, 1, 0:n], stat[:, 2, 0:n]
                dve.tensor_scalar(w, src, 1.0 / count, EPS, ALU.mult, ALU.add)
                dve.drain()
                dve.tensor_scalar(hv, w, -0.5, None, ALU.mult)
                dve.tensor_scalar(r.bitcast(I32), w.bitcast(I32), -0.5, float(0x5F3759DF), ALU.mult, ALU.add)
                dve.drain()
                for _ in range(3):
                    dve.tensor_tensor(w, r, r, ALU.mult)
                    dve.drain()
                    dve.tensor_tensor(w, w, hv, ALU.mult)
                    dve.drain()
                    stt(r, w, 1.5, r, ALU.add, ALU.mult)
                    dve.drain()

            dve.sem_inc(dve_tiles, RING)
            dve.sem_inc(act_tiles, RING)
            dve.wait_ge(consts_in, 48)
            for a in range(2):
                dve.tensor_tensor(lam_p[:, :, a, :], lam_in[:, :, 2 * a, :], lam_in[:, :, 2 * a + 1, :], ALU.mult)
            dve.drain()
            dve.tensor_reduce(lam_s[:], lam_p[:], AX.X, ALU.add)
            dve.drain()
            dve.sem_inc(lam_arg, 1)
            for l in range(DEPTH):
                for name in ("f1_post_g", "f2_post_g"):
                    c = par_all[:, l, PAR[name]:PAR[name] + KD]
                    dve.tensor_scalar(c, c, 0.5, None, ALU.mult)
                c = par_all[:, l, PAR["conf_w"]:PAR["conf_w"] + 2 * CFW]
                dve.tensor_scalar(c, c, 0.5, None, ALU.mult)
                c = par_all[:, l, PAR["subln"]:PAR["subln"] + 1]
                dve.tensor_scalar(c, c, 1.0 - (0.8 - 0.6 * math.exp(-0.3 * l)), None, ALU.mult)
            dve.wait_ge(lam_exp, 1)
            for l in range(DEPTH):
                stt(neg_lam[:, l:l + 1], lam_s[:, 2 * l + 1:2 * l + 2], -(0.8 - 0.6 * math.exp(-0.3 * l)),
                    lam_s[:, 2 * l:2 * l + 1], ALU.add, ALU.subtract)
            dve.drain()
            dve.tensor_copy(mask[:], const[:, C_ROW:C_ROW + P + CHUNK])
            dve.tensor_copy(par_all[:, DEPTH, :], par_all[:, 0, :])
            dve.tensor_copy(par[:], par_all[:, 0, :])
            dve.drain()
            dve.sem_inc(par_ready, 1)
            dve.wait_ge(x_in[0], 16)
            dve.sem_inc(x_ready, X0)
            dve.wait_ge(x_in[1], 16)
            dve.sem_inc(x_ready_p, X0)

            with dve.Fori(0, DEPTH) as l:
                def lo_of(m_dst, in0, gain=None):
                    hi = h_hi[:, m_dst, :].bitcast(F32)
                    if gain is None:
                        dve.tensor_tensor(h_lo[:, m_dst, :], in0, hi, ALU.subtract).then_inc(h_lo_done, 1)
                    else:
                        stt(h_lo[:, m_dst, :], in0, gain, hi, ALU.mult, ALU.subtract).then_inc(h_lo_done, 1)

                def factors(no, width, count, bank=B_STAT):
                    n = width // P
                    dve.wait_ge(stat_sum, l * NSTAT + no + 1)
                    rsqrt(ps[:, bank, 0:n], n, count)
                    dve.tensor_tensor(diag[:, 0:n, :], ident.rearrange("p (o n) -> p o n", o=1).to_broadcast([P, n, P]),
                                      stat[:, 1, 0:n].rearrange("p (n o) -> p n o", o=1).to_broadcast([P, n, P]),
                                      ALU.mult).then_inc(stat_diag, 1)

                def x_lo(first_h, gain, m):
                    dve.wait_ge(h_hi_done, l * NH + first_h + m + 1)
                    lo_of(m, x[:, m, :], g(gain, m))

                def add_squares(name, sq):
                    dve.wait_ge(sq_ready, l * NSQ + NTH[name])
                    if name in ("PRE1", "PRE4"):
                        dve.wait_ge(sq_ready_p, l * 2 + (1 if name == "PRE1" else 2))
                    n = KD // 2
                    while n:
                        e = dve.tensor_tensor(sq[:, 0:n, :], sq[:, 0:n, :], sq[:, n:2 * n, :], ALU.add)
                        if n > 1:
                            dve.drain()
                        n //= 2
                    e.then_inc(sq_summed, 1)

                def pre_norm(name, first_h, gain):
                    for m in range(KD):
                        x_lo(first_h, gain, m)
                    add_squares(name, sqx)
                    factors({"PRE1": S_PRE1, "PRE2": S_PRE2, "PRE3": S_PRE3}[name], SEQ, D)

                def update_x(y, i):
                    c = slice(2 * i, 2 * i + 2)
                    dve.tensor_tensor(y[:, c, :], y[:, c, :], r_post[:].rearrange("p (o n) -> p o n", o=1)
                                      .to_broadcast([P, 2, SEQ]), ALU.mult)
                    dve.drain()
                    dve.tensor_tensor(x[:, c, :], x[:, c, :], y[:, c, :], ALU.add).then_inc(x_ready, 1)

                def post_norm(name, y, pairs=KD // 2):
                    no, nth = POST[name]
                    dve.wait_ge(ysq_ready, (l * 4 + nth) * KD + KD + RING)
                    dve.wait_ge(ysq_used, (l * 4 + nth) * NY + NY + RING)
                    dve.tensor_tensor(acc[:], acc[:], epi[:, 1, :], ALU.add).then_inc(y_summed, 1)
                    factors(no, SEQ, D)
                    if name == "f2dn":
                        dve.tensor_copy(par[:], par_all[:, bass.ds(l + 1, 1), :])
                        dve.drain()
                        dve.sem_inc(par_ready, 1)
                    dve.wait_ge(r_ready, l * NSTAT + no + 1)
                    for i in range(pairs):
                        update_x(y, i)

                def take_y(name, j, s, gain, y, kf=False):
                    dve.wait_ge(w_used, l * NB + BASE[name] + (4 * j + 2 * s + 2 if kf else 2 * j + s + 1) + RING)
                    dve.tensor_scalar(y[:, bass.ds(2 * j + s, 1), :], ps[:, s, :],
                                      par[:, bass.ds(PAR[gain] + 2 * j + s, 1)], None, ALU.mult).then_inc(dve_tiles, 1)

                def ffn_in(n):
                    tile0 = l * NB + BASE[f"f{n}gu"]
                    fi = l * 2 * KF + (n - 1) * KF

                    def pair(j, bank=0):
                        dve.wait_ge(r_ready, l * NSTAT + (S_PRE1, S_PRE4)[n - 1] + 1)
                        dve.wait_ge(w_used, tile0 + 2 * j + 1 + RING)
                        dve.tensor_tensor(epi[:, 0, :], ps[:, bank, :], r_pre[:], ALU.mult).then_inc(dve_tiles, 1)
                        dve.wait_ge(w_used, tile0 + 2 * j + 2 + RING)
                        dve.tensor_tensor(epi[:, 1, :], ps[:, bank + 1, :], r_pre[:], ALU.mult).then_inc(dve_tiles, 1)
                        dve.drain()
                        dve.wait_ge(silu_done, fi + j + 1)
                        dve.tensor_tensor(epi[:, 1, :], epi[:, 1, :], epi[:, 0, :], ALU.mult).then_inc(prod_done, 1)
                        dve.drain()
                        dve.wait_ge(hid_hi_done, fi + j + 1)
                        dve.tensor_tensor(hid_lo[:, bass.ds(j, 1), :], epi[:, 1, :],
                                          hid_hi[:, bass.ds(j, 1), :].bitcast(F32), ALU.subtract).then_inc(hid_lo_done, 1)
                        dve.drain()

                    pair(0)
                    pair(1, 2)
                    with dve.Fori(2, KF) as j:
                        pair(j)

                def out_project(name, gain):
                    with dve.Fori(0, KD // 2) as j:
                        for s in range(2):
                            take_y(name, j, s, gain, y_r)
                    dve.drain()

                pre_norm("PRE1", H_PRE1, "f1_pre_g")
                dve.tensor_copy(neg_lam_l[:], neg_lam[:, bass.ds(l, 1)])
                ffn_in(1)

                add_squares("MEM", mem_sq)
                ang_, k, kh, kl = ang[:, 0, :], ang[:, 1, :], ang[:, 2, :], ang[:, 3, :]
                two_pi = 2 * math.pi
                c1 = math.floor(two_pi * 2 ** 9) / 2 ** 9
                c2 = math.floor((two_pi - c1) * 2 ** 22) / 2 ** 22
                c3 = two_pi - c1 - c2
                dve.wait_ge(pos_in, l * 16 + 16)
                dve.tensor_copy(ang_, pos_i[:])
                dve.drain()
                dve.tensor_scalar(ang_, ang_, const[:, C_FREQ:C_FREQ + 1], None, ALU.mult)
                dve.drain()
                dve.tensor_scalar(k, ang_, 1 / two_pi, 1.5 * 2 ** 23, ALU.mult, ALU.add)
                dve.drain()
                dve.tensor_scalar(k, k, 1.5 * 2 ** 23, None, ALU.subtract)
                dve.drain()
                dve.tensor_scalar(kh, k, 1.5 * 2 ** 35, None, ALU.add)
                dve.drain()
                dve.tensor_scalar(kh, kh, 1.5 * 2 ** 35, None, ALU.subtract)
                dve.drain()
                dve.tensor_tensor(kl, k, kh, ALU.subtract)
                dve.drain()
                for part in (c1, c2):
                    for kk in (kh, kl):
                        stt(ang_, kk, -part, ang_, ALU.mult, ALU.add)
                        dve.drain()
                stt(ang_, k, -c3, ang_, ALU.mult, ALU.add)
                dve.drain()
                dve.tensor_scalar(sin_t[:], ang_, 3.1415925, -3.1415925, ALU.min, ALU.max)
                dve.tensor_scalar(kh, ang_, -1.0, None, ALU.mult)
                dve.drain()
                dve.tensor_tensor(kh, kh, ang_, ALU.max)
                dve.drain()
                dve.tensor_scalar(cos_t[:], kh, -1.0, math.pi / 2, ALU.mult, ALU.add)
                dve.drain()
                dve.sem_inc(trig_arg, 1)

                take_y("f1dn", 0, 0, "f1_post_g", y, True)
                factors(S_MEM, MEM, D)
                take_y("f1dn", 0, 1, "f1_post_g", y, True)
                dve.wait_ge(r_ready, l * NSTAT + S_MEM + 1)
                dve.tensor_tensor(mem_f32[:], mem_f32[:],
                                  r_mem[:].rearrange("p (o n) -> p o n", o=1).to_broadcast([P, KD, MEM]), ALU.mult)
                dve.drain()
                dve.sem_inc(mem_n, 1)
                for m in range(KD):
                    dve.wait_ge(mem_hi_done, l * KD + m + 1)
                    stt(mem_lo[:, m, :], mem_f32[:, m, :], g("x_mem_g", m), mem_hi[:, m, :].bitcast(F32),
                        ALU.mult, ALU.subtract).then_inc(mem_lo_done, 1)
                    if m % (KD // 2) == KD // 2 - 1:
                        take_y("f1dn", 1, m // (KD // 2), "f1_post_g", y, True)
                dve.wait_ge(trig_done, l * 2 + 2)
                dve.tensor_scalar(sin_t[:], sin_t[:], const[:, C_SIGN:C_SIGN + 1], None, ALU.mult)
                with dve.Fori(2, KD // 2) as j:
                    for s in range(2):
                        take_y("f1dn", j, s, "f1_post_g", y, True)
                dve.drain()
                post_norm("f1dn", y)
                pre_norm("PRE2", H_PRE2, "mix_pre_g")

                dve.wait_ge(pads_done, l + 1)
                dve.wait_ge(r_ready, l * NSTAT + S_PRE2 + 1)
                dests = ([ga[:, t, :] for t in range(2)] + [gg[:, t, :] for t in range(2)] + [qk[:, t, :] for t in range(4)]
                         + [vt[:, t, :] for t in range(2)] + [xs[:, t, :] for t in range(2)]
                         + [cg[:, t, :] for t in range(2)] + [bg[:, t, :] for t in range(2)]
                         + [za[:, t, PAD:PAD + SEQ] for t in range(2)])
                half = ROT // 2
                swap = [i + half if i < half else i - half if i < ROT else i for i in range(32)]
                taps_after = {4: 1, 5: 3, 6: 3, 7: 1, 8: 3, 9: 3, 10: 3, 11: 3, 12: 3, 13: 1, 14: 3, 15: 3}
                done_taps = 0
                for i in range(18):
                    dve.wait_ge(w_used, l * NB + BASE["win"] + i + 1 + RING)
                    dve.tensor_tensor(dests[i], ps[:, i if i < 4 else i % 2, :], r_pre[:], ALU.mult).then_inc(dve_tiles, 1)
                    if i == 4:
                        dve.wait_ge(tanh_done, l + 1)
                        stt(upad[:, :, CFW - 1:], gg[:], 1.0, ga[:], ALU.add, ALU.mult)
                        dve.drain()
                        for t in range(2):
                            dve.tensor_scalar(u[:, t, :], upad[:, t, CFW - 1:CFW - 1 + SEQ], g("conf_w", 2 * (CFW - 1) + t),
                                              g("conf_b", t), ALU.mult, ALU.add)
                        dve.drain()
                    if i == 7:
                        dve.drain()
                        for r in range(4):
                            dve.stream_shuffle(rope[:, r, :], qk[:, r, :], swap).then_inc(rope_shuf, 1)
                    n = taps_after.get(i, 0)
                    for tap in range(done_taps, done_taps + n):
                        for t in range(2):
                            stt(u[:, t, :], upad[:, t, tap:tap + SEQ], g("conf_w", 2 * tap + t), u[:, t, :],
                                ALU.mult, ALU.add)
                        dve.drain()
                    done_taps += n
                    if n and done_taps == CFW - 1:
                        dve.sem_inc(u_ready, 1)
                    if i == 16:
                        dve.wait_ge(qk_hi_done, l + 1)
                        stt(qk_lo[:, 0:2, :], qk[:, 0:2, :], DIFF_SCALE, qk_hi[:, 0:2, :].bitcast(F32), ALU.mult, ALU.subtract)
                        dve.tensor_tensor(qk_lo[:, 2:4, :], qk[:, 2:4, :], qk_hi[:, 2:4, :].bitcast(F32),
                                          ALU.subtract).then_inc(qk_lo_done, 1)
                    if i == 13:
                        for r in range(4):
                            dve.wait_ge(rope_mul, l * 4 + r + 1)
                            dve.tensor_tensor(qk[:, r, :], qk[:, r, :], rope[:, r, :], ALU.add).then_inc(qk_ready, 1)
                assert done_taps == CFW - 1

                def short_conv(k_):
                    if k_ == 0:
                        dve.wait_ge(c_done, l + 1)
                    for t in range(2):
                        if k_ == 0:
                            dve.tensor_scalar(xs[:, t, :], cpad[:, t, 0:SEQ], g("sconv_w", t), None, ALU.mult)
                        else:
                            stt(xs[:, t, :], cpad[:, t, k_:k_ + SEQ], g("sconv_w", 2 * k_ + t), xs[:, t, :], ALU.mult, ALU.add)
                    dve.drain()
                    if k_ == SCW - 1:
                        dve.tensor_tensor(bg[:], bg[:], xs[:], ALU.mult).then_inc(yb_ready, 1)

                def pooled(t):
                    dve.wait_ge(pool_sums, l + 1)
                    edge = zc[:, t, PAD:2 * PAD]
                    dve.tensor_tensor(edge, zb[:, t, PAD:2 * PAD], const[:, C_EDGE + t * PAD:C_EDGE + (t + 1) * PAD], ALU.mult)
                    dve.drain()
                    stt(zb[:, t, PAD:PAD + SEQ], zb[:, t, PAD:PAD + SEQ], const[:, C_INVW + t:C_INVW + t + 1],
                        za[:, t, PAD:PAD + SEQ], ALU.mult, ALU.subtract)
                    dve.drain()
                    dve.tensor_tensor(zb[:, t, PAD:2 * PAD], edge, za[:, t, PAD:2 * PAD], ALU.subtract).then_inc(mixed, 1)

                for t in range(NUNIT + 6):
                    if t < NUNIT:
                        keys = (t // DIFF_H + 1) * P
                        dve.wait_ge(a_s, l * NUNIT + t + 1)
                        b = 2 + 2 * (t % 2)
                        dve.tensor_reduce(att_s[:, t % 2, 0, 0:2], ps[:, b:b + 2, 0:keys], AX.X, ALU.max, negate=True)\
                            .then_inc(a_max, 1)
                    if 1 <= t <= NUNIT:
                        n = t - 1
                        keys = (n // DIFF_H + 1) * P
                        r = att_s[:, n % 2, 2, 0:2]
                        dve.wait_ge(a_exp, l * NUNIT + n + 1)
                        if n >= 2:
                            dve.wait_ge(a_tr, l * NUNIT + n - 1)
                        dve.reciprocal(r, att_s[:, n % 2, 1, 0:2])
                        dve.drain()
                        dve.tensor_scalar(r[:, 1:2], r[:, 1:2], neg_lam_l[:], None, ALU.mult)
                        dve.tensor_scalar(amix[:, n % 2, 0:keys], prob[:, n % 2, 0, 0:keys], r[:, 0:1], None, ALU.mult)
                        dve.drain()
                        stt(amix[:, n % 2, 0:keys], prob[:, n % 2, 1, 0:keys], r[:, 1:2], amix[:, n % 2, 0:keys],
                            ALU.mult, ALU.add).then_inc(a_mix, 1)
                    if t >= 8 and (t - 8) % 4 == 0:
                        qb = (t - 8) // 4
                        dve.wait_ge(o_sq, l * QB + qb + 1)
                        rsqrt(stat[:, 3, :], DIFF_H, DIFF_DV)
                        if qb >= 1:
                            dve.wait_ge(o_tr, l * QB + qb)
                        dve.tensor_tensor(oc[:].rearrange("p (h n) -> p h n", h=DIFF_H),
                                          ps[:, (7, 1)[qb % 2], 0:2 * P].rearrange("p (h n) -> p h n", h=DIFF_H),
                                          stat[:, 1, 0:DIFF_H].rearrange("p (h o) -> p h o", o=1)
                                          .to_broadcast([P, DIFF_H, DIFF_DV]), ALU.mult).then_inc(o_out, 1)
                    if t >= 9 and (t - 9) % 4 == 0:
                        qb = (t - 9) // 4
                        dve.wait_ge(yc_hi, l * QB + qb + 1)
                        for f in range(2):
                            e = stt(h_lo[:, 4 + f, qb * P:(qb + 1) * P], ps[:, O_BANK[qb], f * P:(f + 1) * P], g("subln"),
                                    h_hi[:, 4 + f, qb * P:(qb + 1) * P].bitcast(F32), ALU.mult, ALU.subtract)
                        e.then_inc(yc_lo, 1)
                    if t == 2:
                        dve.wait_ge(mu_done, l + 1)
                        for i in range(2):
                            dve.tensor_tensor(u[:, i, :], u[:, i, :], ps[:, 0, :], ALU.subtract).then_inc(xc_ready, 1)
                    if t in (1, 3, 4):
                        short_conv((1, 3, 4).index(t))
                    if t == 4:
                        dve.wait_ge(sq_ready, l * NSQ + NTH["LN"])
                        dve.tensor_tensor(epi[:, 0, :], epi[:, 0, :], epi[:, 1, :], ALU.add).then_inc(sq_summed, 1)
                    if t == 5:
                        factors(S_LN, SEQ, 2 * P, bank=0)
                    if t == 6:
                        dve.wait_ge(r_ready, l * NSTAT + S_LN + 1)
                        for i in range(2):
                            e = stt(u[:, i, :], u[:, i, :], g("ln_g", i), r_post[:], ALU.mult, ALU.mult)
                        e.then_inc(ln_ready, 1)
                    if t == 9:
                        for i in range(2):
                            dve.wait_ge(h_hi_done, l * NH + H_MIX + i + 1)
                            lo_of(2 + i, bg[:, i, :])
                    if t in (10, 13):
                        pooled((10, 13).index(t))
                    if t == NUNIT + 4:
                        for i in range(2):
                            dve.wait_ge(h_hi_done, l * NH + H_MIX + 2 + i + 1)
                            lo_of(6 + i, u[:, i, :])
                        for i in range(2):
                            dve.wait_ge(h_hi_done, l * NH + H_MIX + 4 + i + 1)
                            lo_of(i, ps[:, 2 + i, :], g("pool_scale", i))

                out_project("wo", "mix_post_g")
                post_norm("wo", y_r)
                pre_norm("PRE3", H_PRE3, "x_pre_g")
                for m in range(KD):
                    dve.wait_ge(r_ready, l * NSTAT + S_PRE3 + 1)
                    dve.wait_ge(w_used, l * NB + BASE["qx"] + m + 1 + RING)
                    stt(qx[:, m, :], ps[:, m if m < 4 else m % 2, :], X_SCALE, r_pre[:], ALU.mult, ALU.mult).then_inc(dve_tiles, 1)
                dve.drain()
                for t in range(QB + 1):
                    if t < QB:
                        b = 2 + 2 * (t % 2)
                        m_ = att_s[:, t % 2, 0, :]
                        dve.wait_ge(x_s, l * QB + t + 1)
                        dve.tensor_reduce(m_, ps[:, b:b + 2, :].rearrange("p b (h n) -> p (b h) n", h=2), AX.X, ALU.max, negate=True)\
                            .then_inc(x_max, 1)
                    if t >= 1:
                        n = t - 1
                        dve.wait_ge(x_exp, l * QB + n + 1)
                        dve.reciprocal(att_s[:, n % 2, 2, :], att_s[:, n % 2, 1, :])
                        dve.drain()
                        for h in range(X_H):
                            e = dve.tensor_scalar(px[:, n % 2, h, :], px[:, n % 2, h, :], att_s[:, n % 2, 2, h:h + 1], None, ALU.mult)
                        e.then_inc(x_nrm, 1)
                for n in range(2 * X_H):
                    dve.wait_ge(h_hi_done, l * NH + H_OX + n + 1)
                    lo_of(n, ps[:, 2 + n % 4, :])
                dve.drain()
                out_project("xo", "x_post_g")
                post_norm("xo", y_r, 2)
                for m in range(KD):
                    x_lo(H_PRE4, "f2_pre_g", m)
                add_squares("PRE4", sqx)
                factors(S_PRE4, SEQ, D)
                ffn_in(2)
                with dve.Fori(0, KD // 2) as j:
                    for s in range(2):
                        take_y("f2dn", j, s, "f2_post_g", y, True)
                dve.drain()
                post_norm("f2dn", y, 2)


def _blocks(w, kc):
    L, K, N = w.shape
    w = w.reshape(L, K // (kc * P), kc, P, N // P, P)
    return w.transpose(0, 4, 1, 3, 2, 5).reshape(L, -1, P, kc * P)


def _columns(a):
    a = np.asarray(a)
    L = a.shape[0]
    return a.reshape(L, -1, P).transpose(2, 0, 1)


def _constants():
    c = np.zeros((P, NCONST), np.float32)
    c[:, C_ID:C_ID + P] = np.eye(P, dtype=np.float32)
    inv = np.float32(THETA) ** (-np.arange(0, ROT, 2, dtype=np.float32) / np.float32(ROT))
    for p in range(P):
        d = p % DIFF_DK
        if d < ROT:
            c[p, C_FREQ] = inv[d % (ROT // 2)]
            c[p, C_SIGN] = -1.0 if d < ROT // 2 else 1.0
        for t in range(2):
            w = POOL_WINDOWS[2 * t + p // 64]
            c[p, C_INVW + t] = 1.0 / w
            for i in range(POOL_WINDOWS[-1]):
                c[p, C_EDGE + t * POOL_WINDOWS[-1] + i] = 1.0 / min(i + 1, w)
    c[::DIFF_DK, C_ROW:C_ROW + CHUNK] = 1.0
    c[::DIFF_DK, C_ROW + P:] = -2.0 ** 100
    return c


def kernel(**a):
    import concourse.bacc as bacc
    from concourse.bass_utils import run_bass_kernel_spmd as run

    a = {k: np.asarray(v) for k, v in a.items()}
    win = a["w_in"]
    G = 2 * P
    win = np.concatenate([win[:, :, i * G:(i + 1) * G] for i in (7, 8, 4, 5, 6, 1, 3, 2, 0)], axis=2)

    def gate_up(n):
        gt, up = _blocks(a[f"f{n}_w_gate"], KD), _blocks(a[f"f{n}_w_up"], KD)
        return np.stack([gt, up], axis=2).reshape(DEPTH, 2 * KF, P, KD * P)

    w8 = np.concatenate([gate_up(1)] + [_blocks(w, KD) for w in (a["x_wk"], win, a["w_o"], a["x_wv"], a["x_wq"], a["x_wo"])]
                        + [gate_up(2)], axis=1)
    wd = np.concatenate([_blocks(a["f1_w_down"], KFH), _blocks(a["f2_w_down"], KFH)], axis=1)
    par = np.concatenate([_columns(a[n]) for n in ("f1_pre_g", "f1_post_g", "mix_pre_g", "mix_post_g", "x_pre_g", "x_mem_g",
                                                   "x_post_g", "f2_pre_g", "f2_post_g", "pool_scale", "sconv_w")]
                         + [np.tile(a["diff_subln_g"], (1, 2)).T.reshape(P, DEPTH, 1)]
                         + [_columns(a[n]) for n in ("conf_dw_w", "conf_dw_b", "conf_ln_g", "conf_ln_b")], axis=2)
    poolw = np.zeros((DEPTH, P, 2, P), np.float32)
    for t in range(2):
        for s in range(2):
            poolw[:, 64 * s:64 * s + 64, t, 64 * s:64 * s + 64] = a["pool_w"][:, 2 * t + s]
    lam = np.stack([a["lam_q1"], a["lam_k1"], a["lam_q2"], a["lam_k2"]], axis=1).reshape(1, -1)
    ins = {
        "xT": a["x"][0].T.reshape(KD, P, SEQ).transpose(1, 0, 2),
        "memT": a["mem"][0].T.reshape(KD, P, MEM).transpose(1, 0, 2),
        "pos": a["positions"].reshape(1, SEQ),
        "w8": w8.reshape(-1, P, KD * P), "wd": wd.reshape(-1, P, KFH * P),
        "par": par, "poolw": poolw, "lam": lam, "const": _constants(),
    }
    ins = {k: np.ascontiguousarray(v) for k, v in ins.items()}
    nc = bacc.Bacc("TRN2", target_bir_lowering=False, num_devices=1)
    aps = [nc.dram_tensor(k, v.shape, mybir.dt.from_np(v.dtype), kind="ExternalInput").ap() for k, v in ins.items()]
    out = nc.dram_tensor("out", (P, KD, SEQ), F32, kind="ExternalOutput").ap()
    build(nc, *aps, out)
    got = run(nc, [ins], core_ids=[0]).results[0]["out"]
    return np.ascontiguousarray(got.transpose(1, 0, 2).reshape(D, SEQ).T)[None]
```
